# Optimizing a Trainium2 kernel written in Bass

```python
import jax, jax.numpy as jnp
from jax import lax
import numpy as np
import math

D_MODEL = 1024
BATCH = 1
SEQ = 256
DEPTH = 2

N_META = 16
N_MIXERS = 2
RMS_EPS = 1e-6

MLA_HEADS = 8
QK_NOPE = 128
QK_ROPE = 64
V_HEAD = 128
Q_LORA = 384
KV_LORA = 256
MLA_WIDTH = MLA_HEADS * V_HEAD
ROPE_BASE = 10000.0
Q_BLOCK = 128
MASK_VALUE = -1e30

LRU_WIDTH = 1024
LRU_BLOCKS = 4
LRU_BLOCK = LRU_WIDTH // LRU_BLOCKS
CONV_WIDTH = 4
LRU_C = 8.0


def rmsnorm(x, g):
    xf = x.astype(jnp.float32)
    y = xf * lax.rsqrt(jnp.mean(xf * xf, axis=-1, keepdims=True) + RMS_EPS)
    return (y * g.astype(jnp.float32)).astype(x.dtype)

def rotate_half_split(x, cos, sin):
    x1, x2 = jnp.split(x, 2, axis=-1)
    return jnp.concatenate([x1 * cos - x2 * sin, x1 * sin + x2 * cos], axis=-1).astype(x.dtype)

def block_causal_attention(q_nope, q_rope, k_nope, k_rope, v):
    B, T, H, _ = q_nope.shape
    pad = (-T) % Q_BLOCK
    Tp = T + pad
    nb = Tp // Q_BLOCK

    def padt(a):
        return jnp.pad(a, [(0, 0), (pad, 0)] + [(0, 0)] * (a.ndim - 2))

    q_nope, q_rope, k_nope, k_rope, v = (padt(a) for a in (q_nope, q_rope, k_nope, k_rope, v))
    scale = (QK_NOPE + QK_ROPE) ** -0.5
    key_idx = jnp.arange(Tp)

    def to_blocks(a):
        return jnp.moveaxis(a.reshape(B, nb, Q_BLOCK, *a.shape[2:]), 1, 0)

    def one_block(args):
        blk, qn, qr = args
        s = (jnp.einsum('bqhd,bkhd->bhqk', qn, k_nope, preferred_element_type=jnp.float32)
             + jnp.einsum('bqhr,bkr->bhqk', qr, k_rope, preferred_element_type=jnp.float32)) * scale
        q_idx = blk * Q_BLOCK + jnp.arange(Q_BLOCK)
        mask = (key_idx[None, :] <= q_idx[:, None]) & (key_idx[None, :] >= pad)
        s = jnp.where(mask[None, None], s, MASK_VALUE)
        p = jax.nn.softmax(s, axis=-1)
        return jnp.einsum('bhqk,bkhd->bqhd', p.astype(v.dtype), v)

    out = lax.map(one_block, (jnp.arange(nb), to_blocks(q_nope), to_blocks(q_rope)))
    out = jnp.moveaxis(out, 0, 1).reshape(B, Tp, H, V_HEAD)
    return out[:, pad:]

def mla_mixer(h, w_in, q_norm_g, kv_norm_g, w_uq, w_ukv, w_out):
    B, T, _ = h.shape
    proj = h @ w_in
    q_lat, kv_lat, k_rope, gate = jnp.split(
        proj, [Q_LORA, Q_LORA + KV_LORA, Q_LORA + KV_LORA + QK_ROPE], axis=-1)
    q = (rmsnorm(q_lat, q_norm_g) @ w_uq).reshape(B, T, MLA_HEADS, QK_NOPE + QK_ROPE)
    q_nope, q_rope = q[..., :QK_NOPE], q[..., QK_NOPE:]
    kv = (rmsnorm(kv_lat, kv_norm_g) @ w_ukv).reshape(B, T, MLA_HEADS, QK_NOPE + V_HEAD)
    k_nope, v = kv[..., :QK_NOPE], kv[..., QK_NOPE:]
    pos = jnp.arange(T, dtype=jnp.float32)
    inv_freq = ROPE_BASE ** (-jnp.arange(0, QK_ROPE, 2, dtype=jnp.float32) / QK_ROPE)
    ang = pos[:, None] * inv_freq[None, :]
    cos, sin = jnp.cos(ang), jnp.sin(ang)
    q_rope = rotate_half_split(q_rope, cos[:, None, :], sin[:, None, :])
    k_rope = rotate_half_split(k_rope, cos, sin)
    attn = block_causal_attention(q_nope, q_rope, k_nope, k_rope, v)
    y = attn.reshape(B, T, MLA_WIDTH) * jax.nn.silu(gate)
    return y @ w_out

def rglru_mixer(h, w_in, conv_w, conv_b, w_rg, b_rg, w_ig, b_ig, lam, w_out):
    B, T, _ = h.shape
    proj = h @ w_in
    u, gate = jnp.split(proj, [LRU_WIDTH], axis=-1)
    up = jnp.pad(u, ((0, 0), (CONV_WIDTH - 1, 0), (0, 0)))
    uc = conv_b + up[:, 0:T] * conv_w[0]
    for j in range(1, CONV_WIDTH):
        uc = uc + up[:, j:j + T] * conv_w[j]
    ub = uc.reshape(B, T, LRU_BLOCKS, LRU_BLOCK)
    r = jax.nn.sigmoid(jnp.einsum('btgi,gij->btgj', ub, w_rg).reshape(B, T, LRU_WIDTH) + b_rg)
    i = jax.nn.sigmoid(jnp.einsum('btgi,gij->btgj', ub, w_ig).reshape(B, T, LRU_WIDTH) + b_ig)
    log_a = -LRU_C * r.astype(jnp.float32) * jax.nn.softplus(-lam.astype(jnp.float32))
    a = jnp.exp(log_a)
    mult = jnp.sqrt(-jnp.expm1(2.0 * log_a))
    mult = jnp.where(jnp.arange(T)[None, :, None] == 0, 1.0, mult)
    b = mult * (i * uc).astype(jnp.float32)

    def combine(left, right):
        a1, b1 = left
        a2, b2 = right
        return a1 * a2, a2 * b1 + b2

    _, hs = lax.associative_scan(combine, (a, b), axis=1)
    y = hs.astype(h.dtype) * jax.nn.silu(gate)
    return y @ w_out

def first_inputs(seed: int = 0) -> dict:
    key = jax.random.key(seed)
    ks = jax.random.split(key, 24)
    n_a = (DEPTH + 1) // 2
    n_b = DEPTH // 2
    d = D_MODEL
    f32 = jnp.float32

    def nrm(k, shape, fan_in):
        return jax.random.normal(k, shape, f32) * (fan_in ** -0.5)

    def gain(k, shape):
        return 1.0 + 0.01 * jax.random.normal(k, shape, f32)

    a_in_cols = Q_LORA + KV_LORA + QK_ROPE + MLA_WIDTH
    u0 = jax.random.uniform(ks[17], (n_b, LRU_WIDTH), f32, minval=0.9, maxval=0.999)
    s0 = u0 ** (1.0 / LRU_C)
    lam = jnp.log(s0) - jnp.log1p(-s0)
    return {
        'x': jax.random.normal(ks[0], (BATCH, SEQ, d), f32),
        'meta_tokens': jax.random.normal(ks[1], (N_META, d), f32),
        'a_norm_g': gain(ks[2], (n_a, d)),
        'a_w_in': nrm(ks[3], (n_a, d, a_in_cols), d),
        'a_q_norm_g': gain(ks[4], (n_a, Q_LORA)),
        'a_kv_norm_g': gain(ks[5], (n_a, KV_LORA)),
        'a_w_uq': nrm(ks[6], (n_a, Q_LORA, MLA_HEADS * (QK_NOPE + QK_ROPE)), Q_LORA),
        'a_w_ukv': nrm(ks[7], (n_a, KV_LORA, MLA_HEADS * (QK_NOPE + V_HEAD)), KV_LORA),
        'a_w_out': nrm(ks[8], (n_a, MLA_WIDTH, d), MLA_WIDTH),
        'b_norm_g': gain(ks[9], (n_b, d)),
        'b_w_in': nrm(ks[10], (n_b, d, 2 * LRU_WIDTH), d),
        'b_conv_w': nrm(ks[11], (n_b, CONV_WIDTH, LRU_WIDTH), CONV_WIDTH),
        'b_conv_b': 0.01 * jax.random.normal(ks[12], (n_b, LRU_WIDTH), f32),
        'b_w_rg': nrm(ks[13], (n_b, LRU_BLOCKS, LRU_BLOCK, LRU_BLOCK), LRU_BLOCK),
        'b_b_rg': 0.01 * jax.random.normal(ks[14], (n_b, LRU_WIDTH), f32),
        'b_w_ig': nrm(ks[15], (n_b, LRU_BLOCKS, LRU_BLOCK, LRU_BLOCK), LRU_BLOCK),
        'b_b_ig': 0.01 * jax.random.normal(ks[16], (n_b, LRU_WIDTH), f32),
        'b_lam': lam,
        'b_w_out': nrm(ks[18], (n_b, LRU_WIDTH, d), LRU_WIDTH),
        'final_norm_g': gain(ks[19], (d,)),
    }

def first_block(x, meta_tokens, a_norm_g, a_w_in, a_q_norm_g, a_kv_norm_g, a_w_uq, a_w_ukv,
              a_w_out, b_norm_g, b_w_in, b_conv_w, b_conv_b, b_w_rg, b_b_rg, b_w_ig, b_b_ig,
              b_lam, b_w_out, final_norm_g):
    B = x.shape[0]
    meta = jnp.broadcast_to(meta_tokens[None].astype(x.dtype), (B, N_META, x.shape[-1]))
    h = jnp.concatenate([meta, x], axis=1)
    for layer in range(DEPTH):
        j = layer // N_MIXERS
        if layer % N_MIXERS == 0:
            h = h + mla_mixer(rmsnorm(h, a_norm_g[j]), a_w_in[j], a_q_norm_g[j], a_kv_norm_g[j],
                              a_w_uq[j], a_w_ukv[j], a_w_out[j])
        else:
            h = h + rglru_mixer(rmsnorm(h, b_norm_g[j]), b_w_in[j], b_conv_w[j], b_conv_b[j],
                                b_w_rg[j], b_b_rg[j], b_w_ig[j], b_b_ig[j], b_lam[j], b_w_out[j])
    h = rmsnorm(h, final_norm_g)
    return h[:, N_META:]


MEM_LEN = 256
HEAD_DIM = 64
SELF_WIDTH = 3 * D_MODEL // 4
N_MOBA_HEADS = SELF_WIDTH // HEAD_DIM
N_DIFF_HEADS = SELF_WIDTH // (2 * HEAD_DIM)
N_MEM_HEADS = 4
MEM_WIDTH = N_MEM_HEADS * HEAD_DIM
A_IN = 3 * SELF_WIDTH + MEM_WIDTH
B_IN = SELF_WIDTH + MEM_WIDTH
D_FF = 4 * D_MODEL
MOBA_BLOCK = 256
MOBA_TOPK = 3
MOBA_Q_CHUNK = 32
ROPE_THETA = 10000.0
EPS = 1e-6
NEG = -1e30
N_A_LAYERS = DEPTH // 2
N_B_LAYERS = DEPTH - N_A_LAYERS


def _rmsnorm(x, g):
    xf = x.astype(jnp.float32)
    y = xf * lax.rsqrt(jnp.mean(xf * xf, axis=-1, keepdims=True) + EPS)
    return (y * g.astype(jnp.float32)).astype(x.dtype)

def _rope_tables(n):
    half = HEAD_DIM // 2
    inv = 1.0 / (ROPE_THETA ** (jnp.arange(half, dtype=jnp.float32) / half))
    ang = jnp.arange(n, dtype=jnp.float32)[:, None] * inv[None, :]
    return jnp.cos(ang), jnp.sin(ang)

def _apply_rope(x, cos, sin):
    half = HEAD_DIM // 2
    shp = (x.shape[1],) + (1,) * (x.ndim - 3) + (half,)
    c = cos.reshape(shp)
    s = sin.reshape(shp)
    xf = x.astype(jnp.float32)
    x1, x2 = xf[..., :half], xf[..., half:]
    return jnp.concatenate([x1 * c - x2 * s, x2 * c + x1 * s], axis=-1).astype(x.dtype)

def _sq_relu_mlp(h, w_up, w_down):
    u = jax.nn.relu(h @ w_up)
    return (u * u) @ w_down

def _memory_attention(qm, mem, mem_norm, w_mem_kv):
    B, S = qm.shape[:2]
    M = mem.shape[1]
    kv = _rmsnorm(mem, mem_norm) @ w_mem_kv
    mk = kv[..., :MEM_WIDTH].reshape(B, M, N_MEM_HEADS, HEAD_DIM).astype(jnp.float32)
    mv = kv[..., MEM_WIDTH:].reshape(B, M, N_MEM_HEADS, HEAD_DIM).astype(jnp.float32)
    s = jnp.einsum('bshd,bmhd->bhsm', qm.astype(jnp.float32), mk) * (HEAD_DIM ** -0.5)
    p = jax.nn.softmax(s, axis=-1)
    o = jnp.einsum('bhsm,bmhd->bshd', p, mv)
    return o.reshape(B, S, MEM_WIDTH).astype(qm.dtype)

def _diff_attention(q, k, v, lam, lam_init, subln):
    B, S, H, _, d = q.shape
    nq = S // Q_BLOCK
    kf = k.astype(jnp.float32)
    vf = v.astype(jnp.float32)
    qb = q.astype(jnp.float32).reshape(B, nq, Q_BLOCK, H, 2, d).transpose(1, 0, 2, 3, 4, 5)
    kpos = jnp.arange(S)
    scale = d ** -0.5

    def block(args):
        qi, i = args
        s = jnp.einsum('bqhcd,bkhcd->bhcqk', qi, kf) * scale
        qpos = i * Q_BLOCK + jnp.arange(Q_BLOCK)
        s = jnp.where(kpos[None, :] <= qpos[:, None], s, NEG)
        p = jax.nn.softmax(s, axis=-1)
        w = p[:, :, 0] - lam * p[:, :, 1]
        return jnp.einsum('bhqk,bkhe->bqhe', w, vf)

    o = lax.map(block, (qb, jnp.arange(nq)))
    o = o.transpose(1, 0, 2, 3, 4).reshape(B, S, H, 2 * d)
    o = _rmsnorm(o, subln) * (1.0 - lam_init)
    return o.reshape(B, S, H * 2 * d).astype(v.dtype)

def _moba_attention(q, kbh, vbh, kmean):
    B, S, H, d = q.shape
    NB = kbh.shape[2]
    ksel = min(MOBA_TOPK, NB)
    C = MOBA_Q_CHUNK
    nc = S // C
    qc = q.astype(jnp.float32).transpose(0, 2, 1, 3).reshape(B, H, nc, C, d).transpose(2, 0, 1, 3, 4)
    b_ix = jnp.arange(B)[:, None, None, None]
    h_ix = jnp.arange(H)[None, :, None, None]
    scale = d ** -0.5

    def chunk(args):
        qi, i = args
        qpos = i * C + jnp.arange(C)
        cur = (i * C) // MOBA_BLOCK
        gate = jnp.einsum('bhqd,bhnd->bhqn', qi, kmean)
        gate = jnp.where(jnp.arange(NB) < cur, gate, NEG)
        _, idx = lax.top_k(gate, ksel)
        valid = idx < cur
        k_sel = kbh[b_ix, h_ix, idx]
        v_sel = vbh[b_ix, h_ix, idx]
        s_sel = jnp.einsum('bhqd,bhqnkd->bhqnk', qi, k_sel) * scale
        s_sel = jnp.where(valid[..., None], s_sel, NEG).reshape(B, H, C, ksel * MOBA_BLOCK)
        k_own = lax.dynamic_index_in_dim(kbh, cur, axis=2, keepdims=False)
        v_own = lax.dynamic_index_in_dim(vbh, cur, axis=2, keepdims=False)
        s_own = jnp.einsum('bhqd,bhkd->bhqk', qi, k_own) * scale
        kpos = cur * MOBA_BLOCK + jnp.arange(MOBA_BLOCK)
        s_own = jnp.where(kpos[None, :] <= qpos[:, None], s_own, NEG)
        p = jax.nn.softmax(jnp.concatenate([s_sel, s_own], axis=-1), axis=-1)
        p_sel = p[..., :ksel * MOBA_BLOCK].reshape(B, H, C, ksel, MOBA_BLOCK)
        p_own = p[..., ksel * MOBA_BLOCK:]
        return (jnp.einsum('bhqnk,bhqnkd->bhqd', p_sel, v_sel)
                + jnp.einsum('bhqk,bhkd->bhqd', p_own, v_own))

    o = lax.map(chunk, (qc, jnp.arange(nc)))
    return o.transpose(1, 0, 3, 2, 4).reshape(B, S, H * d).astype(q.dtype)

def second_inputs(seed: int = 0) -> dict:
    key = jax.random.key(seed)
    ks = iter(jax.random.split(key, 40))

    def nrm(shape, scale):
        return jax.random.normal(next(ks), shape, jnp.float32) * scale

    def gain(shape):
        return 1.0 + nrm(shape, 0.02)

    NA, NBL, D = N_A_LAYERS, N_B_LAYERS, D_MODEL
    return {
        "x": nrm((BATCH, SEQ, D), 1.0),
        "mem": nrm((BATCH, MEM_LEN, D), 1.0),
        "a_norm_attn": gain((NA, D)),
        "a_w_in": nrm((NA, D, A_IN), D ** -0.5),
        "a_lambda": nrm((NA, 4, HEAD_DIM), 0.1),
        "a_subln": gain((NA, 2 * HEAD_DIM)),
        "a_mem_norm": gain((NA, D)),
        "a_w_mem_kv": nrm((NA, D, 2 * MEM_WIDTH), D ** -0.5),
        "a_w_out": nrm((NA, D, D), D ** -0.5),
        "a_norm_mlp": gain((NA, D)),
        "a_w_up": nrm((NA, D, D_FF), D ** -0.5),
        "a_w_down": nrm((NA, D_FF, D), D_FF ** -0.5),
        "kv_norm": gain((D,)),
        "w_kv": nrm((D, 2 * SELF_WIDTH), D ** -0.5),
        "b_norm_attn": gain((NBL, D)),
        "b_w_in": nrm((NBL, D, B_IN), D ** -0.5),
        "b_mem_norm": gain((NBL, D)),
        "b_w_mem_kv": nrm((NBL, D, 2 * MEM_WIDTH), D ** -0.5),
        "b_w_out": nrm((NBL, D, D), D ** -0.5),
        "b_norm_mlp": gain((NBL, D)),
        "b_w_up": nrm((NBL, D, D_FF), D ** -0.5),
        "b_w_down": nrm((NBL, D_FF, D), D_FF ** -0.5),
        "final_norm": gain((D,)),
    }

def second_block(x, mem, a_norm_attn, a_w_in, a_lambda, a_subln, a_mem_norm, a_w_mem_kv,
              a_w_out, a_norm_mlp, a_w_up, a_w_down, kv_norm, w_kv, b_norm_attn, b_w_in,
              b_mem_norm, b_w_mem_kv, b_w_out, b_norm_mlp, b_w_up, b_w_down, final_norm):
    B, S, _ = x.shape
    cos, sin = _rope_tables(S)
    kbh = vbh = kmean = None
    for layer in range(DEPTH):
        if layer < N_A_LAYERS:
            i = layer
            h = _rmsnorm(x, a_norm_attn[i])
            z = h @ a_w_in[i]
            w = SELF_WIDTH
            q = z[..., :w].reshape(B, S, N_DIFF_HEADS, 2, HEAD_DIM)
            k = z[..., w:2 * w].reshape(B, S, N_DIFF_HEADS, 2, HEAD_DIM)
            v = z[..., 2 * w:3 * w].reshape(B, S, N_DIFF_HEADS, 2 * HEAD_DIM)
            qm = z[..., 3 * w:].reshape(B, S, N_MEM_HEADS, HEAD_DIM)
            q = _apply_rope(q, cos, sin)
            k = _apply_rope(k, cos, sin)
            lam_init = 0.8 - 0.6 * math.exp(-0.3 * layer)
            lp = a_lambda[i].astype(jnp.float32)
            lam = jnp.exp(jnp.sum(lp[0] * lp[1])) - jnp.exp(jnp.sum(lp[2] * lp[3])) + lam_init
            o_self = _diff_attention(q, k, v, lam, lam_init, a_subln[i])
            o_mem = _memory_attention(qm, mem, a_mem_norm[i], a_w_mem_kv[i])
            x = x + jnp.concatenate([o_self, o_mem], axis=-1) @ a_w_out[i]
            x = x + _sq_relu_mlp(_rmsnorm(x, a_norm_mlp[i]), a_w_up[i], a_w_down[i])
        else:
            j = layer - N_A_LAYERS
            if j == 0:
                hk = _rmsnorm(x, kv_norm)
                kv = hk @ w_kv
                ks_ = _apply_rope(kv[..., :SELF_WIDTH].reshape(B, S, N_MOBA_HEADS, HEAD_DIM), cos, sin)
                vs_ = kv[..., SELF_WIDTH:].reshape(B, S, N_MOBA_HEADS, HEAD_DIM)
                n_blk = -(-S // MOBA_BLOCK)
                pad = n_blk * MOBA_BLOCK - S
                padw = ((0, 0), (0, pad), (0, 0), (0, 0))
                kbh = jnp.pad(ks_.astype(jnp.float32), padw).reshape(
                    B, n_blk, MOBA_BLOCK, N_MOBA_HEADS, HEAD_DIM).transpose(0, 3, 1, 2, 4)
                vbh = jnp.pad(vs_.astype(jnp.float32), padw).reshape(
                    B, n_blk, MOBA_BLOCK, N_MOBA_HEADS, HEAD_DIM).transpose(0, 3, 1, 2, 4)
                kmean = jnp.mean(kbh, axis=3)
            h = _rmsnorm(x, b_norm_attn[j])
            z = h @ b_w_in[j]
            q = _apply_rope(z[..., :SELF_WIDTH].reshape(B, S, N_MOBA_HEADS, HEAD_DIM), cos, sin)
            qm = z[..., SELF_WIDTH:].reshape(B, S, N_MEM_HEADS, HEAD_DIM)
            o_self = _moba_attention(q, kbh, vbh, kmean).astype(x.dtype)
            o_mem = _memory_attention(qm, mem, b_mem_norm[j], b_w_mem_kv[j])
            x = x + jnp.concatenate([o_self, o_mem], axis=-1) @ b_w_out[j]
            x = x + _sq_relu_mlp(_rmsnorm(x, b_norm_mlp[j]), b_w_up[j], b_w_down[j])
    return _rmsnorm(x, final_norm)


def setup_inputs(seed=0):
    out = dict(first_inputs(seed))
    for name, value in second_inputs(seed + 1).items():
        if name != "x":
            out[name + "_2"] = value
    return out


def reference(
    x, meta_tokens, a_norm_g, a_w_in, a_q_norm_g, a_kv_norm_g, a_w_uq, a_w_ukv, a_w_out,
    b_norm_g, b_w_in, b_conv_w, b_conv_b, b_w_rg, b_b_rg, b_w_ig, b_b_ig, b_lam, b_w_out,
    final_norm_g, mem_2, a_norm_attn_2, a_w_in_2, a_lambda_2, a_subln_2, a_mem_norm_2,
    a_w_mem_kv_2, a_w_out_2, a_norm_mlp_2, a_w_up_2, a_w_down_2, kv_norm_2, w_kv_2,
    b_norm_attn_2, b_w_in_2, b_mem_norm_2, b_w_mem_kv_2, b_w_out_2, b_norm_mlp_2, b_w_up_2,
    b_w_down_2, final_norm_2,
):
    x = first_block(
        x, meta_tokens, a_norm_g, a_w_in, a_q_norm_g, a_kv_norm_g, a_w_uq, a_w_ukv, a_w_out,
        b_norm_g, b_w_in, b_conv_w, b_conv_b, b_w_rg, b_b_rg, b_w_ig, b_b_ig, b_lam, b_w_out,
        final_norm_g,
    )
    return second_block(
        x, mem_2, a_norm_attn_2, a_w_in_2, a_lambda_2, a_subln_2, a_mem_norm_2, a_w_mem_kv_2,
        a_w_out_2, a_norm_mlp_2, a_w_up_2, a_w_down_2, kv_norm_2, w_kv_2, b_norm_attn_2,
        b_w_in_2, b_mem_norm_2, b_w_mem_kv_2, b_w_out_2, b_norm_mlp_2, b_w_up_2, b_w_down_2,
        final_norm_2,
    )


_drawn_inputs = setup_inputs


def setup_inputs(seed=0):
    import zlib

    import numpy as np

    out = dict(_drawn_inputs(seed))
    spreads = {}
    factors = {'a_norm_g': 8.0,
     'a_q_norm_g': 8.0,
     'a_kv_norm_g': 8.0,
     'b_norm_g': 8.0,
     'b_b_rg': 8.0,
     'b_b_ig': 8.0,
     'final_norm_g': 4.003,
     'a_norm_attn_2': 2.676,
     'a_subln_2': 3.959,
     'a_mem_norm_2': 8.0,
     'a_norm_mlp_2': 3.228,
     'kv_norm_2': 8.0,
     'b_norm_attn_2': 8.0,
     'b_mem_norm_2': 8.0,
     'b_norm_mlp_2': 11.733,
     'final_norm_2': 8.831}
    for name, (base, spread) in spreads.items():
        noise = np.random.default_rng([zlib.crc32(name.encode()), seed]).standard_normal(out[name].shape)
        drawn = base * np.exp(spread * noise) if base else spread * noise
        out[name] = __import__('jax').numpy.asarray(drawn.astype(out[name].dtype))
    for name, factor in factors.items():
        out[name] = (out[name] * factor).astype(out[name].dtype)
    return out
```

```python
from collections import deque
from contextlib import ExitStack

import numpy as np

import concourse.bass as bass
from concourse import mybir

F32 = mybir.dt.float32
F32R = mybir.dt.float32r
ACT = mybir.ActivationFunctionType
ALU = mybir.AluOpType
AX_X = mybir.AxisListType.X

P = 128
D = 1024
DT = D // P
SEQ = 256
META = 16
T1 = META + SEQ
EPS = 1e-6
NEG = -1e30
CHUNK = 2048
PAD = 3

HEADS, NOPE, ROPE, Q_LORA, KV_LORA = 8, 128, 64, 384, 256
DIFF_HEADS, MOBA_HEADS, MEM_HEADS, DH = 6, 12, 4, 64
D_FF = 4096
LAMBDA_INIT = 0.8 - 0.6 * 1.0
LRU_C = 8.0

SHAPES = {
    "a_in": (8, 256), "a_uq": (3, 512), "a_ukv": (2, 1024), "a_out": (8, 256),
    "b_in": (8, 256), "b_gates": (8, 256), "b_out": (8, 256),
    "mem": (8, 256), "in2": (8, 256), "out2": (8, 256), "up": (8, 256), "down": (8, 256),
}
UP_DOWN = [("up", 0), ("up", 1), ("down", 0), ("up", 2), ("down", 1), ("up", 3), ("down", 2), ("down", 3)]


def chunk_order():
    order = [("a_in", 0, i) for i in range(7)]
    order += [("a_uq", 0, i) for i in range(3)] + [("a_ukv", 0, i) for i in range(2)]
    order += [("a_out", 0, i) for i in range(4)]
    order += [("b_in", 0, i) for i in range(8)] + [("b_gates", 0, i) for i in range(2)]
    order += [("b_out", 0, i) for i in range(4)]
    order += [("mem", 0, i) for i in range(2)]
    for layer in range(2):
        order += [("in2", layer, i) for i in range(10)] + [("out2", layer, i) for i in range(4)]
        for kind, quarter in UP_DOWN:
            order += [(kind, layer, 4 * quarter + i) for i in range(4)]
        if layer == 0:
            order += [("mem", 1, i) for i in range(2)]
    return order


VECTORS = [("a_norm_g", 8), ("a_q_norm_g", 3), ("a_kv_norm_g", 2), ("b_norm_g", 8),
           ("b_conv_w", 32), ("b_conv_b", 8), ("b_b_rg", 8), ("b_b_ig", 8), ("b_lam", 8),
           ("final_norm_g", 8), ("a_norm_attn_2", 8), ("a_subln_2", 1), ("a_mem_norm_2", 8),
           ("a_norm_mlp_2", 8), ("kv_norm_2", 8), ("b_norm_attn_2", 8), ("b_mem_norm_2", 8),
           ("b_norm_mlp_2", 8), ("final_norm_2", 8)]
VEC_AT, _n = {}, 0
for _name, _k in VECTORS:
    VEC_AT[_name] = _n
    _n += _k
N_VEC = _n
C_IDENT, C_ONES, C_MASK, C_COS, C_SIN, C_LAM = 0, 128, 256, 528, 800, 1072
N_CONST = 1072 + 4 * DH


class Queue:

    def __init__(self, sem):
        self.sem, self.count, self.items, self.waited = sem, 0, [], {}

    def do(self, issue, after=(), signal=True):
        need = {}
        for token in flat(after):
            if token[1] > max(self.waited.get(token[0].name, 0), need.get(token[0].name, (None, 0))[1]):
                need[token[0].name] = token
        for name, token in need.items():
            self.waited[name] = token[1]
        self.items.append((list(need.values()), issue, signal))
        if signal:
            self.count += 1
        return (self.sem, self.count)

    def last(self):
        return [(self.sem, self.count)] if self.count else []

    def emit(self, engine):
        for waits, issue, signal in self.items:
            for sem, value in waits:
                engine.wait_ge(sem, value)
            instruction = issue(engine)
            if signal:
                instruction.then_inc(self.sem, 1)


def flat(tokens):
    if tokens is None:
        return
    if isinstance(tokens, tuple) and len(tokens) == 2 and isinstance(tokens[1], int):
        yield tokens
        return
    for t in tokens:
        yield from flat(t)


class Buffers:

    def __init__(self, buffers):
        self.free = deque((b, []) for b in buffers)

    def take(self):
        return self.free.popleft()

    def give(self, buffer, tokens):
        self.free.append((buffer, tokens))


def program(nc, stream, xT, memT, vecs, consts, out, stop_after=None):
    ctx = ExitStack()
    with ctx:
        def sb(name, shape, dt=F32):
            return ctx.enter_context(nc.sbuf_tensor(name, shape, dt))

        def semaphore(name):
            return ctx.enter_context(nc.semaphore(name))

        pe, act, dve, pool = (Queue(semaphore(f"{n}_done")) for n in ("pe", "act", "dve", "pool"))
        sp_items = []

        N_RAW, N_SPLIT, N_OPERAND, N_TEMP = 3, 3, 3, 5
        raw = [sb(f"weights_raw{i}", [P, CHUNK]) for i in range(N_RAW)]
        w_hi = [sb(f"weights_hi{i}", [P, CHUNK], F32R) for i in range(N_SPLIT)]
        w_lo = [sb(f"weights_lo{i}", [P, CHUNK], F32R) for i in range(N_SPLIT)]
        operands = Buffers([(sb(f"operand_hi{i}", [P, DT, T1], F32R), sb(f"operand_lo{i}", [P, DT, T1], F32R))
                            for i in range(N_OPERAND)])
        temps = Buffers([sb(f"temp{i}", [P, 656]) for i in range(N_TEMP)])
        small = Buffers([sb(f"softmax_stats{i}", [P, 16]) for i in range(6)])
        x = sb("residual", [P, DT, T1])
        ARENA = 10960
        arena = sb("arena", [P, ARENA])
        rows = sb("rows", [P, 5, T1])
        cols = sb("cols", [P, 16])
        vec = sb("vectors", [P, N_VEC])
        const = sb("constants", [P, N_CONST])
        lru = sb("lru_scales", [P, 64])
        banks = Buffers([ctx.enter_context(nc.psum_tensor(f"bank{i}", [P, 512], F32)) for i in range(8)])

        ident = const[:, C_IDENT:C_IDENT + P]
        ones = const[:, C_ONES:C_ONES + P]
        mask = const[:, C_MASK:C_MASK + T1]
        cos = const[:, C_COS:C_COS + T1]
        sin = const[:, C_SIN:C_SIN + T1]

        def vcol(name, i=0):
            return vec[:, VEC_AT[name] + i:VEC_AT[name] + i + 1]

        def region(start, *shape):
            n = int(np.prod(shape))
            assert start + n <= ARENA
            ap = arena[:, start:start + n]
            if len(shape) == 2:
                ap = ap.rearrange("p (a b) -> p a b", a=shape[0])
            return ap

        def matmul(out, lhsT, rhs, start, stop, after=(), signal=False, shared=False):
            return pe.do(lambda e: e.matmul(out, lhsT, rhs, start=start, stop=stop, skip_group_check=shared),
                         after, signal)

        def transpose(out, in_, n, after=(), signal=False):
            return pe.do(lambda e: e.transpose(out, in_, ident[0:n, 0:n]), after, signal)

        def activate(out, in_, func, after, scale=1.0, bias=0.0, accum=None):
            if accum is None:
                return act.do(lambda e: e.activation(out, in_, func, bias=bias, scale=scale), after)
            return act.do(lambda e: e.activation(out, in_, func, bias=bias, scale=scale, accum_out=accum), after)

        def tt(out, a, b, op, after):
            return dve.do(lambda e: e.tensor_tensor(out, a, b, op), after)

        def ts(out, a, s1, op0, after, s2=None, op1=None):
            if op1 is None:
                return dve.do(lambda e: e.tensor_scalar(out, a, s1, None, op0), after)
            return dve.do(lambda e: e.tensor_scalar(out, a, s1, s2, op0, op1), after)

        def stt(out, a, s, b, op0, op1, after):
            return dve.do(lambda e: e.scalar_tensor_tensor(out, a, s, b, op0, op1), after)

        def reduce(out, in_, op, after, negate=False):
            return dve.do(lambda e: e.tensor_reduce(out, in_, AX_X, op, negate=negate), after)

        def recip(out, in_, after):
            return dve.do(lambda e: e.reciprocal(out, in_), after)

        def copy(out, in_, after):
            return dve.do(lambda e: e.tensor_copy(out, in_), after)

        def everything():
            return pe.last() + act.last() + dve.last() + pool.last()

        order = chunk_order()
        raw_sems = [semaphore(f"weights_landed{i}") for i in range(N_RAW)]
        split_tokens = {}
        raw_free, split_free = [[] for _ in range(N_RAW)], [[] for _ in range(N_SPLIT)]
        state = {"loaded": 0, "split": 0, "used": 0}

        def load_next():
            n = state["loaded"]
            if n == len(order):
                return
            state["loaded"] += 1
            kt, w = SHAPES[order[n][0]]
            sp_items.append((raw_free[n % N_RAW], raw[n % N_RAW][:, 0:kt * w], stream[n, :, 0:kt * w],
                             raw_sems[n % N_RAW]))

        def split_next():
            n = state["split"]
            if n == len(order):
                return
            state["split"] += 1
            kt, w = SHAPES[order[n][0]]
            r, s, size = n % N_RAW, n % N_SPLIT, kt * w
            landed = (raw_sems[r], 16 * (n // N_RAW + 1))
            src, hi, lo = raw[r][:, 0:size], w_hi[s][:, 0:size], w_lo[s][:, 0:size]
            t_hi = activate(hi, src, ACT.Copy, [landed, split_free[s]])
            t_lo = tt(lo, src, hi.bitcast(F32), ALU.subtract, [landed, t_hi, split_free[s]])
            split_tokens[n] = [t_hi, t_lo]
            raw_free[r] = [t_hi, t_lo]
            load_next()

        def next_chunk(kind, layer):
            n = state["used"]
            assert order[n][0] == kind and order[n][1] == layer, (order[n], kind, layer)
            while state["split"] < min(n + N_SPLIT, len(order)):
                split_next()
            state["used"] += 1
            kt, w = SHAPES[kind]
            s = n % N_SPLIT
            hi = w_hi[s][:, 0:kt * w].rearrange("p (k w) -> p k w", k=kt)
            lo = w_lo[s][:, 0:kt * w].rearrange("p (k w) -> p k w", k=kt)
            return n, hi, lo

        def chunk_done(n, token):
            split_free[n % N_SPLIT] = [token]

        class Operand:

            def __init__(self):
                (self.hi_t, self.lo_t), self.free = operands.take()
                self.ready, self.read = {}, []
                self.base = 0

            def hi(self, k, t0, t1):
                return self.hi_t[:, k, t0:t1]

            def lo(self, k, t0, t1):
                return self.lo_t[:, k, t0:t1]

            def give(self):
                operands.give((self.hi_t, self.lo_t), self.read)

        def split_tile(op, k, src, gain, after, n=1):
            T = src.shape[-1]
            hi, lo = op.hi_t[:, k:k + n, 0:T], op.lo_t[:, k:k + n, 0:T]
            if len(src.shape) == 2:
                hi, lo = op.hi_t[:, k, 0:T], op.lo_t[:, k, 0:T]
            if gain is None:
                t1 = activate(hi, src, ACT.Copy, [after, op.free])
                t2 = tt(lo, src, hi.bitcast(F32), ALU.subtract, [after, op.free, t1])
            else:
                t1 = activate(hi, src, ACT.Copy, [after, op.free], scale=gain)
                t2 = stt(lo, src, gain, hi.bitcast(F32), ALU.mult, ALU.subtract, [after, op.free, t1])
            for i in range(n):
                op.ready[k + i] = [t1, t2]
            return [t1, t2]

        def three(out, w_h, w_l, x_h, x_l, first, last, after, signal, shared=False):
            matmul(out, w_h, x_h, first, False, after, shared=shared)
            matmul(out, w_h, x_l, False, False, shared=shared)
            return matmul(out, w_l, x_h, False, last, signal=signal, shared=shared)

        def project(kind, layer, op, T, evacuate, t0=0, base=0):
            n, hi, lo = next_chunk(kind, layer)
            kt, w = SHAPES[kind]
            per = 2 if 2 * T <= 512 else 1
            for m0 in range(0, w // P, per):
                bank, free = banks.take()
                for j in range(per):
                    m = m0 + j
                    for k in range(kt):
                        token = three(bank[:, j * T:(j + 1) * T],
                                      hi[:, k, m * P:(m + 1) * P], lo[:, k, m * P:(m + 1) * P],
                                      op.hi(base + k, t0, t0 + T), op.lo(base + k, t0, t0 + T),
                                      k == 0, k == kt - 1, [split_tokens[n], free, op.ready[base + k]],
                                      k == kt - 1 and j == per - 1)
                view = bank[:, 0:per * T].rearrange("p (n t) -> p n t", n=per)
                banks.give(bank, evacuate(order[n][2] * (w // P) + m0, view, token))
            chunk_done(n, token)
            op.read = [token]

        def project_tokens(kind, layer, op, starts, evacuate, base=0):
            n, hi, lo = next_chunk(kind, layer)
            kt, w = SHAPES[kind]
            for i, t0 in enumerate(starts):
                for c0 in range(0, w, 512):
                    c1 = min(c0 + 512, w)
                    bank, free = banks.take()
                    for k in range(kt):
                        after = [split_tokens[n], free, op.ready[base + k]]
                        o, x_h, x_l = bank[:, 0:c1 - c0], op.hi(base + k, t0, t0 + P), op.lo(base + k, t0, t0 + P)
                        matmul(o, x_h, hi[:, k, c0:c1], k == 0, False, after)
                        matmul(o, x_h, lo[:, k, c0:c1], False, False)
                        token = matmul(o, x_l, hi[:, k, c0:c1], False, k == kt - 1, signal=k == kt - 1)
                    banks.give(bank, evacuate(i, c0, bank[:, 0:c1 - c0], token))
            chunk_done(n, token)
            op.read = [token]

        def square_sum(src, sq, after):
            T = src.shape[-1]
            t1 = activate(sq, src, ACT.Square, after)
            temp, free = temps.take()
            t2 = reduce(temp[:, 0:T], sq.rearrange("p k t -> p t k"), ALU.add, [t1, free])
            return temp, t2

        def rstd_row(temp, token, n_features, T, row, after):
            bank, free = banks.take()
            t1 = matmul(bank[:, 0:T], ones, temp[:, 0:T], True, True, [token, free], True)
            t2 = ts(row, bank[:, 0:T], 1.0 / n_features, ALU.mult, [t1, after], EPS, ALU.add)
            banks.give(bank, [t2])
            t3 = activate(row, row, ACT.Sqrt, [t2])
            return t1, recip(row, row, [t3])

        def rstd_col(temp, token, n_features, starts, col, after):
            bank, free = banks.take()
            for i, t0 in enumerate(starts):
                t1 = matmul(bank[:, i:i + 1], temp[:, t0:t0 + P], ones[:, 0:1], True, True, [token, free],
                            i == len(starts) - 1)
            t2 = ts(col, bank[:, 0:len(starts)], 1.0 / n_features, ALU.mult, [t1, after], EPS, ALU.add)
            banks.give(bank, [t2])
            t3 = activate(col, col, ACT.Sqrt, [t2])
            return t1, recip(col, col, [t3])

        SWAP = [(r + 16) % 32 for r in range(32)]

        def rope(out, psum, n, T, cos_row, sin_row, token, after):
            a, free_a = temps.take()
            b, free_b = temps.take()
            ap = a[:, 0:n * T].rearrange("p (n t) -> p n t", n=n)
            bp = b[:, 0:n * T].rearrange("p (n t) -> p n t", n=n)
            cb = cos_row.unsqueeze(1).to_broadcast([P, n, T])
            sb_ = sin_row.unsqueeze(1).to_broadcast([P, n, T])
            t1 = activate(ap, psum, ACT.Copy, [token, free_a])
            t2 = dve.do(lambda e: e.stream_shuffle(b[:, 0:n * T], a[:, 0:n * T], SWAP), [t1, free_b])
            t3 = tt(bp, bp, sb_, ALU.mult, [t2, after])
            t4 = tt(ap, ap, cb, ALU.mult, [t2, after])
            t5 = tt(out, ap, bp, ALU.add, [t3, t4, after])
            temps.give(a, [t5])
            temps.give(b, [t5])
            return [t1], [t5]

        def softmax(prob, psum, scale, mask_ap, token, free, stats, j):
            qn = psum.shape[0]
            top, neg = stats[0:qn, 4 * j:4 * j + 1], stats[0:qn, 4 * j + 1:4 * j + 2]
            total, inv = stats[0:qn, 4 * j + 2:4 * j + 3], stats[0:qn, 4 * j + 3:4 * j + 4]
            if mask_ap is not None:
                t1 = dve.do(lambda e: e.tensor_tensor_reduce(prob, psum, mask_ap, scale, 3.0 * NEG, ALU.add,
                                                             ALU.max, top), [token, free])
                t2 = ts(neg, top, -1.0, ALU.mult, [t1])
                t3 = activate(prob, prob, ACT.Exp, [t2], bias=neg, accum=total)
                freed = [t1]
            else:
                t1 = reduce(top, psum, ALU.max, [token, free])
                t2 = ts(neg, top, -scale, ALU.mult, [t1])
                t3 = activate(prob, psum, ACT.Exp, [t2, free], scale=scale, bias=neg, accum=total)
                freed = [t1, t3]
            t4 = recip(inv, total, [t3])
            return freed, [t3], [t4], inv

        for _ in range(N_RAW):
            load_next()
        load_sem = [semaphore(f"{n}_landed") for n in ("residual", "vectors", "constants", "memory0", "memory1")]
        act.do(lambda e: e.dma_start(x[:], xT.rearrange("(k p) t -> p k t", p=P)).then_inc(load_sem[0], 16), signal=False)
        act.do(lambda e: e.dma_start(vec[:], vecs).then_inc(load_sem[1], 16), signal=False)
        act.do(lambda e: e.dma_start(const[:], consts).then_inc(load_sem[2], 16), signal=False)
        X_IN, VEC_IN, CONST_IN = [(s, 16) for s in load_sem[0:3]]
        loaded = [X_IN, VEC_IN, CONST_IN]

        lam_ap = vec[:, VEC_AT["b_lam"]:VEC_AT["b_lam"] + 8]
        L = [lru[:, 8 * i:8 * i + 8] for i in range(6)]
        t = activate(L[0], lam_ap, ACT.Abs, loaded)
        t = activate(L[1], L[0], ACT.Exp, [t], scale=-1.0)
        t = ts(L[0], L[1], 2.0, ALU.add, [t])
        t = recip(L[2], L[0], [t])
        t = tt(L[0], L[1], L[2], ALU.mult, [t])
        t = tt(L[1], L[0], L[0], ALU.mult, [t])
        terms = [1.0 / (2 * i + 1) for i in range(10)]
        t = ts(L[2], L[1], terms[9], ALU.mult, [t], terms[8], ALU.add)
        for i in range(7, -1, -1):
            t = tt(L[3], L[2], L[1], ALU.mult, [t])
            t = ts(L[2], L[3], terms[i], ALU.add, [t])
        t = stt(L[3], L[0], 2.0, L[2], ALU.mult, ALU.mult, [t])
        t = ts(L[2], lam_ap, -1.0, ALU.mult, [t], 0.0, ALU.max)
        t = tt(L[3], L[3], L[2], ALU.add, [t])
        POS_SCALE, NEG_SCALE = L[4], L[5]
        t = ts(POS_SCALE, L[3], LRU_C, ALU.mult, [t])
        LRU_READY = ts(NEG_SCALE, L[3], -LRU_C, ALU.mult, [t])
        lam4 = const[:, C_LAM:C_LAM + 4 * DH].rearrange("p (a b d) -> p a b d", a=2, b=2)
        lam_prod = region(0, 2, DH)
        t = tt(lam_prod, lam4[:, :, 0, :], lam4[:, :, 1, :], ALU.mult, loaded)
        t = reduce(cols[:, 8:10], lam_prod, ALU.add, [t])
        t = activate(cols[:, 8:10], cols[:, 8:10], ACT.Exp, [t])
        t = tt(cols[:, 10:11], cols[:, 9:10], cols[:, 8:9], ALU.subtract, [t])
        t = ts(cols[:, 11:12], cols[:, 10:11], -LAMBDA_INIT, ALU.add, [t])
        NEG_LAMBDA, SUB_GAIN = cols[:, 11:12], cols[:, 12:13]
        SMALL_READY = [t, ts(SUB_GAIN, vcol("a_subln_2"), 1.0 - LAMBDA_INIT, ALU.mult, loaded)]

        R, RQ, CR, SR, RKV = (rows[:, i, :] for i in range(5))
        lat = region(7700, 5, T1)
        V16, V = region(5712, 1024), region(6736, 2, 1024)
        qn, kn, qr, kr = region(0, 8, T1), region(2176, 8, T1), region(4352, 4, T1), region(5440, 1, T1)
        silu_gate = region(8784, 8, T1)

        temp, t = square_sum(x[:], region(0, 8, T1), [loaded, SMALL_READY])
        t_pe, R_READY = rstd_row(temp, t, D, T1, R, [])
        temps.give(temp, [t_pe])

        op = Operand()
        for k in range(DT):
            split_tile(op, k, x[:, k, :], vcol("a_norm_g", k), loaded)

        t1 = tt(CR, cos, R, ALU.mult, [R_READY])
        ROPE_READY = [t1, tt(SR, sin, R, ALU.mult, [R_READY])]
        lat_tokens, kr_tokens, gate_tokens = [], [], []

        lat = region(6000, 5, T1)

        def evacuate_a_in(m, psum, token):
            if m < 5:
                lat_tokens.append(tt(lat[:, m, :], psum[:, 0, :], R, ALU.mult, [token, R_READY]))
                return [lat_tokens[-1]]
            if m == 5:
                freed, done = rope(kr, psum, 1, T1, CR, SR, token, ROPE_READY)
                kr_tokens.extend(done)
                return freed
            g = silu_gate[:, m - 6, :]
            t1 = tt(g, psum[:, 0, :], R, ALU.mult, [token, R_READY])
            gate_tokens.append(activate(g, g, ACT.Silu, [t1]))
            return [t1]

        for _ in range(3):
            project("a_in", 0, op, T1, evacuate_a_in)
        sq = region(0, 5, T1)
        temp, t = square_sum(lat[:, 0:3, :], sq[:, 0:3, :], [lat_tokens, R_READY, pe.last()])
        t_pe, RQ_READY = rstd_row(temp, t, Q_LORA, T1, RQ, [])
        temps.give(temp, [t_pe])
        temp, t = square_sum(lat[:, 3:5, :], sq[:, 3:5, :], [lat_tokens])
        t_pe, RKV_READY = rstd_row(temp, t, KV_LORA, T1, RKV, [])
        kv_starts = (0, META, META + P)
        t_pe2, RKV_COL_READY = rstd_col(temp, t, KV_LORA, kv_starts, cols[:, 0:3], [])
        temps.give(temp, [t_pe, t_pe2])
        latent = Operand()
        for k in range(5):
            split_tile(latent, k, lat[:, k, :], vcol("a_q_norm_g", k) if k < 3 else vcol("a_kv_norm_g", k - 3),
                       lat_tokens)
        LAT_READ = everything()
        for _ in range(4):
            project("a_in", 0, op, T1, evacuate_a_in)
        op.give()
        t1 = tt(CR, cos, RQ, ALU.mult, [RQ_READY, kr_tokens])
        ROPE_READY = [t1, tt(SR, sin, RQ, ALU.mult, [RQ_READY, kr_tokens])]
        q_tokens = {}

        def evacuate_q(m, psum, token):
            if m < 8:
                q_tokens[m] = [tt(qn[:, m, :], psum[:, 0, :], RQ, ALU.mult, [token, RQ_READY, LAT_READ])]
                return q_tokens[m]
            freed, q_tokens[m] = rope(qr[:, m - 8:m - 7, :], psum, 1, T1, CR, SR, token, ROPE_READY)
            return freed

        for _ in range(3):
            project("a_uq", 0, latent, T1, evacuate_q)
        k_tokens = {}

        def evacuate_k(m, psum, token):
            k_tokens[m] = tt(kn[:, m, :], psum[:, 0, :], RKV, ALU.mult, [token, RKV_READY, LAT_READ])
            return [k_tokens[m]]

        project("a_ukv", 0, latent, T1, evacuate_k, base=3)
        v_tokens = []

        def evacuate_v(i, c0, psum, token):
            n, dst = (META, V16[0:META, c0:c0 + 512]) if i == 0 else (P, V[:, i - 1, c0:c0 + 512])
            v_tokens.append(activate(dst, psum[0:n, :], ACT.Copy, [token, RKV_COL_READY, LAT_READ],
                                     scale=cols[0:n, i:i + 1]))
            return [v_tokens[-1]]

        project_tokens("a_ukv", 0, latent, kv_starts, evacuate_v, base=3)
        latent.give()

        TILES_A = [(0, META, META), (META, P, META + P), (META + P, P, T1)]
        PROB_AT = [0, META, META + META + P]
        heads_in_flight = deque()
        y_op = Operand()

        def scores_a(h):
            prob, free = temps.take()
            stats, sfree = small.take()
            done = []
            pair, half = h // 2, 64 * (h % 2)
            for j, (q0, nq, nk) in enumerate(TILES_A):
                bank, bfree = banks.take()
                matmul(bank[0:nq, 0:nk], qn[:, h, q0:q0 + nq], kn[:, h, 0:nk], True, False,
                       [bfree, q_tokens[h], k_tokens[h]])
                token = matmul(bank[0:nq, 0:nk], qr[half:half + ROPE, pair, q0:q0 + nq],
                               kr[half:half + ROPE, 0, 0:nk], False, True, [q_tokens[8 + pair], kr_tokens], True)
                at = PROB_AT[j]
                m0 = 144 if j == 0 else (128 if j == 1 else 0)
                freed, t_p, t_i, inv = softmax(prob[0:nq, at:at + nk], bank[0:nq, 0:nk], (NOPE + ROPE) ** -0.5,
                                               mask[0:nq, m0:m0 + nk], token, [free, sfree], stats, j)
                banks.give(bank, freed)
                done.append(ts(prob[0:nq, at:at + nk], prob[0:nq, at:at + nk], inv, ALU.mult, [t_p, t_i]))
            small.give(stats, done)
            heads_in_flight.append((h, prob, done))

        def values_a():
            h, prob, done = heads_in_flight.popleft()
            bank16, free16 = banks.take()
            bank, bfree = banks.take()
            for j, (q0, nq, nk) in enumerate(TILES_A):
                at = PROB_AT[j]
                t16 = transpose(bank16[0:META, q0:q0 + nq], prob[0:nq, at:at + META], nq, [done[j], free16, bfree],
                                j == 2)
                if j:
                    t_pe = transpose(bank[:, q0 - META:q0 - META + nq], prob[0:nq, at + META:at + META + P], nq,
                                     signal=True)
                if j == 2:
                    t_pe = transpose(bank[:, SEQ:SEQ + P], prob[0:nq, at + META + P:at + T1], nq, signal=True)
            temps.give(prob, [t_pe])
            pt, free = temps.take()
            t1 = activate(pt[0:META, 0:T1], bank16[0:META, 0:T1], ACT.Copy, [t16, free])
            t2 = activate(pt[:, T1:T1 + SEQ + P], bank[:, 0:SEQ + P], ACT.Copy, [t_pe, free])
            banks.give(bank16, [t1])
            banks.give(bank, [t2])
            o, ofree = banks.take()
            cs = slice(h * P, (h + 1) * P)
            matmul(o[:, 0:T1], V16[0:META, cs], pt[0:META, 0:T1], True, False, [ofree, t1, t2, v_tokens])
            matmul(o[:, META:T1], V[:, 0, cs], pt[:, T1:T1 + SEQ], False, False)
            t3 = matmul(o[:, META + P:T1], V[:, 1, cs], pt[:, T1 + SEQ:T1 + SEQ + P], False, True, signal=True)
            temps.give(pt, [t3])
            y, yfree = temps.take()
            t4 = tt(y[:, 0:T1], o[:, 0:T1], silu_gate[:, h, :], ALU.mult, [t3, yfree, gate_tokens])
            banks.give(o, [t4])
            temps.give(y, split_tile(y_op, h, y[:, 0:T1], None, t4))

        for h in range(HEADS):
            scores_a(h)
            if h:
                values_a()
        values_a()

        x_tokens = {}

        def add_to_residual(T, t0):
            def evacuate(m, psum, token):
                n = psum.shape[1]
                t1 = tt(x[:, m:m + n, t0:t0 + T], x[:, m:m + n, t0:t0 + T], psum, ALU.add, [token])
                for i in range(n):
                    x_tokens[m + i] = t1
                return [t1]
            return evacuate

        FENCE = everything()
        next_op = Operand()

        def residual_then_split(T, t0, op, gain):
            add = add_to_residual(T, t0)

            def evacuate(m, psum, token):
                freed = add(m, psum, token)
                for i in range(psum.shape[1]):
                    split_tile(op, m + i, x[:, m + i, t0:t0 + T], vcol(gain, m + i), freed)
                return freed
            return evacuate

        for _ in range(4):
            project("a_out", 0, y_op, T1, residual_then_split(T1, 0, next_op, "b_norm_g"))
        y_op.give()

        U = T1 + PAD
        u = region(0, 8, U)
        a_gate = region(0, 8, U)
        uc, rg = region(2200, 8, T1), region(4376, 8, T1)
        ig, silu_b = region(6552, 8, T1), region(8728, 8, SEQ)
        temp, t = square_sum(x[:], region(4376, 8, T1), [list(x_tokens.values()), FENCE])
        t_pe, R_READY = rstd_row(temp, t, D, T1, R, [FENCE])
        temps.give(temp, [t_pe])
        t_pad = dve.do(lambda e: e.memset(u[:, :, 0:PAD], 0.0), [FENCE])
        uc_op = Operand()
        uc_tokens, rg_tokens, ig_tokens, gate_tokens = {}, {}, {}, {}

        def evacuate_u(m, psum, token):
            if m >= 8:
                g = silu_b[:, m - 8:m - 8 + psum.shape[1], :]
                row = R[:, META:T1].unsqueeze(1).to_broadcast([P, psum.shape[1], SEQ])
                t1 = tt(g, psum, row, ALU.mult, [token, R_READY, FENCE])
                gate_tokens[m] = activate(g, g, ACT.Silu, [t1])
                return [t1]
            t0 = tt(u[:, m, PAD:U], psum[:, 0, :], R, ALU.mult, [token, R_READY, FENCE])
            c = uc[:, m, :]
            t1 = activate(c, u[:, m, 0:T1], ACT.Identity, [t0, t_pad, FENCE], scale=vcol("b_conv_w", m),
                          bias=vcol("b_conv_b", m))
            for j in range(1, 4):
                t1 = stt(c, u[:, m, j:j + T1], vcol("b_conv_w", 8 * j + m), c, ALU.mult, ALU.add, [t1])
            uc_tokens[m] = t1
            split_tile(uc_op, m, c, None, t1)
            return [t0]

        for _ in range(4):
            project("b_in", 0, next_op, T1, evacuate_u)
        for _ in range(4):
            project("b_in", 0, next_op, SEQ, evacuate_u, t0=META)
        next_op.give()

        def block_gates(bias, dst, tokens, use):
            n, hi, lo = next_chunk("b_gates", 0)
            for m in range(8):
                bank, free = banks.take()
                for k in range(2):
                    token = three(bank[:, 0:T1], hi[:, 2 * (m // 2) + k, P * (m % 2):P * (m % 2) + P],
                                  lo[:, 2 * (m // 2) + k, P * (m % 2):P * (m % 2) + P],
                                  uc_op.hi(2 * (m // 2) + k, 0, T1), uc_op.lo(2 * (m // 2) + k, 0, T1),
                                  k == 0, k == 1, [split_tokens[n], free, uc_op.ready[2 * (m // 2) + k]], k == 1)
                tokens[m] = activate(dst[:, m, :], bank[:, 0:T1], ACT.Sigmoid, [token, FENCE, t_dead],
                                     bias=vcol(bias, m))
                banks.give(bank, [tokens[m]])
            chunk_done(n, token)
            uc_op.read = [token]

        t_dead = R_READY
        block_gates("b_b_rg", rg, rg_tokens, 0)
        block_gates("b_b_ig", ig, ig_tokens, 1)
        uc_op.give()
        a_tokens, th_tokens = {}, {}
        for m in range(8):
            a_tokens[m] = activate(a_gate[:, m, 0:T1], rg[:, m, :], ACT.Exp,
                                   [rg_tokens[m], list(uc_tokens.values()), LRU_READY], scale=NEG_SCALE[:, m:m + 1])
            th_tokens[m] = activate(rg[:, m, :], rg[:, m, :], ACT.Tanh, [a_tokens[m]],
                                    scale=POS_SCALE[:, m:m + 1])
        sqrt_tokens, in_tokens = {}, {}
        for m in range(8):
            a, th, inp = a_gate[:, m, 0:T1], rg[:, m, :], ig[:, m, :]
            temp, free = temps.take()
            t1 = tt(temp[:, 0:T1], a, a, ALU.mult, [a_tokens[m], free])
            t2 = stt(th, temp[:, 0:T1], 1.0, th, ALU.add, ALU.mult, [t1, th_tokens[m]])
            temps.give(temp, [t2])
            sqrt_tokens[m] = activate(th, th, ACT.Sqrt, [t2])
            in_tokens[m] = tt(inp, inp, uc[:, m, :], ALU.mult, [ig_tokens[m], uc_tokens[m]])
        y_op = Operand()
        for m in range(8):
            a, mult, inp = a_gate[:, m, 0:T1], rg[:, m, :], ig[:, m, :]
            t1 = tt(inp[:, 1:T1], inp[:, 1:T1], mult[:, 1:T1], ALU.mult, [sqrt_tokens[m], in_tokens[m]])
            h_out = uc[:, m, :]
            t2 = dve.do(lambda e, h_out=h_out, a=a, inp=inp: e.tensor_tensor_scan(h_out, a, inp, 0.0, ALU.mult,
                                                                               ALU.add),
                        [t1, uc_op.ready[m]])
            temp, free = temps.take()
            t3 = tt(temp[:, 0:SEQ], uc[:, m, META:T1], silu_b[:, m, :], ALU.mult,
                    [t2, free, list(gate_tokens.values())])
            temps.give(temp, split_tile(y_op, m, temp[:, 0:SEQ], None, t3))
        FENCE = everything()
        xs = x[:, :, META:T1]

        mem = region(0, 8, SEQ)
        MK, MV = region(6656, 2, SEQ), region(7168, 2, SEQ)
        SQ = region(8704, 8, SEQ)
        R_MEM, MEM_COL = rows[:, 4, 0:SEQ], cols[:, 4:6]
        starts2 = (0, P)

        def load_memory(layer, gain):
            act.do(lambda e: e.dma_start(mem, memT.rearrange("(k p) t -> p k t", p=P))
                   .then_inc(load_sem[3 + layer], 16), FENCE, signal=False)
            landed = (load_sem[3 + layer], 16)
            op = Operand()
            for k in range(DT):
                split_tile(op, k, mem[:, k, :], vcol(gain, k), [landed])
            return op, landed

        mem_tokens = {}

        def memory_keys_values(layer, op, ready):
            def evacuate_mk(m, psum, token):
                row = R_MEM.unsqueeze(1).to_broadcast([P, 2, SEQ])
                mem_tokens["k"] = tt(MK, psum, row, ALU.mult, [token, ready, FENCE])
                return [mem_tokens["k"]]

            def evacuate_mv(i, c0, psum, token):
                mem_tokens["v", i] = activate(MV[:, i, :], psum, ACT.Copy, [token, ready, FENCE],
                                              scale=cols[:, 4 + i:5 + i])
                return [mem_tokens["v", i]]

            project("mem", layer, op, SEQ, evacuate_mk)
            project_tokens("mem", layer, op, starts2, evacuate_mv)
            op.give()

        mem_op, landed = load_memory(0, "a_mem_norm_2")
        temp, t = square_sum(mem, SQ, [landed, FENCE])
        t_pe1, t1 = rstd_row(temp, t, D, SEQ, R_MEM, [FENCE])
        t_pe2, t2 = rstd_col(temp, t, D, starts2, MEM_COL, [FENCE])
        temps.give(temp, [t_pe1, t_pe2])
        MEM_READY = [t1, t2]

        for _ in range(4):
            project("b_out", 0, y_op, SEQ, add_to_residual(SEQ, META))
        y_op.give()

        temp, t = square_sum(xs, SQ, [list(x_tokens.values()), t])
        t_pe, R_READY = rstd_row(temp, t, D, SEQ, R[:, 0:SEQ], [FENCE])
        temps.give(temp, [t_pe])
        memory_keys_values(0, mem_op, MEM_READY)
        op = Operand()
        for k in range(DT):
            x_tokens[k] = stt(xs[:, k, :], xs[:, k, :], vcol("final_norm_g", k), R[:, 0:SEQ], ALU.mult, ALU.mult,
                              [R_READY, x_tokens[k]])
            split_tile(op, k, xs[:, k, :], vcol("a_norm_attn_2", k), x_tokens[k])

        q = region(0, 6, SEQ)
        kk = region(1536, 6, SEQ)
        vv = region(3072, 2, 768)
        qm = region(4608, 2, SEQ)
        o_tok = region(5120, 2, 768)
        RC = R[:, 0:SEQ]
        CR2, SR2, R2 = CR[:, 0:SEQ], SR[:, 0:SEQ], RQ[:, 0:SEQ]
        X_COL = cols[:, 0:2]
        TILES = [(0, P, P), (P, P, SEQ)]
        scale = DH ** -0.5

        def residual_statistics(row, with_col):
            temp, t = square_sum(xs, SQ, [list(x_tokens.values()), FENCE])
            t_pe, t_row = rstd_row(temp, t, D, SEQ, row, FENCE)
            read, ready = [t_pe], [t_row]
            if with_col:
                t_pe, t_col = rstd_col(temp, t, D, starts2, X_COL, FENCE)
                read.append(t_pe)
                ready.append(t_col)
            temps.give(temp, read)
            return ready

        def rope_rows(ready):
            t1 = tt(CR2, cos[:, 0:SEQ], RC, ALU.mult, [ready, FENCE])
            return [ready, t1, tt(SR2, sin[:, 0:SEQ], RC, ALU.mult, [ready, FENCE])]

        tokens2 = {}

        def evacuate_rope(dst, name, first):
            def evacuate(m, psum, token):
                m -= first
                freed, done = rope(dst[:, m:m + 2, :], psum, 2, SEQ, CR2, SR2, token, [ready_rows, FENCE])
                tokens2[name, m] = tokens2[name, m + 1] = done
                return freed
            return evacuate

        def evacuate_v2(base):
            def evacuate(i, c0, psum, token):
                t1 = activate(vv[:, i, base:base + 256], psum, ACT.Copy, [token, ready_rows, FENCE],
                              scale=cols[:, i:i + 1])
                tokens2.setdefault("v", []).append(t1)
                return [t1]
            return evacuate

        def evacuate_qm(m, psum, token):
            row = RC.unsqueeze(1).to_broadcast([P, 2, SEQ])
            t1 = tt(qm, psum, row, ALU.mult, [token, ready_rows, FENCE])
            tokens2["qm"] = [t1]
            return [t1]

        def score_tile(prob, free, stats, sfree, qt, kt_, p0, tiles, masked, after):
            done = []
            for j, (q0, nq, nk) in enumerate(tiles):
                bank, bfree = banks.take()
                token = matmul(bank[:, 0:nk], qt[p0:p0 + DH, q0:q0 + nq], kt_[p0:p0 + DH, 0:nk], True, True,
                               [bfree, after], True)
                at = 0 if j == 0 else SEQ
                m_ap = None if not masked else (mask[:, 144:144 + P] if j == 0 else mask[:, META:META + SEQ])
                freed, t_p, t_i, inv = softmax(prob[:, at:at + nk], bank[:, 0:nk], scale, m_ap, token,
                                               [free, sfree], stats, j)
                banks.give(bank, freed)
                done.append((t_p, t_i, inv, at, nk))
            return done

        def transposed(prob, done, causal):
            bank, bfree = banks.take()
            transpose(bank[:, 0:P], prob[:, 0:P], P, [done, bfree])
            t_pe = transpose(bank[:, P:SEQ], prob[:, SEQ:SEQ + P], P, signal=True)
            if causal:
                t_pe = transpose(bank[:, SEQ:SEQ + P], prob[:, SEQ + P:2 * SEQ], P, signal=True)
            else:
                transpose(bank[:, SEQ:SEQ + P], prob[:, P:SEQ], P)
                t_pe = transpose(bank[:, SEQ + P:2 * SEQ], prob[:, SEQ + P:2 * SEQ], P, signal=True)
            temps.give(prob, [t_pe])
            n = 3 * P if causal else 2 * SEQ
            pt, free = temps.take()
            t1 = activate(pt[:, 0:n], bank[:, 0:n], ACT.Copy, [t_pe, free])
            banks.give(bank, [t1])
            return pt, [t1]

        def normalize(prob, done):
            return [ts(prob[:, at:at + nk], prob[:, at:at + nk], inv, ALU.mult, [t_p, t_i])
                    for t_p, t_i, inv, at, nk in done]

        def head_pairs(n_heads, qt, kt_, v_of, causal, q_after, v_after, y_first):
            waiting = deque()
            state_o = {}

            def values():
                h, prob, done, stats = waiting.popleft()
                pt, t_pt = transposed(prob, done, causal)
                p0 = DH * (h % 2)
                if p0 == 0:
                    state_o["o"] = banks.take()
                o, ofree = state_o["o"]
                n0 = SEQ if causal else 2 * SEQ
                matmul(o[p0:p0 + DH, 0:SEQ], v_of(0, h), pt[:, 0:SEQ], True, False, [ofree, t_pt, v_after])
                if causal:
                    t3 = matmul(o[p0:p0 + DH, P:SEQ], v_of(1, h), pt[:, SEQ:SEQ + P], False, True, signal=True)
                else:
                    t3 = matmul(o[p0:p0 + DH, 0:SEQ], v_of(1, h), pt[:, SEQ:2 * SEQ], False, True, signal=True)
                temps.give(pt, [t3])
                if p0:
                    banks.give(o, split_tile(y_op, y_first + h // 2, o[:, 0:SEQ], None, t3))

            for h in range(n_heads):
                prob, free = temps.take()
                stats, sfree = small.take()
                done = score_tile(prob, free, stats, sfree, qt[:, h // 2, :], kt_[:, h // 2, :], DH * (h % 2),
                                  TILES if causal else [(0, P, SEQ), (P, P, SEQ)], causal, q_after(h // 2))
                normed = normalize(prob, done)
                small.give(stats, normed)
                waiting.append((h, prob, normed, stats))
                if h:
                    values()
            values()

        def differential_attention():
            waiting = deque()
            o_sum = cols[:, 0:0]
            sums = lru[:, 48:60]
            done_o = []

            def values():
                h, prob, done = waiting.popleft()
                pt, t_pt = transposed(prob, done, True)
                cs = slice(h * P, (h + 1) * P)
                o, ofree = banks.take()
                matmul(o[:, 0:P], pt[:, 0:P], vv[:, 0, cs], True, True, [ofree, t_pt, tokens2["v"]])
                matmul(o[:, P:SEQ], pt[:, P:SEQ], vv[:, 0, cs], True, False)
                t3 = matmul(o[:, P:SEQ], pt[:, SEQ:SEQ + P], vv[:, 1, cs], False, True, signal=True)
                temps.give(pt, [t3])
                dst = o_tok[:, :, cs]
                t4 = copy(dst, o[:, 0:SEQ].rearrange("p (n t) -> p n t", n=2), [t3, FENCE])
                banks.give(o, [t4])
                junk, jfree = temps.take()
                for i in range(2):
                    t5 = activate(junk[:, 0:P], o_tok[:, i, cs], ACT.Square, [t4, jfree, act.last()],
                                  accum=sums[:, 6 * i + h:6 * i + h + 1])
                done_o.append(t5)
                temps.give(junk, [t5])

            for h in range(DIFF_HEADS):
                parts = []
                for c in range(2):
                    prob, free = temps.take()
                    stats, sfree = small.take()
                    after = [tokens2["q", h], tokens2["k", h]]
                    parts.append((prob, stats, score_tile(prob, free, stats, sfree, q[:, h, :], kk[:, h, :],
                                                          DH * c, TILES, True, after)))
                (p_0, s_0, d_0), (p_1, s_1, d_1) = parts
                merged = []
                for j in range(2):
                    (tp0, ti0, inv0, at, nk), (tp1, ti1, inv1, _, _) = d_0[j], d_1[j]
                    t1 = ts(p_1[:, at:at + nk], p_1[:, at:at + nk], inv1, ALU.mult, [tp1, ti1, SMALL_READY],
                            NEG_LAMBDA, ALU.mult)
                    merged.append(stt(p_0[:, at:at + nk], p_0[:, at:at + nk], inv0, p_1[:, at:at + nk], ALU.mult,
                                      ALU.add, [tp0, ti0, t1]))
                small.give(s_0, merged)
                small.give(s_1, merged)
                temps.give(p_1, merged)
                waiting.append((h, p_0, merged))
                if h:
                    values()
            values()
            t1 = ts(sums, sums, 1.0 / P, ALU.mult, done_o, EPS, ALU.add)
            t2 = activate(sums, sums, ACT.Sqrt, [t1])
            t3 = recip(sums, sums, [t2])
            return sums, t3

        def differential_output(sums, t3):
            for h in range(0, DIFF_HEADS, 2):
                bank, bfree = banks.take()
                for hh in range(2):
                    cs = slice((h + hh) * P, (h + hh + 1) * P)
                    for i in range(2):
                        s = sums[:, 6 * i + h + hh:6 * i + h + hh + 1]
                        t4 = ts(o_tok[:, i, cs], o_tok[:, i, cs], s, ALU.mult, [t3])
                        t_pe = transpose(bank[:, hh * SEQ + i * P:hh * SEQ + (i + 1) * P], o_tok[:, i, cs], P,
                                         [t4, bfree], True)
                view = bank[:, 0:2 * SEQ].rearrange("p (n t) -> p n t", n=2)
                banks.give(bank, split_tile(y_op, h, view, SUB_GAIN, [t_pe, SMALL_READY], n=2))

        def mlp(layer, x_op, ready, R_row):
            hidden = {}
            sums = [banks.take() for _ in range(4)]

            def up(quarter):
                u_op = hidden[quarter] = Operand()

                def evacuate(m, psum, token):
                    m -= 8 * quarter
                    t_buf, free = temps.take()
                    v = t_buf[:, 0:2 * SEQ].rearrange("p (n t) -> p n t", n=2)
                    row = R_row.unsqueeze(1).to_broadcast([P, 2, SEQ])
                    t1 = stt(v, psum, 0.0, row, ALU.max, ALU.mult, [token, ready, free])
                    t2 = activate(v, v, ACT.Square, [t1])
                    temps.give(t_buf, split_tile(u_op, m, v, None, t2, n=2))
                    return [t1]

                for _ in range(4):
                    project("up", layer, x_op, SEQ, evacuate)

            def down(quarter, after_sum):
                u_op = hidden.pop(quarter)
                for c in range(4):
                    n, hi, lo = next_chunk("down", layer)
                    bank, free = sums[c]
                    for j in range(2):
                        for k in range(8):
                            token = three(bank[:, j * SEQ:(j + 1) * SEQ], hi[:, k, j * P:(j + 1) * P],
                                          lo[:, k, j * P:(j + 1) * P], u_op.hi(k, 0, SEQ), u_op.lo(k, 0, SEQ),
                                          quarter == 0 and k == 0 and j == 0, quarter == 3 and k == 7,
                                          [split_tokens[n], free if quarter == 0 else [], u_op.ready[k]],
                                          k == 7 and j == 1, shared=True)
                    chunk_done(n, token)
                    u_op.read = [token]
                    if quarter == 3:
                        view = bank[:, 0:2 * SEQ].rearrange("p (n t) -> p n t", n=2)
                        banks.give(bank, after_sum(2 * c, view, token))
                u_op.give()

            return up, down

        for layer in range(2):
            if layer == 0:
                ready = residual_statistics(RC, True)
                ready_rows = rope_rows(ready)
                for _ in range(3):
                    project("in2", 0, op, SEQ, evacuate_rope(q, "q", 0))
                for _ in range(3):
                    project("in2", 0, op, SEQ, evacuate_rope(kk, "k", 6))
                for i in range(3):
                    project_tokens("in2", 0, op, starts2, evacuate_v2(256 * i))
                project("in2", 0, op, SEQ, evacuate_qm)
                op.give()
            else:
                ready = residual_statistics(RC, True)
                ready_rows = rope_rows(ready)
                tokens2.clear()
                for _ in range(3):
                    project("in2", 1, op, SEQ, evacuate_rope(kk, "k", 0))
                for i in range(3):
                    project_tokens("in2", 1, op, starts2, evacuate_v2(256 * i))
                op.give()
                op = Operand()
                for k in range(DT):
                    split_tile(op, k, xs[:, k, :], vcol("b_norm_attn_2", k), x_tokens[k])
                for _ in range(3):
                    project("in2", 1, op, SEQ, evacuate_rope(q, "q", 12))
                project("in2", 1, op, SEQ, evacuate_qm)
                op.give()
            y_op = Operand()
            if layer == 0:
                sums, t3 = differential_attention()
            else:
                head_pairs(MOBA_HEADS, q, kk, lambda i, h: vv[:, i, h * DH:(h + 1) * DH], True,
                           lambda p: [tokens2["q", p], tokens2["k", p]], tokens2["v"], 0)
            head_pairs(MEM_HEADS, qm, MK, lambda i, h: MV[:, i, h * DH:(h + 1) * DH], False,
                       lambda p: [tokens2["qm"], mem_tokens["k"]], [mem_tokens["v", 0], mem_tokens["v", 1]], 6)
            if layer == 0:
                differential_output(sums, t3)
            FENCE = everything()
            op = Operand()
            gain = "a_norm_mlp_2" if layer == 0 else "b_norm_mlp_2"
            for _ in range(4):
                project("out2", layer, y_op, SEQ, residual_then_split(SEQ, META, op, gain))
            y_op.give()
            ready = residual_statistics(R2, False)
            up, down = mlp(layer, op, ready, R2)
            up(0)
            up(1)
            down(0, None)
            up(2)
            down(1, None)
            up(3)
            op.give()
            down(2, None)
            if layer == 0:
                mem_op, _ = load_memory(1, "b_mem_norm_2")
                op = Operand()
                down(3, residual_then_split(SEQ, META, op, "kv_norm_2"))
                memory_keys_values(1, mem_op, MEM_READY)
            else:
                down(3, add_to_residual(SEQ, META))
            FENCE = everything()

        ready = residual_statistics(RC, False)
        out_sem = semaphore("output_written")
        stores = []
        for k in range(DT):
            t1 = stt(xs[:, k, :], xs[:, k, :], vcol("final_norm_2", k), RC, ALU.mult, ALU.mult, [ready, x_tokens[k]])
            stores.append((k, t1))

        block = ctx.enter_context(nc.Block())

        @block.sync
        def _(sp):
            for waits, dst, src, sem in sp_items:
                for s, v in flat(waits):
                    sp.wait_ge(s, v)
                sp.dma_start(dst, src).then_inc(sem, 16)
            for k, (s, v) in stores:
                sp.wait_ge(s, v)
                sp.dma_start(out[k * P:(k + 1) * P, :], xs[:, k, :]).then_inc(out_sem, 16)
            sp.wait_ge(out_sem, 16 * len(stores))

        @block.scalar
        def _(e):
            act.emit(e)

        @block.vector
        def _(e):
            dve.emit(e)

        @block.tensor
        def _(e):
            pe.emit(e)


def rope_order():
    return [(p % 32) // 16 * 32 + 16 * (p // 32) + p % 16 for p in range(64)]


def rope_columns(first, n_heads, stride):
    return np.concatenate([first + h * stride + np.array(rope_order()) for h in range(n_heads)])


def shape_constants():
    c = np.zeros((P, N_CONST), np.float32)
    c[:, C_IDENT:C_IDENT + P] = np.eye(P, dtype=np.float32)
    c[:, C_ONES:C_ONES + P] = 1.0
    i = np.arange(P)
    c[:, C_MASK + 144:C_MASK + 272] = np.where(i[None, :] <= i[:, None], 0.0, NEG).astype(np.float32)
    inv = (np.float32(10000.0) ** (-np.arange(0, 64, 2, dtype=np.float32) / np.float32(64))).astype(np.float32)
    ang = (np.arange(T1, dtype=np.float32)[:, None] * inv[None, :]).astype(np.float64)
    for p in range(P):
        f = rope_order()[p % 64]
        c[p, C_COS:C_COS + T1] = np.cos(ang[:, f % 32])
        c[p, C_SIN:C_SIN + T1] = np.sin(ang[:, f % 32]) * (-1.0 if f < 32 else 1.0)
    return c


def kernel(**inputs):
    import concourse.bacc as bacc
    from concourse.bass_utils import run_bass_kernel_spmd

    v = {k: np.asarray(a) for k, a in inputs.items()}
    wi = v["a_w_in"][0]
    rope_k = wi[:, 640 + np.array(rope_order())]
    a_in = np.concatenate([wi[:, :640], rope_k, rope_k, wi[:, 704:]], axis=1)
    hd = NOPE + ROPE
    a_uq = v["a_w_uq"][0][:, np.concatenate(
        [h * hd + np.arange(NOPE) for h in range(HEADS)] + [rope_columns(NOPE, HEADS, hd)])]
    a_ukv = v["a_w_ukv"][0][:, np.concatenate(
        [h * 256 + np.arange(NOPE) for h in range(HEADS)] + [h * 256 + NOPE + np.arange(128) for h in range(HEADS)])]
    gates = [v[n][0].reshape(D, 256) for n in ("b_w_rg", "b_w_ig")]
    r12 = rope_columns(0, 12, DH)
    in_a = v["a_w_in_2"][0][:, np.concatenate([r12, 768 + r12, np.arange(1536, 2560)])]
    in_b = np.concatenate([v["w_kv_2"][:, r12], v["w_kv_2"][:, 768:],
                           v["b_w_in_2"][0][:, r12], v["b_w_in_2"][0][:, 768:]], axis=1)
    weights = {
        ("a_in", 0): a_in, ("a_uq", 0): a_uq, ("a_ukv", 0): a_ukv, ("a_out", 0): v["a_w_out"][0],
        ("b_in", 0): v["b_w_in"][0], ("b_out", 0): v["b_w_out"][0],
        ("mem", 0): v["a_w_mem_kv_2"][0], ("mem", 1): v["b_w_mem_kv_2"][0],
        ("in2", 0): in_a, ("in2", 1): in_b,
        ("out2", 0): v["a_w_out_2"][0], ("out2", 1): v["b_w_out_2"][0],
        ("up", 0): v["a_w_up_2"][0], ("up", 1): v["b_w_up_2"][0],
        ("down", 0): v["a_w_down_2"][0], ("down", 1): v["b_w_down_2"][0],
    }
    order = chunk_order()
    stream = np.zeros((len(order), P, CHUNK), np.float32)
    for n, (kind, layer, i) in enumerate(order):
        kt, w = SHAPES[kind]
        if kind == "b_gates":
            block = gates[i]
        elif kind == "down":
            block = weights[kind, layer][(i // 4) * 1024:(i // 4 + 1) * 1024, (i % 4) * w:(i % 4 + 1) * w]
        else:
            block = weights[kind, layer][:, i * w:(i + 1) * w]
        stream[n, :, :kt * w] = block.reshape(kt, P, w).transpose(1, 0, 2).reshape(P, kt * w)
    vecs = np.concatenate([v[n].reshape(k, P).T for n, k in VECTORS], axis=1)
    consts = shape_constants()
    consts[:, C_LAM:] = v["a_lambda_2"].reshape(1, -1)
    arrays = {
        "stream": stream,
        "xT": np.ascontiguousarray(np.concatenate([v["meta_tokens"], v["x"][0]], axis=0).T),
        "memT": np.ascontiguousarray(v["mem_2"][0].T),
        "vecs": np.ascontiguousarray(vecs),
        "consts": consts,
    }
    nc = bacc.Bacc("TRN2", target_bir_lowering=False, num_devices=1)
    args = [nc.dram_tensor(f"{n}_dram", a.shape, F32, kind="ExternalInput").ap() for n, a in arrays.items()]
    out = nc.dram_tensor("out_dram", (D, SEQ), F32, kind="ExternalOutput").ap()
    program(nc, *args, out)
    r = run_bass_kernel_spmd(nc, [{f"{n}_dram": a for n, a in arrays.items()}], core_ids=[0])
    return np.ascontiguousarray(r.results[0]["out_dram"].T).reshape(1, SEQ, D)
```

```python
from collections import deque
from contextlib import ExitStack

import numpy as np

import concourse.bass as bass
from concourse import mybir

F32 = mybir.dt.float32
F32R = mybir.dt.float32r
ACT = mybir.ActivationFunctionType
ALU = mybir.AluOpType
AX_X = mybir.AxisListType.X

P = 128
D = 1024
DT = D // P
SEQ = 256
META = 16
T1 = META + SEQ
EPS = 1e-6
NEG = -1e30
CHUNK = 2048
PAD = 3

HEADS, NOPE, ROPE, Q_LORA, KV_LORA = 8, 128, 64, 384, 256
DIFF_HEADS, MOBA_HEADS, MEM_HEADS, DH = 6, 12, 4, 64
D_FF = 4096
LAMBDA_INIT = 0.8 - 0.6 * 1.0
LRU_C = 8.0

SHAPES = {
    "a_in": (8, 256), "a_uq": (3, 512), "a_ukv": (2, 1024), "a_out": (8, 256),
    "b_in": (8, 256), "b_gates": (8, 256), "b_out": (8, 256),
    "mem": (8, 256), "in2": (8, 256), "out2": (8, 256), "up": (8, 256), "down": (8, 256),
}
HALF = CHUNK // 2


def halves_of(kind, index):
    kt, w = SHAPES[kind]
    by_inputs = ((kind, index) == ("a_in", 0) or kind == "b_gates" or (kind == "mem" and index == 1)
                 or (kind == "in2" and index in (6, 7, 8)))
    return (True, kt // 2, w) if by_inputs else (False, kt, w // 2)


UP_DOWN = [("up", 0), ("up", 1), ("down", 0), ("up", 2), ("down", 1), ("up", 3), ("down", 2), ("down", 3)]


def chunk_order():
    order = [("a_in", 0, i) for i in range(5)]
    order += [("a_uq", 0, 0), ("a_uq", 0, 2), ("a_ukv", 0, 0), ("a_ukv", 0, 1)]
    order += [("a_in", 0, 5), ("a_in", 0, 6), ("a_uq", 0, 1)]
    order += [("a_out", 0, i) for i in range(4)]
    order += [("b_in", 0, i) for i in range(4)] + [("b_gates", 0, i) for i in range(2)]
    order += [("b_in", 0, i) for i in range(4, 8)] + [("mem", 1, i) for i in range(2)]
    order += [("b_out", 0, i) for i in range(4)]
    order += [("mem", 0, i) for i in range(2)]
    for layer in range(2):
        order += [("in2", layer, i) for i in (9, 0, 3, 6, 1, 4, 7, 2, 5, 8)]
        order += [("out2", layer, i) for i in range(4)]
        for kind, quarter in UP_DOWN:
            order += [(kind, layer, 4 * quarter + i) for i in range(4)]
    return order


VECTORS = [("a_norm_g", 8), ("a_q_norm_g", 3), ("a_kv_norm_g", 2), ("b_norm_g", 8),
           ("b_conv_w", 32), ("b_conv_b", 8), ("b_b_rg", 8), ("b_b_ig", 8), ("b_lam", 8),
           ("final_norm_g", 8), ("a_norm_attn_2", 8), ("a_subln_2", 1), ("a_mem_norm_2", 8),
           ("a_norm_mlp_2", 8), ("kv_norm_2", 8), ("b_norm_attn_2", 8), ("b_mem_norm_2", 8),
           ("b_norm_mlp_2", 8), ("final_norm_2", 8)]
VEC_AT, _n = {}, 0
for _name, _k in VECTORS:
    VEC_AT[_name] = _n
    _n += _k
N_VEC = _n
C_IDENT, C_ONES, C_MASK, C_COS, C_SIN, C_LAM = 0, 128, 256, 528, 800, 1072
N_CONST = 1072 + 4 * DH


class Instruction:

    def __init__(self, queue, number, issue, after, cost, strand, signal, table, sem, value):
        self.queue, self.number, self.issue, self.after = queue, number, issue, after
        self.cost, self.strand, self.counted, self.table = cost, strand, signal, table
        self.sem, self.value = sem, value
        self.late = self.end = None


class Fence:

    def __init__(self, number):
        self.number = number


def flat(tokens):
    if isinstance(tokens, (Instruction, Fence)):
        yield tokens
    elif tokens is not None:
        for t in tokens:
            yield from flat(t)


class Queue:

    def __init__(self, plan, name, sem):
        self.plan, self.name, self.sem = plan, name, sem
        self.strand, self.order = "main", []
        plan.queues.append(self)

    def do(self, issue, after=(), signal=True, cost=0.1, strand=None, table=None, sem=None, value=None):
        i = Instruction(self, len(self.plan.all), issue, list(flat(after)), cost, strand or self.strand,
                        signal, table, sem, value)
        self.plan.all.append(i)
        return i

    def emit(self, engine):
        waited = {}
        for i in self.order:
            need = {}
            for sem, value in self.plan.values(i.after):
                if value > max(waited.get(sem.name, 0), need.get(sem.name, (None, 0))[1]):
                    need[sem.name] = (sem, value)
            for name, (sem, value) in need.items():
                waited[name] = value
                engine.wait_ge(sem, value)
            instruction = i.issue(engine)
            if i.counted:
                instruction.then_inc(i.sem, 16 if i.queue.name == "sp" or i.table == "dma" else 1)


class Plan:

    LATENCY, TABLE, WINDOW, DMA_START, DMA_TIME = 0.13, 1.3, 60, 1.9, 3.0

    def __init__(self):
        self.queues, self.all = [], []

    def fence(self):
        return Fence(len(self.all))

    def values(self, tokens):
        for t in tokens:
            if isinstance(t, Instruction):
                yield t.sem, t.value
            else:
                for q in self.queues:
                    last = max((i.value for i in q.order if i.number < t.number and i.counted and i.sem is q.sem),
                               default=0)
                    if last:
                        yield q.sem, last

    def latest_starts(self):
        clock = 0.0
        for i in self.all:
            if i.queue.name == "pe":
                i.late = clock
                clock += i.cost
        for i in self.all:
            if i.late is None:
                i.late = 1e9
        for i in reversed(self.all):
            if i.late > 1e8:
                i.late = clock
            for t in i.after:
                if isinstance(t, Instruction):
                    t.late = min(t.late, i.late - t.cost - self.LATENCY)

    def arrange(self):
        self.latest_starts()
        waiting = {q: [i for i in self.all if i.queue is q] for q in self.queues}
        free = {q: 0.0 for q in self.queues}
        table, dma_free = None, 0.0
        pe = next(q for q in self.queues if q.name == "pe")
        strands = {}
        for i in waiting[pe]:
            strands.setdefault(i.strand, deque()).append(i)

        def heads():
            return [s[0] for s in strands.values() if s]

        def unit(i):
            members = []
            for j in strands[i.strand]:
                members.append(j)
                if j.counted:
                    return members

        done, lowest, prefix = 0, 0, [0.0]
        while done < len(self.all):
            while lowest < len(self.all) and self.all[lowest].end is not None:
                prefix.append(max(prefix[-1], self.all[lowest].end))
                lowest += 1

            def ready(i):
                at = 0.0
                for t in i.after:
                    if isinstance(t, Fence):
                        if t.number > lowest:
                            return None
                        at = max(at, prefix[t.number])
                    elif t.end is None:
                        return None
                    else:
                        at = max(at, t.end)
                return at + self.LATENCY

            best = None
            for q in self.queues:
                for n, i in enumerate(heads() if q is pe else waiting[q][:self.WINDOW]):
                    if q.name in ("sp", "pool") and n:
                        break
                    at = ready(i)
                    if at is None:
                        continue
                    start = max(at, free[q])
                    rank = i.late
                    if q is pe:
                        if any(ready(j) is None for j in unit(i)):
                            continue
                        rank = {"statistics": 0, "attention": 1}.get(i.strand, 2)
                    if i.table not in (None, "dma", table):
                        rank += self.TABLE
                    key = (start, rank, i.number)
                    if best is None or key < best[0]:
                        best = (key, q, n, i, start)
            _, q, n, i, start = best
            if q is pe:
                for j in unit(i):
                    free[pe] = j.end = max(free[pe], ready(j)) + j.cost
                    pe.order.append(j)
                    strands[i.strand].popleft()
                    done += 1
                continue
            waiting[q].pop(n)
            q.order.append(i)
            if i.table not in (None, "dma", table):
                table = i.table
                start += self.TABLE
            free[q] = i.end = start + i.cost
            if q.name == "sp" or i.table == "dma":
                dma_free = i.end = max(start + self.DMA_START, dma_free) + self.DMA_TIME * i.cost / 0.1
            done += 1
        for q in self.queues:
            count = 0
            for i in q.order:
                if i.sem is None:
                    i.sem = q.sem
                    count += i.counted
                    i.value = count


def columns(ap):
    return int(np.prod(ap.shape[1:]))


class Buffers:

    def __init__(self, buffers):
        self.free = deque((b, []) for b in buffers)

    def take(self):
        return self.free.popleft()

    def give(self, buffer, tokens):
        self.free.append((buffer, tokens))


def program(nc, stream, xT, memT, vecs, consts, out):
    ctx = ExitStack()
    with ctx:
        def sb(name, shape, dt=F32):
            return ctx.enter_context(nc.sbuf_tensor(name, shape, dt))

        def semaphore(name):
            return ctx.enter_context(nc.semaphore(name))

        plan = Plan()
        pe, act, dve, pool, sp = (Queue(plan, n, semaphore(f"{n}_done")) for n in ("pe", "act", "dve", "pool", "sp"))

        N_RAW, N_SPLIT, N_OPERAND, N_TEMP = 3, 6, 3, 7
        raw = [sb(f"weights_raw{i}", [P, CHUNK]) for i in range(N_RAW)]
        w_hi = [sb(f"weights_hi{i}", [P, HALF], F32R) for i in range(N_SPLIT)]
        w_lo = [sb(f"weights_lo{i}", [P, HALF], F32R) for i in range(N_SPLIT)]
        operands = Buffers([(sb(f"operand_hi{i}", [P, DT, T1], F32R), sb(f"operand_lo{i}", [P, DT, T1], F32R))
                            for i in range(N_OPERAND)])
        temps = Buffers([sb(f"temp{i}", [P, 656]) for i in range(N_TEMP)])
        small = Buffers([sb(f"softmax_stats{i}", [P, 16]) for i in range(6)])
        x = sb("residual", [P, DT, T1])
        ARENA = 10960
        arena = sb("arena", [P, ARENA])
        rows = sb("rows", [P, 5, T1])
        cols = sb("cols", [P, 16])
        vec = sb("vectors", [P, N_VEC])
        const = sb("constants", [P, C_LAM])
        lru = sb("lru_scales", [P, 64])
        mem_kv = sb("memory_keys_values", [P, 1024])
        banks = Buffers([ctx.enter_context(nc.psum_tensor(f"bank{i}", [P, 512], F32)) for i in range(8)])

        ident = const[:, C_IDENT:C_IDENT + P]
        ones = const[:, C_ONES:C_ONES + P]
        mask = const[:, C_MASK:C_MASK + T1]
        cos = const[:, C_COS:C_COS + T1]
        sin = const[:, C_SIN:C_SIN + T1]

        def vcol(name, i=0):
            return vec[:, VEC_AT[name] + i:VEC_AT[name] + i + 1]

        def region(start, *shape):
            n = int(np.prod(shape))
            assert start + n <= ARENA
            ap = arena[:, start:start + n]
            if len(shape) == 2:
                ap = ap.rearrange("p (a b) -> p a b", a=shape[0])
            return ap

        def matmul(out, lhsT, rhs, start, stop, after=(), signal=False, shared=False):
            cost = columns(rhs) * (4.2e-4 if rhs.dtype == F32R else 1.7e-3)
            return pe.do(lambda e: e.matmul(out, lhsT, rhs, start=start, stop=stop, skip_group_check=shared),
                         after, signal, cost)

        def transpose(out, in_, n, after=(), signal=False):
            return pe.do(lambda e: e.transpose(out, in_, ident[0:n, 0:n]), after, signal, 1.7e-3 * n)

        SETS = {ACT.Exp: "exp", ACT.Silu: "silu", ACT.Sigmoid: "sigmoid", ACT.Tanh: "exp", ACT.Sqrt: "sqrt"}

        def activate(out, in_, func, after, scale=1.0, bias=0.0, accum=None):
            cost = 0.08 + 8.5e-4 * columns(out) + (0.1 if accum is not None or isinstance(scale, bass.AP) else 0)
            if accum is None:
                return act.do(lambda e: e.activation(out, in_, func, bias=bias, scale=scale), after, cost=cost,
                              table=SETS.get(func))
            return act.do(lambda e: e.activation(out, in_, func, bias=bias, scale=scale, accum_out=accum), after,
                          cost=cost, table=SETS.get(func))

        def on_dve(out, issue, after, rate=1.0):
            return dve.do(issue, after, cost=0.07 + 1.05e-3 * rate * columns(out))

        def tt(out, a, b, op, after):
            return on_dve(out, lambda e: e.tensor_tensor(out, a, b, op), after)

        def ts(out, a, s1, op0, after, s2=None, op1=None):
            if op1 is None:
                return on_dve(out, lambda e: e.tensor_scalar(out, a, s1, None, op0), after)
            return on_dve(out, lambda e: e.tensor_scalar(out, a, s1, s2, op0, op1), after)

        def stt(out, a, s, b, op0, op1, after):
            return on_dve(out, lambda e: e.scalar_tensor_tensor(out, a, s, b, op0, op1), after, 1.2)

        def reduce(out, in_, op, after, negate=False):
            return on_dve(in_, lambda e: e.tensor_reduce(out, in_, AX_X, op, negate=negate), after)

        def recip(out, in_, after):
            return on_dve(out, lambda e: e.reciprocal(out, in_), after, 5.5)

        def copy(out, in_, after):
            return on_dve(out, lambda e: e.tensor_copy(out, in_), after)

        def everything():
            return plan.fence()

        order = chunk_order()
        PIECES = 4
        raw_sems = [semaphore(f"weights_landed{i}") for i in range(N_RAW)]
        piece_sems = [semaphore(f"first_weights_landed{i}") for i in range(PIECES)]
        split_tokens, arrived = {}, {}
        raw_free, split_free = [[] for _ in range(N_RAW)], [[] for _ in range(N_SPLIT)]
        state = {"loaded": 0, "split": 0, "used": 0}

        def load_next():
            n = state["loaded"]
            if n == len(order):
                return
            state["loaded"] += 1
            kt, w = SHAPES[order[n][0]]
            size = kt * w
            pieces = [(0, size, raw_sems[n % N_RAW])]
            if n == 0:
                step = size // PIECES
                pieces = [(i * step, (i + 1) * step, piece_sems[i]) for i in range(PIECES)]
            for a, b, sem in pieces:
                r = n % N_RAW
                dst, src = raw[r][:, a:b], stream[n, :, a:b]
                value = 16 if n == 0 else 16 * (n // N_RAW + (r != 0))
                arrived[n, a] = sp.do(lambda e, dst=dst, src=src: e.dma_start(dst, src), raw_free[r],
                                     cost=0.1 * (b - a) / CHUNK, sem=sem, value=value)

        def split_columns(n, a, b, in_raw):
            kind, _, index = order[n]
            by_inputs, kh, wh = halves_of(kind, index)
            half, size = a // (kh * wh), kh * wh
            s = (2 * n + half) % N_SPLIT
            src = raw[n % N_RAW][:, a:b]
            hi, lo = w_hi[s][:, a - half * size:b - half * size], w_lo[s][:, a - half * size:b - half * size]
            t_hi = activate(hi, src, ACT.Copy, [in_raw, split_free[s]])
            tokens = [t_hi, tt(lo, src, hi.bitcast(F32), ALU.subtract, [in_raw, t_hi, split_free[s]])]
            for k in range((a - half * size) // wh, (b - half * size) // wh):
                split_tokens[n, half, k] = tokens
            return tokens

        def split_first(i):
            size = int(np.prod(SHAPES[order[0][0]])) // PIECES
            tokens = split_columns(0, i * size, (i + 1) * size, arrived[0, i * size])
            raw_free[0] = raw_free[0] + tokens
            if i == PIECES - 1:
                state["split"] = 2
                load_next()

        def split_next():
            n, half = divmod(state["split"], 2)
            state["split"] += 1
            size = int(np.prod(SHAPES[order[n][0]])) // 2
            r = n % N_RAW
            tokens = split_columns(n, half * size, (half + 1) * size, arrived[n, 0])
            raw_free[r] = tokens + (raw_free[r] if half else [])
            if half:
                load_next()

        class Chunk:

            def __init__(self, kind, layer):
                self.n = n = state["used"]
                assert order[n][0] == kind and order[n][1] == layer, (order[n], kind, layer)
                state["used"] += 1
                self.index = order[n][2]
                self.by_inputs, self.kh, self.wh = halves_of(kind, self.index)
                self.begun = -1

            def begin(self, half):
                if half == self.begun:
                    return
                self.begun = half
                while state["split"] < min(2 * self.n + half + N_SPLIT, 2 * len(order)):
                    split_next()

            def part(self, k, c0, c1):
                half, k, c = (k // self.kh, k % self.kh, c0) if self.by_inputs else (c0 // self.wh, k, c0 % self.wh)
                self.begin(half)
                s, a = (2 * self.n + half) % N_SPLIT, k * self.wh + c
                return (w_hi[s][:, a:a + c1 - c0], w_lo[s][:, a:a + c1 - c0], split_tokens[self.n, half, k])

            def done(self, half, token):
                split_free[(2 * self.n + half) % N_SPLIT] = [token]

        waiting_steps = deque()

        def background(stage, rate=1):
            waiting_steps.append((stage, rate))

        def step():
            if waiting_steps:
                stage, rate = waiting_steps[0]
                pe.strand = "attention"
                for _ in range(rate):
                    if next(stage, "end") == "end":
                        waiting_steps.popleft()
                        break
                pe.strand = "main"

        def finish_background():
            while waiting_steps:
                step()

        class Operand:

            def __init__(self):
                (self.hi_t, self.lo_t), self.free = operands.take()
                self.ready, self.read = {}, []
                self.base = 0

            def hi(self, k, t0, t1):
                return self.hi_t[:, k, t0:t1]

            def lo(self, k, t0, t1):
                return self.lo_t[:, k, t0:t1]

            def give(self):
                operands.give((self.hi_t, self.lo_t), self.read)

        def split_tile(op, k, src, gain, after, n=1):
            T = src.shape[-1]
            hi, lo = op.hi_t[:, k:k + n, 0:T], op.lo_t[:, k:k + n, 0:T]
            if len(src.shape) == 2:
                hi, lo = op.hi_t[:, k, 0:T], op.lo_t[:, k, 0:T]
            if gain is None:
                t1 = activate(hi, src, ACT.Copy, [after, op.free])
                t2 = tt(lo, src, hi.bitcast(F32), ALU.subtract, [after, op.free, t1])
            else:
                t1 = activate(hi, src, ACT.Copy, [after, op.free], scale=gain)
                t2 = stt(lo, src, gain, hi.bitcast(F32), ALU.mult, ALU.subtract, [after, op.free, t1])
            for i in range(n):
                op.ready[k + i] = [t1, t2]
            return [t1, t2]

        def three(out, w_h, w_l, x_h, x_l, first, last, after, signal, shared=False):
            matmul(out, w_h, x_h, first, False, after, shared=shared)
            matmul(out, w_h, x_l, False, False, shared=shared)
            return matmul(out, w_l, x_h, False, last, signal=signal, shared=shared)

        held = []

        def release(before=None):
            if before is not None:
                pe.strand = "statistics"
                before()
                pe.strand = "main"
            while held:
                evacuate, m, view, token, bank = held.pop(0)
                banks.give(bank, evacuate(m, view, token))

        def project(kind, layer, op, T, evacuate, t0=0, base=0, hold=False):
            chunk = Chunk(kind, layer)
            kt, w = SHAPES[kind]
            per = 2 if 2 * T <= 512 else 1
            groups = []

            def product(bank, free, m, j, ks):
                for k in ks:
                    w_h, w_l, ready = chunk.part(k, m * P, (m + 1) * P)
                    last = k == kt - 1
                    token = three(bank[:, j * T:(j + 1) * T], w_h, w_l,
                                  op.hi(base + k, t0, t0 + T), op.lo(base + k, t0, t0 + T),
                                  k == 0, last, [ready, free, op.ready[base + k]],
                                  k == ks[-1], shared=chunk.by_inputs)
                return token

            def finished(m0, bank, token):
                view = bank[:, 0:per * T].rearrange("p (n t) -> p n t", n=per)
                held.append((evacuate, chunk.index * (w // P) + m0, view, token, bank))
                if not hold:
                    release()

            if chunk.by_inputs:
                taken = [banks.take() for _ in range(w // P)]
                for half in range(2):
                    for m, (bank, free) in enumerate(taken):
                        token = product(bank, free, m, 0, range(half * chunk.kh, (half + 1) * chunk.kh))
                        if half:
                            finished(m, bank, token)
                            step()
                    chunk.done(half, token)
            else:
                for m0 in range(0, w // P, per):
                    bank, free = banks.take()
                    for j in range(per):
                        m = m0 + j
                        token = product(bank, free, m, j, range(kt))
                        if (m + 1) * P % chunk.wh == 0:
                            chunk.done(m * P // chunk.wh, token)
                        if j == per - 1:
                            finished(m0, bank, token)
                        step()
            op.read = [token]

        def project_tokens(kind, layer, op, starts, evacuate, base=0):
            chunk = Chunk(kind, layer)
            kt, w = SHAPES[kind]

            def product(o, t0, c0, c1, ks, free):
                for k in ks:
                    w_h, w_l, ready = chunk.part(k, c0, c1)
                    x_h, x_l = op.hi(base + k, t0, t0 + P), op.lo(base + k, t0, t0 + P)
                    matmul(o, x_h, w_h, k == 0, False, [ready, free, op.ready[base + k]])
                    matmul(o, x_h, w_l, False, False)
                    token = matmul(o, x_l, w_h, False, k == kt - 1, signal=k == ks[-1])
                return token

            if chunk.by_inputs:
                taken = [banks.take() for _ in starts]
                for half in range(2):
                    for i, (bank, free) in enumerate(taken):
                        token = product(bank[:, 0:w], starts[i], 0, w, range(half * chunk.kh, (half + 1) * chunk.kh),
                                        free)
                        if half:
                            banks.give(bank, evacuate(i, 0, bank[:, 0:w], token))
                        step()
                    chunk.done(half, token)
            else:
                for c0 in range(0, w, chunk.wh):
                    for i, t0 in enumerate(starts):
                        bank, free = banks.take()
                        token = product(bank[:, 0:chunk.wh], t0, c0, c0 + chunk.wh, range(kt), free)
                        banks.give(bank, evacuate(i, c0, bank[:, 0:chunk.wh], token))
                        step()
                    chunk.done(c0 // chunk.wh, token)
            op.read = [token]

        class SquareSum:

            def __init__(self):
                (self.acc, self.free), self.token = temps.take(), None
                self.read = []

            def add(self, src, after):
                n, T = (1, src.shape[-1]) if len(src.shape) == 2 else (src.shape[1], src.shape[2])
                acc = self.acc[:, 0:n * T]
                if n > 1:
                    acc = acc.rearrange("p (n t) -> p n t", n=n)
                if self.token is None:
                    self.n, self.T = n, T
                    self.token = activate(acc, src, ACT.Square, [after, self.free])
                    return self.token
                sq, free = temps.take()
                v = sq[:, 0:n * T]
                if n > 1:
                    v = v.rearrange("p (n t) -> p n t", n=n)
                t1 = activate(v, src, ACT.Square, [after, free])
                self.token = tt(acc, acc, v, ALU.add, [t1, self.token])
                temps.give(sq, [self.token])
                return t1

            def total(self):
                T = self.T
                if self.n == 2:
                    self.token = tt(self.acc[:, 0:T], self.acc[:, 0:T], self.acc[:, T:2 * T], ALU.add,
                                    [self.token])
                    self.n = 1
                return self.acc, self.token

            def give(self, read):
                temps.give(self.acc, read)

        def rstd_row(temp, token, n_features, T, row, after):
            bank, free = banks.take()
            t1 = matmul(bank[:, 0:T], ones, temp[:, 0:T], True, True, [token, free], True)
            t2 = ts(row, bank[:, 0:T], 1.0 / n_features, ALU.mult, [t1, after], EPS, ALU.add)
            banks.give(bank, [t2])
            t3 = activate(row, row, ACT.Sqrt, [t2])
            return t1, recip(row, row, [t3])

        def rstd_col(temp, token, n_features, starts, col, after):
            bank, free = banks.take()
            for i, t0 in enumerate(starts):
                t1 = matmul(bank[:, i:i + 1], temp[:, t0:t0 + P], ones[:, 0:1], True, True, [token, free],
                            i == len(starts) - 1)
            t2 = ts(col, bank[:, 0:len(starts)], 1.0 / n_features, ALU.mult, [t1, after], EPS, ALU.add)
            banks.give(bank, [t2])
            t3 = activate(col, col, ACT.Sqrt, [t2])
            return t1, recip(col, col, [t3])

        SWAP = [(r + 16) % 32 for r in range(32)]

        def rope(out, psum, n, T, cos_row, sin_row, token, after):
            a, free_a = temps.take()
            b, free_b = temps.take()
            ap = a[:, 0:n * T].rearrange("p (n t) -> p n t", n=n)
            bp = b[:, 0:n * T].rearrange("p (n t) -> p n t", n=n)
            cb = cos_row.unsqueeze(1).to_broadcast([P, n, T])
            sb_ = sin_row.unsqueeze(1).to_broadcast([P, n, T])
            t1 = activate(ap, psum, ACT.Copy, [token, free_a])
            t2 = on_dve(b[:, 0:n * T], lambda e: e.stream_shuffle(b[:, 0:n * T], a[:, 0:n * T], SWAP), [t1, free_b])
            t3 = tt(bp, bp, sb_, ALU.mult, [t2, after])
            t4 = tt(ap, ap, cb, ALU.mult, [t2, after])
            t5 = tt(out, ap, bp, ALU.add, [t3, t4, after])
            temps.give(a, [t5])
            temps.give(b, [t5])
            return [t1], [t5]

        def softmax(prob, psum, scale, mask_ap, token, free, stats, j):
            qn = psum.shape[0]
            top, neg = stats[0:qn, 4 * j:4 * j + 1], stats[0:qn, 4 * j + 1:4 * j + 2]
            total, inv = stats[0:qn, 4 * j + 2:4 * j + 3], stats[0:qn, 4 * j + 3:4 * j + 4]
            if mask_ap is not None:
                t1 = on_dve(prob, lambda e: e.tensor_tensor_reduce(prob, psum, mask_ap, scale, 3.0 * NEG, ALU.add,
                                                                   ALU.max, top), [token, free])
                t2 = ts(neg, top, -1.0, ALU.mult, [t1])
                t3 = activate(prob, prob, ACT.Exp, [t2], bias=neg, accum=total)
                freed = [t1]
            else:
                t1 = reduce(top, psum, ALU.max, [token, free])
                t2 = ts(neg, top, -scale, ALU.mult, [t1])
                t3 = activate(prob, psum, ACT.Exp, [t2, free], scale=scale, bias=neg, accum=total)
                freed = [t1, t3]
            t4 = recip(inv, total, [t3])
            return freed, [t3], [t4], inv

        x_sems = [semaphore(f"x_landed{i}") for i in range(4)]
        load_sem = {n: semaphore(f"{n}_landed") for n in ("vectors", "constants", "lambda")}
        x_in = xT.rearrange("(k p) t -> p k t", p=P)

        def load(dst, src, sem, after=()):
            return act.do(lambda e: e.dma_start(dst, src), after, cost=0.07, table="dma", sem=sem, value=16)

        VEC_IN = load(vec[:], vecs, load_sem["vectors"])
        X_IN = [load(x[:, 2 * i:2 * i + 2, :], x_in[:, 2 * i:2 * i + 2, :], x_sems[i]) for i in range(4)]
        for _ in range(N_RAW):
            load_next()
        CONST_IN = load(const[:], consts[:, 0:C_LAM], load_sem["constants"])
        lam_in = region(10700, 256)
        LAM_IN = load(lam_in, consts[:, C_LAM:N_CONST], load_sem["lambda"])

        R, RQ, CR, SR, RKV = (rows[:, i, :] for i in range(5))
        qn, kn, qr, kr = region(0, 8, T1), region(2176, 8, T1), region(4352, 4, T1), region(5440, 1, T1)
        V16, V = region(5712, 1024), region(6736, 2, 1024)
        silu_gate = region(8784, 8, T1)
        lat = region(6000, 5, T1)

        op = Operand()
        sum_x = SquareSum()
        for k in range(DT):
            landed = [X_IN[k // 2], VEC_IN]
            split_tile(op, k, x[:, k, :], vcol("a_norm_g", k), landed)
            if k % 2:
                split_first(k // 2)
        for k in range(DT):
            sum_x.add(x[:, k, :], X_IN[k // 2])
        lat_tokens, kr_tokens, gate_tokens = [], [], []

        def statistics_a():
            nonlocal R_READY, ROPE_READY
            temp, t = sum_x.total()
            t_pe, R_READY = rstd_row(temp, [t, CONST_IN], D, T1, R, [])
            sum_x.give([t_pe])
            t1 = tt(CR, cos, R, ALU.mult, [R_READY])
            ROPE_READY = [t1, tt(SR, sin, R, ALU.mult, [R_READY])]

        R_READY = ROPE_READY = RQ_READY = RKV_READY = RKV_COL_READY = SMALL_READY = LRU_READY = None
        sum_q, sum_kv = SquareSum(), SquareSum()
        latent = Operand()

        def evacuate_a_in(m, psum, token):
            if m < 5:
                t1 = tt(lat[:, m, :], psum[:, 0, :], R, ALU.mult, [token, R_READY])
                lat_tokens.append(t1)
                split_tile(latent, m, lat[:, m, :],
                           vcol("a_q_norm_g", m) if m < 3 else vcol("a_kv_norm_g", m - 3), t1)
                (sum_q if m < 3 else sum_kv).add(lat[:, m, :], t1)
                return [t1]
            if m == 5:
                freed, done = rope(kr, psum, 1, T1, CR, SR, token, ROPE_READY)
                kr_tokens.extend(done)
                return freed
            g = silu_gate[:, m - 6, :]
            t1 = tt(g, psum[:, 0, :], R, ALU.mult, [token, R_READY, SMALL_READY])
            gate_tokens.append(activate(g, g, ACT.Silu, [t1]))
            return [t1]

        def small_values():
            nonlocal SMALL_READY, LRU_READY
            lam_ap = vec[:, VEC_AT["b_lam"]:VEC_AT["b_lam"] + 8]
            t = activate(L[0], lam_ap, ACT.Abs, [VEC_IN])
            t = activate(L[1], L[0], ACT.Exp, [t], scale=-1.0)
            t = ts(L[0], L[1], 2.0, ALU.add, [t])
            t = recip(L[2], L[0], [t])
            t = tt(L[0], L[1], L[2], ALU.mult, [t])
            t = tt(L[1], L[0], L[0], ALU.mult, [t])
            terms = [1.0 / (2 * i + 1) for i in range(10)]
            t = ts(L[2], L[1], terms[9], ALU.mult, [t], terms[8], ALU.add)
            for i in range(7, -1, -1):
                t = tt(L[3], L[2], L[1], ALU.mult, [t])
                t = ts(L[2], L[3], terms[i], ALU.add, [t])
            t = stt(L[3], L[0], 2.0, L[2], ALU.mult, ALU.mult, [t])
            t = ts(L[2], lam_ap, -1.0, ALU.mult, [t], 0.0, ALU.max)
            t = tt(L[3], L[3], L[2], ALU.add, [t])
            t = ts(POS_SCALE, L[3], LRU_C, ALU.mult, [t])
            LRU_READY = ts(NEG_SCALE, L[3], -LRU_C, ALU.mult, [t])
            lam4 = lam_in.rearrange("p (a b d) -> p a b d", a=2, b=2)
            lam_prod = lam4[:, :, 0, :]
            t = tt(lam_prod, lam_prod, lam4[:, :, 1, :], ALU.mult, [LAM_IN])
            t = reduce(cols[:, 8:10], lam_prod, ALU.add, [t])
            t = activate(cols[:, 8:10], cols[:, 8:10], ACT.Exp, [t])
            t = tt(cols[:, 10:11], cols[:, 9:10], cols[:, 8:9], ALU.subtract, [t])
            t = ts(cols[:, 11:12], cols[:, 10:11], -LAMBDA_INIT, ALU.add, [t])
            SMALL_READY = [t, ts(SUB_GAIN, vcol("a_subln_2"), 1.0 - LAMBDA_INIT, ALU.mult, [VEC_IN])]

        L = [lru[:, 8 * i:8 * i + 8] for i in range(6)]
        POS_SCALE, NEG_SCALE = L[4], L[5]
        NEG_LAMBDA, SUB_GAIN = cols[:, 11:12], cols[:, 12:13]

        project("a_in", 0, op, T1, evacuate_a_in, hold=True)
        release(statistics_a)
        for _ in range(2):
            project("a_in", 0, op, T1, evacuate_a_in)
        LAT_DONE = everything()
        kv_starts = (0, META, META + P)

        def statistics_latents():
            nonlocal RQ_READY, RKV_READY, RKV_COL_READY, ROPE_READY
            temp, t = sum_q.total()
            t_pe, RQ_READY = rstd_row(temp, t, Q_LORA, T1, RQ, [])
            sum_q.give([t_pe])
            temp, t = sum_kv.total()
            t_pe, RKV_READY = rstd_row(temp, t, KV_LORA, T1, RKV, [])
            t_pe2, RKV_COL_READY = rstd_col(temp, t, KV_LORA, kv_starts, cols[:, 0:3], [])
            sum_kv.give([t_pe, t_pe2])
            t1 = tt(CR, cos, RQ, ALU.mult, [RQ_READY, kr_tokens])
            ROPE_READY = [t1, tt(SR, sin, RQ, ALU.mult, [RQ_READY, kr_tokens])]

        small_values()
        project("a_in", 0, op, T1, evacuate_a_in, hold=True)
        release(statistics_latents)
        project("a_in", 0, op, T1, evacuate_a_in)
        q_tokens, k_tokens, v_tokens = {}, {}, []

        def evacuate_q(m, psum, token):
            if m < 8:
                q_tokens[m] = [tt(qn[:, m, :], psum[:, 0, :], RQ, ALU.mult, [token, RQ_READY])]
                return q_tokens[m]
            freed, q_tokens[m] = rope(qr[:, m - 8:m - 7, :], psum, 1, T1, CR, SR, token, ROPE_READY)
            return freed

        def evacuate_k(m, psum, token):
            k_tokens[m] = tt(kn[:, m, :], psum[:, 0, :], RKV, ALU.mult, [token, RKV_READY])
            return [k_tokens[m]]

        def evacuate_v(i, c0, psum, token):
            n, dst = (META, V16[0:META, c0:c0 + 512]) if i == 0 else (P, V[:, i - 1, c0:c0 + 512])
            v_tokens.append(activate(dst, psum[0:n, :], ACT.Copy, [token, RKV_COL_READY, LAT_DONE],
                                     scale=cols[0:n, i:i + 1]))
            return [v_tokens[-1]]

        project("a_uq", 0, latent, T1, evacuate_q)
        project("a_uq", 0, latent, T1, evacuate_q)
        project("a_ukv", 0, latent, T1, evacuate_k, base=3)
        project_tokens("a_ukv", 0, latent, kv_starts, evacuate_v, base=3)

        TILES_A = [(0, META, META), (META, P, META + P), (META + P, P, T1)]
        PROB_AT = [0, META, META + META + P]
        heads_in_flight = deque()
        y_op = Operand()

        def scores_a(h):
            prob, free = temps.take()
            stats, sfree = small.take()
            done = []
            pair, half = h // 2, 64 * (h % 2)
            for j, (q0, nq, nk) in enumerate(TILES_A):
                bank, bfree = banks.take()
                matmul(bank[0:nq, 0:nk], qn[:, h, q0:q0 + nq], kn[:, h, 0:nk], True, False,
                       [bfree, q_tokens[h], k_tokens[h]])
                token = matmul(bank[0:nq, 0:nk], qr[half:half + ROPE, pair, q0:q0 + nq],
                               kr[half:half + ROPE, 0, 0:nk], False, True, [q_tokens[8 + pair], kr_tokens], True)
                at = PROB_AT[j]
                m0 = 144 if j == 0 else (128 if j == 1 else 0)
                freed, t_p, t_i, inv = softmax(prob[0:nq, at:at + nk], bank[0:nq, 0:nk], (NOPE + ROPE) ** -0.5,
                                               mask[0:nq, m0:m0 + nk], token, [free, sfree], stats, j)
                banks.give(bank, freed)
                done.append(ts(prob[0:nq, at:at + nk], prob[0:nq, at:at + nk], inv, ALU.mult, [t_p, t_i]))
            small.give(stats, done)
            heads_in_flight.append((h, prob, done))

        def values_a():
            h, prob, done = heads_in_flight.popleft()
            bank16, free16 = banks.take()
            bank, bfree = banks.take()
            for j, (q0, nq, nk) in enumerate(TILES_A):
                at = PROB_AT[j]
                t16 = transpose(bank16[0:META, q0:q0 + nq], prob[0:nq, at:at + META], nq, [done[j], free16, bfree],
                                j == 2)
                if j:
                    t_pe = transpose(bank[:, q0 - META:q0 - META + nq], prob[0:nq, at + META:at + META + P], nq,
                                     signal=True)
                if j == 2:
                    t_pe = transpose(bank[:, SEQ:SEQ + P], prob[0:nq, at + META + P:at + T1], nq, signal=True)
            temps.give(prob, [t_pe])
            pt, free = temps.take()
            t1 = activate(pt[0:META, 0:T1], bank16[0:META, 0:T1], ACT.Copy, [t16, free])
            t2 = activate(pt[:, T1:T1 + SEQ + P], bank[:, 0:SEQ + P], ACT.Copy, [t_pe, free])
            banks.give(bank16, [t1])
            banks.give(bank, [t2])
            return h, pt, t1, t2

        def outputs_a(h, pt, t1, t2):
            o, ofree = banks.take()
            cs = slice(h * P, (h + 1) * P)
            matmul(o[:, 0:T1], V16[0:META, cs], pt[0:META, 0:T1], True, False, [ofree, t1, t2, v_tokens])
            matmul(o[:, META:T1], V[:, 0, cs], pt[:, T1:T1 + SEQ], False, False)
            t3 = matmul(o[:, META + P:T1], V[:, 1, cs], pt[:, T1 + SEQ:T1 + SEQ + P], False, True, signal=True)
            temps.give(pt, [t3])
            y, yfree = temps.take()
            t4 = tt(y[:, 0:T1], o[:, 0:T1], silu_gate[:, h, :], ALU.mult, [t3, yfree, gate_tokens])
            banks.give(o, [t4])
            temps.give(y, split_tile(y_op, h, y[:, 0:T1], None, t4))

        def latent_attention():
            turned = deque()
            for h in range(HEADS + 2):
                if h < HEADS:
                    scores_a(h)
                    yield
                if len(turned) > 0:
                    outputs_a(*turned.popleft())
                if 1 <= h <= HEADS:
                    turned.append(values_a())
                yield

        background(latent_attention())
        project("a_in", 0, op, T1, evacuate_a_in)
        project("a_in", 0, op, T1, evacuate_a_in)
        op.give()
        project("a_uq", 0, latent, T1, evacuate_q)
        latent.give()
        finish_background()

        x_tokens = {}

        def add_to_residual(T, t0):
            def evacuate(m, psum, token):
                n = psum.shape[1]
                t1 = tt(x[:, m:m + n, t0:t0 + T], x[:, m:m + n, t0:t0 + T], psum, ALU.add, [token])
                for i in range(n):
                    x_tokens[m + i] = t1
                return [t1]
            return evacuate

        FENCE = everything()
        next_op = Operand()
        sum_x = SquareSum()

        def residual_then_split(T, t0, op, gain, total):
            add = add_to_residual(T, t0)

            def evacuate(m, psum, token):
                freed = add(m, psum, token)
                n = psum.shape[1]
                if gain is not None:
                    for i in range(n):
                        split_tile(op, m + i, x[:, m + i, t0:t0 + T], vcol(gain, m + i), freed)
                total.add(x[:, m:m + n, t0:t0 + T] if n > 1 else x[:, m, t0:t0 + T], freed)
                return freed
            return evacuate

        for _ in range(4):
            project("a_out", 0, y_op, T1, residual_then_split(T1, 0, next_op, "b_norm_g", sum_x))
        y_op.give()

        U = T1 + PAD
        u = region(0, 8, U)
        a_gate = region(0, 8, U)
        uc, rg = region(2200, 8, T1), region(4376, 8, T1)
        ig, silu_b = region(6552, 8, T1), region(8728, 8, SEQ)

        def statistics_b():
            nonlocal R_READY
            temp, t = sum_x.total()
            t_pe, R_READY = rstd_row(temp, t, D, T1, R, [FENCE])
            sum_x.give([t_pe])

        t_pad = on_dve(u[:, :, 0:PAD], lambda e: e.memset(u[:, :, 0:PAD], 0.0), [FENCE])
        uc_op = Operand()
        uc_tokens, rg_tokens, ig_tokens, gate_tokens = {}, {}, {}, {}

        def evacuate_u(m, psum, token):
            t0 = tt(u[:, m, PAD:U], psum[:, 0, :], R, ALU.mult, [token, R_READY, FENCE])
            c = uc[:, m, :]
            t1 = activate(c, u[:, m, 0:T1], ACT.Identity, [t0, t_pad, FENCE], scale=vcol("b_conv_w", m),
                          bias=vcol("b_conv_b", m))
            for j in range(1, 4):
                t1 = stt(c, u[:, m, j:j + T1], vcol("b_conv_w", 8 * j + m), c, ALU.mult, ALU.add, [t1])
            uc_tokens[m] = t1
            split_tile(uc_op, m, c, None, t1)
            return [t0]

        def evacuate_gate_b(m, psum, token):
            m, n = m - 8, psum.shape[1]
            row = R[:, META:T1].unsqueeze(1).to_broadcast([P, n, SEQ])
            t1 = tt(silu_b[:, m:m + n, :], psum, row, ALU.mult, [token, R_READY, FENCE])
            for i in range(n):
                gate_tokens[m + i] = t1
            return [t1]

        project("b_in", 0, next_op, T1, evacuate_u, hold=True)
        release(statistics_b)
        for _ in range(3):
            project("b_in", 0, next_op, T1, evacuate_u)

        def block_gates(bias, dst, tokens):
            chunk = Chunk("b_gates", 0)
            for m in range(8):
                bank, free = banks.take()
                for k in (2 * (m // 2), 2 * (m // 2) + 1):
                    w_h, w_l, ready = chunk.part(k, P * (m % 2), P * (m % 2) + P)
                    token = three(bank[:, 0:T1], w_h, w_l, uc_op.hi(k, 0, T1), uc_op.lo(k, 0, T1),
                                  k % 2 == 0, k % 2 == 1, [ready, free, uc_op.ready[k]], k % 2 == 1)
                tokens[m] = activate(dst[:, m, :], bank[:, 0:T1], ACT.Sigmoid, [token, FENCE], bias=vcol(bias, m))
                banks.give(bank, [tokens[m]])
                if m % 4 == 3:
                    chunk.done(m // 4, token)
            uc_op.read = [token]

        block_gates("b_b_rg", rg, rg_tokens)
        block_gates("b_b_ig", ig, ig_tokens)
        uc_op.give()
        y_op = Operand()

        def recurrence():
            conv_done = list(uc_tokens.values())
            a_tokens, th_tokens, in_tokens, sqrt_tokens = {}, {}, {}, {}
            th = [uc[:, m, :] for m in range(8)]
            for m in range(8):
                in_tokens[m] = tt(ig[:, m, :], ig[:, m, :], uc[:, m, :], ALU.mult, [ig_tokens[m], uc_tokens[m]])
            for m in range(8):
                th_tokens[m] = activate(th[m], rg[:, m, :], ACT.Tanh, [rg_tokens[m], LRU_READY, in_tokens[m],
                                                                       uc_op.ready[m]],
                                        scale=POS_SCALE[:, m:m + 1])
            yield
            for m in range(8):
                a_tokens[m] = activate(a_gate[:, m, 0:T1], rg[:, m, :], ACT.Exp,
                                       [rg_tokens[m], conv_done, LRU_READY], scale=NEG_SCALE[:, m:m + 1])
                sq_token = activate(rg[:, m, :], a_gate[:, m, 0:T1], ACT.Square, [a_tokens[m], th_tokens[m]])
                th_tokens[m] = stt(th[m], rg[:, m, :], 1.0, th[m], ALU.add, ALU.mult, [sq_token, th_tokens[m]])
                if m == 3:
                    yield
            yield
            for m0 in (0, 4):
                mult = uc[:, m0:m0 + 4, :]
                t = activate(mult, mult, ACT.Sqrt, [th_tokens[m] for m in range(m0, m0 + 4)])
                for m in range(m0, m0 + 4):
                    sqrt_tokens[m] = t
                yield
            while len(gate_tokens) < 8:
                yield
            silu = activate(silu_b, silu_b, ACT.Silu, list(gate_tokens.values()))
            for m in range(8):
                a, inp = a_gate[:, m, 0:T1], ig[:, m, :]
                t1 = tt(inp[:, 1:T1], inp[:, 1:T1], th[m][:, 1:T1], ALU.mult, [sqrt_tokens[m], in_tokens[m]])
                h_out = rg[:, m, :]
                t2 = on_dve(h_out, lambda e, h_out=h_out, a=a, inp=inp: e.tensor_tensor_scan(
                    h_out, a, inp, 0.0, ALU.mult, ALU.add), [t1, th_tokens[m]], 1.2)
                temp, free = temps.take()
                t3 = tt(temp[:, 0:SEQ], rg[:, m, META:T1], silu_b[:, m, :], ALU.mult, [t2, free, silu])
                temps.give(temp, split_tile(y_op, m, temp[:, 0:SEQ], None, t3))
                if m % 2:
                    yield

        MEM_KV = [(region(6656, 2, SEQ), region(7168, 2, SEQ)),
                  (mem_kv[:, 0:512].rearrange("p (n t) -> p n t", n=2),
                   mem_kv[:, 512:1024].rearrange("p (n t) -> p n t", n=2))]
        R_MEM, MEM_COL = RKV[:, 0:SEQ], cols[:, 4:6]
        starts2 = (0, P)
        mem_in = memT.rearrange("(k p) t -> p k t", p=P)
        mem_tokens = {}
        MEM_READY = []

        def split_memory(layer, gain, total):
            op = Operand()
            for i in range(4):
                temp, free = temps.take()
                v = temp[:, 0:2 * SEQ].rearrange("p (n t) -> p n t", n=2)
                sem = semaphore(f"memory{layer}_landed{i}")
                src = mem_in[:, 2 * i:2 * i + 2, :]
                in_temp = sp.do(lambda e, v=v, src=src: e.dma_start(v, src), free, cost=0.025, sem=sem, value=16)
                read = []
                for j in range(2):
                    read += split_tile(op, 2 * i + j, v[:, j, :], vcol(gain, 2 * i + j), in_temp)
                if total is not None:
                    read.append(total.add(v, in_temp))
                temps.give(temp, read)
            return op

        def memory_keys_values(layer, op, before=None):
            MK, MV = MEM_KV[layer]

            def evacuate_mk(m, psum, token):
                row = R_MEM.unsqueeze(1).to_broadcast([P, 2, SEQ])
                mem_tokens["k", layer] = tt(MK, psum, row, ALU.mult, [token, MEM_READY, FENCE])
                return [mem_tokens["k", layer]]

            def evacuate_mv(i, c0, psum, token):
                mem_tokens["v", layer, i] = activate(MV[:, i, :], psum, ACT.Copy, [token, MEM_READY, FENCE],
                                                     scale=cols[:, 4 + i:5 + i])
                return [mem_tokens["v", layer, i]]

            project("mem", layer, op, SEQ, evacuate_mk, hold=True)
            release(before)
            project_tokens("mem", layer, op, starts2, evacuate_mv)
            op.give()

        def statistics_memory():
            temp, t = sum_mem.total()
            t_pe1, t1 = rstd_row(temp, t, D, SEQ, R_MEM, [FENCE])
            t_pe2, t2 = rstd_col(temp, t, D, starts2, MEM_COL, [FENCE])
            sum_mem.give([t_pe1, t_pe2])
            MEM_READY.extend([t1, t2])

        background(recurrence())
        for _ in range(4):
            project("b_in", 0, next_op, SEQ, evacuate_gate_b, t0=META)
        next_op.give()
        sum_mem = SquareSum()
        mem_op = split_memory(1, "b_mem_norm_2", sum_mem)
        memory_keys_values(1, mem_op, statistics_memory)
        finish_background()
        FENCE = everything()
        xs = x[:, :, META:T1]

        mem_op = split_memory(0, "a_mem_norm_2", None)
        sum_x = SquareSum()
        for _ in range(4):
            project("b_out", 0, y_op, SEQ, residual_then_split(SEQ, META, None, None, sum_x))
        y_op.give()

        def final_norm_rows():
            nonlocal R_READY
            temp, t = sum_x.total()
            t_pe, R_READY = rstd_row(temp, t, D, SEQ, R[:, 0:SEQ], [FENCE])
            sum_x.give([t_pe])

        memory_keys_values(0, mem_op, final_norm_rows)
        op = Operand()
        sum_x = SquareSum()
        for k in range(DT):
            x_tokens[k] = stt(xs[:, k, :], xs[:, k, :], vcol("final_norm_g", k), R[:, 0:SEQ], ALU.mult, ALU.mult,
                              [R_READY, x_tokens[k]])
            split_tile(op, k, xs[:, k, :], vcol("a_norm_attn_2", k), x_tokens[k])
            sum_x.add(xs[:, k, :], x_tokens[k])

        q = region(0, 6, SEQ)
        kk = region(1536, 6, SEQ)
        vv = region(3072, 2, 768)
        qm = region(4608, 2, SEQ)
        o_tok = region(5120, 2, 768)
        RC = R[:, 0:SEQ]
        CR2, SR2, R2 = CR[:, 0:SEQ], SR[:, 0:SEQ], RQ[:, 0:SEQ]
        X_COL = cols[:, 0:2]
        TILES = [(0, P, P), (P, P, SEQ)]
        FULL_TILES = [(0, P, SEQ), (P, P, SEQ)]
        scale = DH ** -0.5
        tokens2 = {}

        def statistics_attention():
            temp, t = sum_x.total()
            t_pe1, t_row = rstd_row(temp, t, D, SEQ, RC, [FENCE])
            t_pe2, t_col = rstd_col(temp, t, D, starts2, X_COL, [FENCE])
            sum_x.give([t_pe1, t_pe2])
            tokens2["row"], tokens2["col"] = t_row, t_col
            tokens2["rope"] = [tt(CR2, cos[:, 0:SEQ], RC, ALU.mult, [t_row, FENCE]),
                               tt(SR2, sin[:, 0:SEQ], RC, ALU.mult, [t_row, FENCE])]

        def evacuate_qk(m, psum, token):
            dst, name, m = (q, "q", m) if m < 6 else (kk, "k", m - 6)
            freed, done = rope(dst[:, m:m + 2, :], psum, 2, SEQ, CR2, SR2, token, [tokens2["rope"], FENCE])
            tokens2[name, m] = tokens2[name, m + 1] = done
            return freed

        def evacuate_v2(group):
            def evacuate(i, c0, psum, token):
                t1 = activate(vv[:, i, 256 * group:256 * group + 256], psum, ACT.Copy,
                              [token, tokens2["col"], FENCE], scale=cols[:, i:i + 1])
                tokens2["v", i, group] = t1
                return [t1]
            return evacuate

        def evacuate_qm(m, psum, token):
            row = RC.unsqueeze(1).to_broadcast([P, 2, SEQ])
            t1 = tt(qm, psum, row, ALU.mult, [token, tokens2["row"], FENCE])
            tokens2["qm"] = [t1]
            return [t1]

        def score_tile(prob, free, stats, sfree, qt, kt_, p0, tiles, masked, after):
            done = []
            for j, (q0, nq, nk) in enumerate(tiles):
                bank, bfree = banks.take()
                token = matmul(bank[:, 0:nk], qt[p0:p0 + DH, q0:q0 + nq], kt_[p0:p0 + DH, 0:nk], True, True,
                               [bfree, after], True)
                at = 0 if j == 0 else SEQ
                m_ap = None if not masked else (mask[:, 144:144 + P] if j == 0 else mask[:, META:META + SEQ])
                freed, t_p, t_i, inv = softmax(prob[:, at:at + nk], bank[:, 0:nk], scale, m_ap, token,
                                               [free, sfree], stats, j)
                banks.give(bank, freed)
                done.append((t_p, t_i, inv, at, nk))
            return done

        def transposed(prob, done, causal):
            bank, bfree = banks.take()
            transpose(bank[:, 0:P], prob[:, 0:P], P, [done, bfree])
            t_pe = transpose(bank[:, P:SEQ], prob[:, SEQ:SEQ + P], P, signal=True)
            if causal:
                t_pe = transpose(bank[:, SEQ:SEQ + P], prob[:, SEQ + P:2 * SEQ], P, signal=True)
            else:
                transpose(bank[:, SEQ:SEQ + P], prob[:, P:SEQ], P)
                t_pe = transpose(bank[:, SEQ + P:2 * SEQ], prob[:, SEQ + P:2 * SEQ], P, signal=True)
            temps.give(prob, [t_pe])
            n = 3 * P if causal else 2 * SEQ
            pt, free = temps.take()
            t1 = activate(pt[:, 0:n], bank[:, 0:n], ACT.Copy, [t_pe, free])
            banks.give(bank, [t1])
            return pt, [t1]

        def normalize(prob, done):
            return [ts(prob[:, at:at + nk], prob[:, at:at + nk], inv, ALU.mult, [t_p, t_i])
                    for t_p, t_i, inv, at, nk in done]

        def head_pairs(n_heads, qt, kt_, v_of, causal, q_after, v_after, y_first):
            scored, turned, shared = deque(), deque(), {}

            def outputs(h, pt, t_pt):
                p0 = DH * (h % 2)
                if p0 == 0:
                    shared["o"] = banks.take()
                o, ofree = shared["o"]
                matmul(o[p0:p0 + DH, 0:SEQ], v_of(0, h), pt[:, 0:SEQ], True, False, [ofree, t_pt, v_after(h)])
                if causal:
                    t3 = matmul(o[p0:p0 + DH, P:SEQ], v_of(1, h), pt[:, SEQ:SEQ + P], False, True, signal=True)
                else:
                    t3 = matmul(o[p0:p0 + DH, 0:SEQ], v_of(1, h), pt[:, SEQ:2 * SEQ], False, True, signal=True)
                temps.give(pt, [t3])
                if p0:
                    banks.give(o, split_tile(y_op, y_first + h // 2, o[:, 0:SEQ], None, t3))

            for h in range(n_heads + 2):
                if h < n_heads:
                    while causal and ("v", 1, h // 4) not in tokens2:
                        yield
                    prob, free = temps.take()
                    stats, sfree = small.take()
                    done = score_tile(prob, free, stats, sfree, qt[:, h // 2, :], kt_[:, h // 2, :], DH * (h % 2),
                                      TILES if causal else FULL_TILES, causal, q_after(h // 2))
                    normed = normalize(prob, done)
                    small.give(stats, normed)
                    scored.append((h, prob, normed))
                    yield
                if turned:
                    outputs(*turned.popleft())
                if 1 <= h <= n_heads:
                    hh, prob, normed = scored.popleft()
                    turned.append((hh, *transposed(prob, normed, causal)))
                yield

        sums = lru[:, 48:60]

        def differential_attention():
            scored, turned, squared = deque(), deque(), []

            def outputs(h, pt, t_pt):
                cs = slice(h * P, (h + 1) * P)
                o, ofree = banks.take()
                v_after = [tokens2["v", 0, h // 2], tokens2["v", 1, h // 2]]
                matmul(o[:, 0:P], pt[:, 0:P], vv[:, 0, cs], True, True, [ofree, t_pt, v_after])
                matmul(o[:, P:SEQ], pt[:, P:SEQ], vv[:, 0, cs], True, False)
                t3 = matmul(o[:, P:SEQ], pt[:, SEQ:SEQ + P], vv[:, 1, cs], False, True, signal=True)
                temps.give(pt, [t3])
                t4 = copy(o_tok[:, :, cs], o[:, 0:SEQ].rearrange("p (n t) -> p n t", n=2), [t3, FENCE])
                banks.give(o, [t4])
                junk, jfree = temps.take()
                read = []
                for i in range(2):
                    t5 = activate(junk[:, i * P:(i + 1) * P], o_tok[:, i, cs], ACT.Square, [t4, jfree],
                                  accum=sums[:, 6 * i + h:6 * i + h + 1])
                    read.append(t5)
                squared.extend(read)
                temps.give(junk, read)

            for h in range(DIFF_HEADS + 2):
                if h < DIFF_HEADS:
                    while ("v", 1, h // 2) not in tokens2:
                        yield
                    parts = []
                    for c in range(2):
                        prob, free = temps.take()
                        stats, sfree = small.take()
                        after = [tokens2["q", h], tokens2["k", h]]
                        parts.append((prob, stats, score_tile(prob, free, stats, sfree, q[:, h, :], kk[:, h, :],
                                                              DH * c, TILES, True, after)))
                        if c == 0:
                            yield
                    (p_0, s_0, d_0), (p_1, s_1, d_1) = parts
                    merged = []
                    for j in range(2):
                        (tp0, ti0, inv0, at, nk), (tp1, ti1, inv1, _, _) = d_0[j], d_1[j]
                        t1 = ts(p_1[:, at:at + nk], p_1[:, at:at + nk], inv1, ALU.mult, [tp1, ti1, SMALL_READY],
                                NEG_LAMBDA, ALU.mult)
                        merged.append(stt(p_0[:, at:at + nk], p_0[:, at:at + nk], inv0, p_1[:, at:at + nk],
                                          ALU.mult, ALU.add, [tp0, ti0, t1]))
                    small.give(s_0, merged)
                    small.give(s_1, merged)
                    temps.give(p_1, merged)
                    scored.append((h, p_0, merged))
                    yield
                if turned:
                    outputs(*turned.popleft())
                if 1 <= h <= DIFF_HEADS:
                    hh, prob, merged = scored.popleft()
                    turned.append((hh, *transposed(prob, merged, True)))
                yield
            t1 = ts(sums, sums, 1.0 / P, ALU.mult, squared, EPS, ALU.add)
            t2 = activate(sums, sums, ACT.Sqrt, [t1])
            t3 = recip(sums, sums, [t2])
            for h in range(0, DIFF_HEADS, 2):
                bank, bfree = banks.take()
                for hh in range(2):
                    cs = slice((h + hh) * P, (h + hh + 1) * P)
                    for i in range(2):
                        s = sums[:, 6 * i + h + hh:6 * i + h + hh + 1]
                        t4 = ts(o_tok[:, i, cs], o_tok[:, i, cs], s, ALU.mult, [t3])
                        t_pe = transpose(bank[:, hh * SEQ + i * P:hh * SEQ + (i + 1) * P], o_tok[:, i, cs], P,
                                         [t4, bfree], True)
                view = bank[:, 0:2 * SEQ].rearrange("p (n t) -> p n t", n=2)
                banks.give(bank, split_tile(y_op, h, view, SUB_GAIN, [t_pe, SMALL_READY], n=2))

        def mlp(layer, x_op, R_row, statistics, after_sum, total_ready):
            hidden = {}
            down_sums = [banks.take() for _ in range(4)]

            def up(quarter, before=None):
                u_op = hidden[quarter] = Operand()

                def evacuate(m, psum, token):
                    m -= 8 * quarter
                    t_buf, free = temps.take()
                    v = t_buf[:, 0:2 * SEQ].rearrange("p (n t) -> p n t", n=2)
                    row = R_row.unsqueeze(1).to_broadcast([P, 2, SEQ])
                    t1 = stt(v, psum, 0.0, row, ALU.max, ALU.mult, [token, total_ready(), free])
                    t2 = activate(v, v, ACT.Square, [t1])
                    temps.give(t_buf, split_tile(u_op, m, v, None, t2, n=2))
                    return [t1]

                for i in range(4):
                    project("up", layer, x_op, SEQ, evacuate, hold=before is not None and i == 0)
                    if i == 0:
                        release(before)

            def down(quarter):
                u_op = hidden.pop(quarter)
                for c in range(4):
                    chunk = Chunk("down", layer)
                    bank, free = down_sums[c]
                    for j in range(2):
                        for k in range(8):
                            w_h, w_l, ready = chunk.part(k, j * P, (j + 1) * P)
                            token = three(bank[:, j * SEQ:(j + 1) * SEQ], w_h, w_l,
                                          u_op.hi(k, 0, SEQ), u_op.lo(k, 0, SEQ),
                                          quarter == 0 and k == 0 and j == 0, quarter == 3 and k == 7,
                                          [ready, free if quarter == 0 else [], u_op.ready[k]],
                                          k == 7, shared=True)
                        chunk.done(j, token)
                    u_op.read = [token]
                    if quarter == 3:
                        view = bank[:, 0:2 * SEQ].rearrange("p (n t) -> p n t", n=2)
                        banks.give(bank, after_sum(2 * c, view, token))
                u_op.give()

            up(0, statistics)
            up(1)
            down(0)
            up(2)
            down(1)
            up(3)
            x_op.give()
            down(2)
            return lambda: down(3)

        for layer in range(2):
            if layer == 0:
                q_op = kv_op = op
            y_op = Operand()
            project("in2", layer, q_op, SEQ, evacuate_qm, hold=True)
            release(statistics_attention)
            MK, MV = MEM_KV[layer]
            background(head_pairs(MEM_HEADS, qm, MK, lambda i, h, MV=MV: MV[:, i, h * DH:(h + 1) * DH], False,
                                  lambda p, layer=layer: [tokens2["qm"], mem_tokens["k", layer]],
                                  lambda h, layer=layer: [mem_tokens["v", layer, 0], mem_tokens["v", layer, 1]], 6),
                       rate=2)
            if layer == 1:
                attention = head_pairs(MOBA_HEADS, q, kk, lambda i, h: vv[:, i, h * DH:(h + 1) * DH], True,
                                       lambda p: [tokens2["q", p], tokens2["k", p]],
                                       lambda h: [tokens2["v", 0, h // 4], tokens2["v", 1, h // 4]], 0)
            else:
                attention = differential_attention()
            for group in range(3):
                project("in2", layer, q_op, SEQ, evacuate_qk)
                project("in2", layer, kv_op, SEQ, evacuate_qk)
                if group == 2:
                    q_op.give()
                project_tokens("in2", layer, kv_op, starts2, evacuate_v2(group))
                if group == 0:
                    finish_background()
                    background(attention, rate=1 + layer)
            if layer == 1:
                kv_op.give()
            finish_background()
            FENCE = everything()
            op = Operand()
            sum_x = SquareSum()
            gain = "a_norm_mlp_2" if layer == 0 else "b_norm_mlp_2"
            for _ in range(4):
                project("out2", layer, y_op, SEQ, residual_then_split(SEQ, META, op, gain, sum_x))
            y_op.give()

            def statistics_mlp():
                temp, t = sum_x.total()
                t_pe, tokens2["mlp"] = rstd_row(temp, t, D, SEQ, R2, [FENCE])
                sum_x.give([t_pe])

            def after_mlp(m, psum, token):
                return finish_x(m, psum, token)

            down_last = mlp(layer, op, R2, statistics_mlp, after_mlp, lambda: tokens2["mlp"])
            sum_x = SquareSum()
            if layer == 0:
                q_op = Operand()
                finish_x = residual_then_split(SEQ, META, q_op, "b_norm_attn_2", sum_x)
                down_last()
                kv_op = Operand()
                for k in range(DT):
                    split_tile(kv_op, k, xs[:, k, :], vcol("kv_norm_2", k), x_tokens[k])
            else:
                finish_x = residual_then_split(SEQ, META, None, None, sum_x)
                down_last()
            FENCE = everything()
            tokens2.clear()

        temp, t = sum_x.total()
        t_pe, R_READY = rstd_row(temp, t, D, SEQ, RC, [FENCE])
        for k in range(DT):
            x_tokens[k] = activate(xs[:, k, :], xs[:, k, :], ACT.Copy, [x_tokens[k], FENCE],
                                   scale=vcol("final_norm_2", k))
        out_sem = semaphore("output_written")
        stores = []
        row = RC.unsqueeze(1).to_broadcast([P, 2, SEQ])
        for k in (0, 2, 4):
            stores.append((k, 2, [tt(xs[:, k:k + 2, :], xs[:, k:k + 2, :], row, ALU.mult,
                                     [R_READY, x_tokens[k], x_tokens[k + 1]])]))
            if k == 2:
                for kp in (6, 7):
                    v = xs[:, kp, :]
                    t1 = pool.do(lambda e, v=v: e.tensor_tensor(v, v, RC, ALU.mult), [R_READY, x_tokens[kp]])
                    stores.append((kp, 1, [t1]))
        stores.sort(key=lambda s: s[0] if s[0] < 6 else s[0] - 3.5)

        for k, n, tokens in stores:
            dst, src = out[k * P:(k + n) * P, :].rearrange("(n p) t -> p n t", p=P), xs[:, k:k + n, :]
            sp.do(lambda e, dst=dst, src=src: e.dma_start(dst, src), tokens, sem=out_sem, value=0)
        plan.arrange()

        block = ctx.enter_context(nc.Block())

        @block.sync
        def _(e):
            sp.emit(e)
            e.wait_ge(out_sem, 16 * len(stores))

        @block.scalar
        def _(e):
            act.emit(e)

        @block.vector
        def _(e):
            dve.emit(e)

        @block.tensor
        def _(e):
            pe.emit(e)

        @block.gpsimd
        def _(e):
            pool.emit(e)


def rope_order():
    return [(p % 32) // 16 * 32 + 16 * (p // 32) + p % 16 for p in range(64)]


def rope_columns(first, n_heads, stride):
    return np.concatenate([first + h * stride + np.array(rope_order()) for h in range(n_heads)])


def shape_constants():
    c = np.zeros((P, N_CONST), np.float32)
    c[:, C_IDENT:C_IDENT + P] = np.eye(P, dtype=np.float32)
    c[:, C_ONES:C_ONES + P] = 1.0
    i = np.arange(P)
    c[:, C_MASK + 144:C_MASK + 272] = np.where(i[None, :] <= i[:, None], 0.0, NEG).astype(np.float32)
    inv = (np.float32(10000.0) ** (-np.arange(0, 64, 2, dtype=np.float32) / np.float32(64))).astype(np.float32)
    ang = (np.arange(T1, dtype=np.float32)[:, None] * inv[None, :]).astype(np.float64)
    for p in range(P):
        f = rope_order()[p % 64]
        c[p, C_COS:C_COS + T1] = np.cos(ang[:, f % 32])
        c[p, C_SIN:C_SIN + T1] = np.sin(ang[:, f % 32]) * (-1.0 if f < 32 else 1.0)
    return c


def kernel(**inputs):
    import concourse.bacc as bacc
    from concourse.bass_utils import run_bass_kernel_spmd

    v = {k: np.asarray(a) for k, a in inputs.items()}
    wi = v["a_w_in"][0]
    rope_k = wi[:, 640 + np.array(rope_order())]
    a_in = np.concatenate([wi[:, :640], rope_k, rope_k, wi[:, 704:]], axis=1)
    hd = NOPE + ROPE
    a_uq = v["a_w_uq"][0][:, np.concatenate(
        [h * hd + np.arange(NOPE) for h in range(HEADS)] + [rope_columns(NOPE, HEADS, hd)])]
    a_ukv = v["a_w_ukv"][0][:, np.concatenate(
        [h * 256 + np.arange(NOPE) for h in range(HEADS)] + [h * 256 + NOPE + np.arange(128) for h in range(HEADS)])]
    gates = [v[n][0].reshape(D, 256) for n in ("b_w_rg", "b_w_ig")]
    r12 = rope_columns(0, 12, DH)
    in_a = v["a_w_in_2"][0][:, np.concatenate([r12, 768 + r12, np.arange(1536, 2560)])]
    in_b = np.concatenate([v["b_w_in_2"][0][:, r12], v["w_kv_2"][:, r12], v["w_kv_2"][:, 768:],
                           v["b_w_in_2"][0][:, 768:]], axis=1)
    weights = {
        ("a_in", 0): a_in, ("a_uq", 0): a_uq, ("a_ukv", 0): a_ukv, ("a_out", 0): v["a_w_out"][0],
        ("b_in", 0): v["b_w_in"][0], ("b_out", 0): v["b_w_out"][0],
        ("mem", 0): v["a_w_mem_kv_2"][0], ("mem", 1): v["b_w_mem_kv_2"][0],
        ("in2", 0): in_a, ("in2", 1): in_b,
        ("out2", 0): v["a_w_out_2"][0], ("out2", 1): v["b_w_out_2"][0],
        ("up", 0): v["a_w_up_2"][0], ("up", 1): v["b_w_up_2"][0],
        ("down", 0): v["a_w_down_2"][0], ("down", 1): v["b_w_down_2"][0],
    }
    order = chunk_order()
    stream = np.zeros((len(order), P, CHUNK), np.float32)
    for n, (kind, layer, i) in enumerate(order):
        kt, w = SHAPES[kind]
        if kind == "b_gates":
            block = gates[i]
        elif kind == "down":
            block = weights[kind, layer][(i // 4) * 1024:(i // 4 + 1) * 1024, (i % 4) * w:(i % 4 + 1) * w]
        else:
            block = weights[kind, layer][:, i * w:(i + 1) * w]
        by_inputs, kh, wh = halves_of(kind, i)
        tiles = block.reshape(kt, P, w).transpose(1, 0, 2)
        for half in range(2):
            part = tiles[:, half * kh:(half + 1) * kh] if by_inputs else tiles[:, :, half * wh:(half + 1) * wh]
            stream[n, :, half * kh * wh:(half + 1) * kh * wh] = part.reshape(P, kh * wh)
    vecs = np.concatenate([v[n].reshape(k, P).T for n, k in VECTORS], axis=1)
    consts = shape_constants()
    consts[:, C_LAM:] = v["a_lambda_2"].reshape(1, -1)
    arrays = {
        "stream": stream,
        "xT": np.ascontiguousarray(np.concatenate([v["meta_tokens"], v["x"][0]], axis=0).T),
        "memT": np.ascontiguousarray(v["mem_2"][0].T),
        "vecs": np.ascontiguousarray(vecs),
        "consts": consts,
    }
    nc = bacc.Bacc("TRN2", target_bir_lowering=False, num_devices=1)
    args = [nc.dram_tensor(f"{n}_dram", a.shape, F32, kind="ExternalInput").ap() for n, a in arrays.items()]
    out = nc.dram_tensor("out_dram", (D, SEQ), F32, kind="ExternalOutput").ap()
    program(nc, *args, out)
    r = run_bass_kernel_spmd(nc, [{f"{n}_dram": a for n, a in arrays.items()}], core_ids=[0])
    return np.ascontiguousarray(r.results[0]["out_dram"].T).reshape(1, SEQ, D)
```

```python
from collections import deque
from contextlib import ExitStack

import numpy as np

import concourse.bass as bass
from concourse import mybir

F32 = mybir.dt.float32
F32R = mybir.dt.float32r
ACT = mybir.ActivationFunctionType
ALU = mybir.AluOpType
AX_X = mybir.AxisListType.X

P = 128
D = 1024
DT = D // P
SEQ = 256
META = 16
T1 = META + SEQ
EPS = 1e-6
NEG = -1e30
CHUNK = 2048
PAD = 3

HEADS, NOPE, ROPE, Q_LORA, KV_LORA = 8, 128, 64, 384, 256
DIFF_HEADS, MOBA_HEADS, MEM_HEADS, DH = 6, 12, 4, 64
D_FF = 4096
LAMBDA_INIT = 0.8 - 0.6 * 1.0
LRU_C = 8.0

SHAPES = {
    "a_in": (8, 256), "a_uq": (3, 512), "a_ukv": (2, 1024), "a_out": (8, 256),
    "b_in": (8, 256), "b_gates": (8, 256), "b_out": (8, 256),
    "mem": (8, 256), "in2": (8, 256), "out2": (8, 256), "up": (8, 256), "down": (8, 256),
}
HALF = CHUNK // 2


def halves_of(kind, index):
    kt, w = SHAPES[kind]
    by_inputs = ((kind, index) == ("a_in", 0) or kind == "b_gates" or (kind == "mem" and index == 1)
                 or (kind == "in2" and index in (6, 7, 8)))
    return (True, kt // 2, w) if by_inputs else (False, kt, w // 2)


UP_DOWN = [("up", 0), ("up", 1), ("down", 0), ("up", 2), ("down", 1), ("up", 3), ("down", 2), ("down", 3)]


IN2_ORDER = (9, 0, 3, 6, 1, 4, 2, 5, 7, 8)


def chunk_order():
    order = [("a_in", 0, i) for i in range(5)]
    order += [("a_uq", 0, 0), ("a_uq", 0, 2), ("a_ukv", 0, 0), ("a_ukv", 0, 1)]
    order += [("a_in", 0, 5), ("a_in", 0, 6), ("a_uq", 0, 1)]
    order += [("mem", 0, i) for i in range(2)] + [("a_out", 0, i) for i in range(4)]
    order += [("b_in", 0, i) for i in range(3)] + [("b_gates", 0, 0), ("b_in", 0, 3), ("b_in", 0, 4)]
    order += [("b_gates", 0, 1)] + [("b_in", 0, i) for i in range(5, 8)]
    order += [("b_out", 0, i) for i in range(4)]
    for layer in range(2):
        order += [("in2", layer, i) for i in IN2_ORDER]
        if layer == 0:
            order += [("mem", 1, i) for i in range(2)]
        order += [("out2", layer, i) for i in range(4)]
        for kind, quarter in UP_DOWN:
            order += [(kind, layer, 4 * quarter + i) for i in range(4)]
    return order


VECTORS = [("a_norm_g", 8), ("a_q_norm_g", 3), ("a_kv_norm_g", 2), ("b_norm_g", 8),
           ("b_conv_w", 32), ("b_conv_b", 8), ("b_b_rg", 8), ("b_b_ig", 8), ("b_lam", 8),
           ("final_norm_g", 8), ("a_norm_attn_2", 8), ("a_subln_2", 1), ("a_mem_norm_2", 8),
           ("a_norm_mlp_2", 8), ("kv_norm_2", 8), ("b_norm_attn_2", 8), ("b_mem_norm_2", 8),
           ("b_norm_mlp_2", 8), ("final_norm_2", 8)]
VEC_AT, _n = {}, 0
for _name, _k in VECTORS:
    VEC_AT[_name] = _n
    _n += _k
N_VEC = _n
C_IDENT, C_ONES, C_MASK, C_COS, C_SIN, C_LAM = 0, 128, 256, 528, 800, 1072
N_CONST = 1072 + 4 * DH


class Instruction:

    def __init__(self, queue, number, issue, after, cost, strand, signal, table, sem, value):
        self.queue, self.number, self.issue, self.after = queue, number, issue, after
        self.cost, self.strand, self.counted, self.table = cost, strand, signal, table
        self.sem, self.value = sem, value
        self.late = self.end = None


class Fence:

    def __init__(self, number):
        self.number = number


def flat(tokens):
    if isinstance(tokens, (Instruction, Fence)):
        yield tokens
    elif tokens is not None:
        for t in tokens:
            yield from flat(t)


class Queue:

    def __init__(self, plan, name, sem):
        self.plan, self.name, self.sem = plan, name, sem
        self.strand, self.order = "main", []
        plan.queues.append(self)

    def do(self, issue, after=(), signal=True, cost=0.1, strand=None, table=None, sem=None, value=None):
        i = Instruction(self, len(self.plan.all), issue, list(flat(after)), cost, strand or self.strand,
                        signal, table, sem, value)
        self.plan.all.append(i)
        return i

    def emit(self, engine):
        waited = {}
        for i in self.order:
            need = {}
            for sem, value in self.plan.values(i.after):
                if value > max(waited.get(sem.name, 0), need.get(sem.name, (None, 0))[1]):
                    need[sem.name] = (sem, value)
            for name, (sem, value) in need.items():
                waited[name] = value
                engine.wait_ge(sem, value)
            instruction = i.issue(engine)
            if i.counted:
                instruction.then_inc(i.sem, 16 if i.queue.name == "sp" else 1)


class Plan:

    LATENCY = {"pe": 0.2, "dve": 0.13, "act": 0.235, "pool": 0.2, "sp": 0.1}
    TABLE_LOAD, DMA_LATENCY, DMA_ISSUE = 1.3, 1.9, 0.45
    PATIENCE = 0.3
    TABLE_RANK, LEAD = 2.5, {"statistics": 20.0, "attention": 10.0}
    WINDOW = 120

    def __init__(self):
        self.queues, self.all = [], []

    def fence(self):
        return Fence(len(self.all))

    def values(self, tokens):
        for t in tokens:
            if isinstance(t, Instruction):
                yield t.sem, t.value
            else:
                for q in self.queues:
                    last = max((i.value for i in q.order if i.number < t.number and i.counted and i.sem is q.sem),
                               default=0)
                    if last:
                        yield q.sem, last

    def latency(self, t, i):
        return self.LATENCY[t.queue.name] - (0.09 if t.queue is i.queue and t.queue.name == "act" else 0)

    def latest_starts(self):
        clock = 0.0
        for i in self.all:
            if i.queue.name == "pe":
                i.late = clock
                clock += i.cost
        for i in self.all:
            if i.late is None:
                i.late = 1e9
        for i in reversed(self.all):
            if i.late > 1e8:
                i.late = clock
            for t in i.after:
                if isinstance(t, Instruction):
                    t.late = min(t.late, i.late - t.cost - self.latency(t, i))

    @staticmethod
    def loads(i, table):
        return i.table not in (None, table) and not (i.table == "tanh" and table in ("exp", "sigmoid"))

    def arrange(self):
        self.latest_starts()
        waiting = {q: [i for i in self.all if i.queue is q] for q in self.queues}
        free = {q: 0.0 for q in self.queues}
        table, dma_free = None, 0.0
        pe = next(q for q in self.queues if q.name == "pe")
        strands = {}
        for i in waiting[pe]:
            strands.setdefault(i.strand, deque()).append(i)

        def heads():
            return [s[0] for s in strands.values() if s]

        def unit(i):
            members = []
            for j in strands[i.strand]:
                members.append(j)
                if j.counted:
                    return members

        done, lowest, prefix = 0, 0, [0.0]
        while done < len(self.all):
            while lowest < len(self.all) and self.all[lowest].end is not None:
                prefix.append(max(prefix[-1], self.all[lowest].end))
                lowest += 1

            def ready(i):
                at = 0.0
                for t in i.after:
                    if isinstance(t, Fence):
                        if t.number > lowest:
                            return None
                        at = max(at, prefix[t.number] + self.LATENCY["act"])
                    elif t.end is None:
                        return None
                    else:
                        at = max(at, t.end + self.latency(t, i))
                return at

            best = None
            for q in self.queues:
                candidates = []
                for n, i in enumerate(heads() if q is pe else waiting[q][:self.WINDOW]):
                    at = ready(i)
                    if at is None:
                        continue
                    start = max(at, free[q])
                    rank = i.late
                    if q is pe:
                        if any(ready(j) is None for j in unit(i)):
                            continue
                        rank -= self.LEAD.get(i.strand, 0.0)
                    if self.loads(i, table):
                        rank += self.TABLE_RANK
                    candidates.append((start, rank, i.number, n, i))
                if candidates:
                    soonest = min(candidates)[0] + self.PATIENCE
                    start, rank, number, n, i = min((c for c in candidates if c[0] <= soonest), key=lambda c: c[1:3])
                    if best is None or (start, rank) < best[0]:
                        best = ((start, rank), q, n, i, start)
            _, q, n, i, start = best
            if q is pe:
                for j in unit(i):
                    free[pe] = j.end = max(free[pe], ready(j)) + j.cost
                    pe.order.append(j)
                    strands[i.strand].popleft()
                    done += 1
                continue
            waiting[q].pop(n)
            q.order.append(i)
            if self.loads(i, table):
                table = i.table
                start += self.TABLE_LOAD
            free[q] = i.end = start + i.cost
            if q.name == "sp":
                free[q] = start + self.DMA_ISSUE
                dma_free = max(start + self.DMA_LATENCY / 2, dma_free) + i.cost
                i.end = dma_free + self.DMA_LATENCY
            done += 1
        for q in self.queues:
            count = 0
            for i in q.order:
                if i.sem is None:
                    i.sem = q.sem
                    count += i.counted
                    i.value = count


def columns(ap):
    return int(np.prod(ap.shape[1:]))


class Buffers:

    def __init__(self, buffers):
        self.free = deque((b, []) for b in buffers)

    def take(self):
        return self.free.popleft()

    def give(self, buffer, tokens):
        self.free.append((buffer, tokens))


def program(nc, stream, xT, memT, vecs, consts, out):
    ctx = ExitStack()
    with ctx:
        def sb(name, shape, dt=F32):
            return ctx.enter_context(nc.sbuf_tensor(name, shape, dt))

        def semaphore(name):
            return ctx.enter_context(nc.semaphore(name))

        plan = Plan()
        pe, act, dve, pool, sp = (Queue(plan, n, semaphore(f"{n}_done")) for n in ("pe", "act", "dve", "pool", "sp"))

        N_RAW, N_SPLIT, N_OPERAND, N_TEMP = 5, 6, 3, 7
        raw = [sb(f"weights_raw{i}", [P, HALF]) for i in range(N_RAW)]
        w_hi = [sb(f"weights_hi{i}", [P, HALF], F32R) for i in range(N_SPLIT)]
        w_lo = [sb(f"weights_lo{i}", [P, HALF], F32R) for i in range(N_SPLIT)]
        operands = Buffers([(sb(f"operand_hi{i}", [P, DT, T1], F32R), sb(f"operand_lo{i}", [P, DT, T1], F32R))
                            for i in range(N_OPERAND)])
        temps = Buffers([sb(f"temp{i}", [P, 656]) for i in range(N_TEMP)])
        small = Buffers([sb(f"softmax_stats{i}", [P, 16]) for i in range(6)])
        x = sb("residual", [P, DT, T1])
        ARENA = 10960
        arena = sb("arena", [P, ARENA])
        rows = sb("rows", [P, 5, T1])
        cols = sb("cols", [P, 16])
        vec = sb("vectors", [P, N_VEC])
        const = sb("constants", [P, C_LAM])
        lru = sb("lru_scales", [P, 68])
        mem_kv = [sb(f"memory_keys_values{i}", [P, 1024]) for i in range(2)]
        banks = Buffers([ctx.enter_context(nc.psum_tensor(f"bank{i}", [P, 512], F32)) for i in range(8)])

        ident = const[:, C_IDENT:C_IDENT + P]
        ones = const[:, C_ONES:C_ONES + P]
        mask = const[:, C_MASK:C_MASK + T1]
        cos = const[:, C_COS:C_COS + T1]
        sin = const[:, C_SIN:C_SIN + T1]

        def vcol(name, i=0):
            return vec[:, VEC_AT[name] + i:VEC_AT[name] + i + 1]

        def region(start, *shape):
            n = int(np.prod(shape))
            assert start + n <= ARENA
            ap = arena[:, start:start + n]
            if len(shape) == 2:
                ap = ap.rearrange("p (a b) -> p a b", a=shape[0])
            return ap

        def matmul(out, lhsT, rhs, start, stop, after=(), signal=False, shared=False):
            cost = 0.002 + max(0.107, columns(rhs) * (4.17e-4 if rhs.dtype == F32R else 1.68e-3))
            return pe.do(lambda e: e.matmul(out, lhsT, rhs, start=start, stop=stop, skip_group_check=shared),
                         after, signal, cost)

        def transpose(out, in_, n, after=(), signal=False):
            return pe.do(lambda e: e.transpose(out, in_, ident[0:n, 0:n]), after, signal, 8.4e-4 * n)

        SETS = {ACT.Exp: "exp", ACT.Silu: "silu", ACT.Sigmoid: "sigmoid", ACT.Tanh: "tanh", ACT.Sqrt: "sqrt"}

        def activate(out, in_, func, after, scale=1.0, bias=0.0, accum=None):
            cost = 0.08 + 8.5e-4 * columns(out) + (0.1 if accum is not None or isinstance(scale, bass.AP) else 0)
            if accum is None:
                return act.do(lambda e: e.activation(out, in_, func, bias=bias, scale=scale), after, cost=cost,
                              table=SETS.get(func))
            return act.do(lambda e: e.activation(out, in_, func, bias=bias, scale=scale, accum_out=accum), after,
                          cost=cost, table=SETS.get(func))

        def on_dve(out, issue, after, rate=1.0):
            return dve.do(issue, after, cost=0.07 + 1.05e-3 * rate * columns(out))

        def tt(out, a, b, op, after):
            return on_dve(out, lambda e: e.tensor_tensor(out, a, b, op), after)

        def ts(out, a, s1, op0, after, s2=None, op1=None):
            if op1 is None:
                return on_dve(out, lambda e: e.tensor_scalar(out, a, s1, None, op0), after)
            return on_dve(out, lambda e: e.tensor_scalar(out, a, s1, s2, op0, op1), after)

        def stt(out, a, s, b, op0, op1, after):
            return on_dve(out, lambda e: e.scalar_tensor_tensor(out, a, s, b, op0, op1), after, 1.05)

        def reduce(out, in_, op, after):
            return on_dve(in_, lambda e: e.tensor_reduce(out, in_, AX_X, op), after)

        def recip(out, in_, after):
            return on_dve(out, lambda e: e.reciprocal(out, in_), after, 5.5)

        def copy(out, in_, after):
            return on_dve(out, lambda e: e.tensor_copy(out, in_), after)

        def everything():
            return plan.fence()

        order = chunk_order()
        PIECES = 4
        raw_sems = [semaphore(f"weights_landed{i}") for i in range(N_RAW)]
        piece_sems = [semaphore(f"first_weights_landed{i}") for i in range(PIECES)]
        split_tokens, arrived = {}, {}
        raw_free, split_free = [[] for _ in range(N_RAW)], [[] for _ in range(N_SPLIT)]
        state = {"loaded": 2, "split": 0, "used": 0}

        def load(dst, src, sem, after=(), value=16):
            return sp.do(lambda e: e.dma_start(dst, src), after, cost=1.43e-3 * columns(dst), sem=sem, value=value)

        def half_size(v):
            return int(np.prod(SHAPES[order[v // 2][0]])) // 2

        def load_next():
            v = state["loaded"]
            if v == 2 * len(order):
                return
            state["loaded"] += 1
            r, size = v % N_RAW, half_size(v)
            value = 16 * (v // N_RAW + (r > 1))
            src = stream[v // 2, :, (v % 2) * size:(v % 2 + 1) * size]
            arrived[v, 0] = load(raw[r][:, 0:size], src, raw_sems[r], raw_free[r], value)

        def load_first(i):
            v, size = i // 2, half_size(0) // 2
            a = (i % 2) * size
            src = stream[0, :, v * 2 * size + a:v * 2 * size + a + size]
            arrived[v, a] = load(raw[v][:, a:a + size], src, piece_sems[i])

        def split_columns(v, a, b):
            s, (_, _, wh) = v % N_SPLIT, halves_of(order[v // 2][0], order[v // 2][2])
            src, hi, lo = raw[v % N_RAW][:, a:b], w_hi[s][:, a:b], w_lo[s][:, a:b]
            t_hi = activate(hi, src, ACT.Copy, [arrived[v, a], split_free[s]])
            tokens = [t_hi, tt(lo, src, hi.bitcast(F32), ALU.subtract, [arrived[v, a], t_hi, split_free[s]])]
            for k in range(a // wh, b // wh):
                split_tokens[v, k] = tokens
            return tokens

        def split_first(i):
            v, size = i // 2, half_size(0) // 2
            a = (i % 2) * size
            raw_free[v] = raw_free[v] + split_columns(v, a, a + size)
            if i % 2:
                state["split"] += 1
                load_next()

        def split_next():
            v = state["split"]
            state["split"] += 1
            raw_free[v % N_RAW] = split_columns(v, 0, half_size(v))
            load_next()

        class Chunk:

            def __init__(self, kind, layer):
                self.n = n = state["used"]
                assert order[n][0] == kind and order[n][1] == layer, (order[n], kind, layer)
                state["used"] += 1
                self.index = order[n][2]
                self.by_inputs, self.kh, self.wh = halves_of(kind, self.index)
                self.begun = -1

            def begin(self, half):
                if half == self.begun:
                    return
                self.begun = half
                while state["split"] < min(2 * self.n + half + N_SPLIT, 2 * len(order)):
                    split_next()

            def part(self, k, c0, c1):
                half, k, c = (k // self.kh, k % self.kh, c0) if self.by_inputs else (c0 // self.wh, k, c0 % self.wh)
                self.begin(half)
                s, a = (2 * self.n + half) % N_SPLIT, k * self.wh + c
                return (w_hi[s][:, a:a + c1 - c0], w_lo[s][:, a:a + c1 - c0], split_tokens[2 * self.n + half, k])

            def done(self, half, token):
                split_free[(2 * self.n + half) % N_SPLIT] = [token]

        waiting_steps = deque()

        def background(stage, rate=1):
            waiting_steps.append((stage, rate))

        def step():
            if waiting_steps:
                stage, rate = waiting_steps[0]
                pe.strand = "attention"
                for _ in range(rate):
                    if next(stage, "end") == "end":
                        waiting_steps.popleft()
                        break
                pe.strand = "main"

        def finish_background():
            while waiting_steps:
                step()

        class Operand:

            def __init__(self):
                (self.hi_t, self.lo_t), self.free = operands.take()
                self.ready, self.read = {}, []
                self.base = 0

            def hi(self, k, t0, t1):
                return self.hi_t[:, k, t0:t1]

            def lo(self, k, t0, t1):
                return self.lo_t[:, k, t0:t1]

            def give(self):
                operands.give((self.hi_t, self.lo_t), self.read)

        def split_tile(op, k, src, gain, after, n=1):
            T = src.shape[-1]
            hi, lo = op.hi_t[:, k:k + n, 0:T], op.lo_t[:, k:k + n, 0:T]
            if len(src.shape) == 2:
                hi, lo = op.hi_t[:, k, 0:T], op.lo_t[:, k, 0:T]
            if gain is None:
                t1 = activate(hi, src, ACT.Copy, [after, op.free])
                t2 = tt(lo, src, hi.bitcast(F32), ALU.subtract, [after, op.free, t1])
            else:
                t1 = activate(hi, src, ACT.Copy, [after, op.free], scale=gain)
                t2 = stt(lo, src, gain, hi.bitcast(F32), ALU.mult, ALU.subtract, [after, op.free, t1])
            for i in range(n):
                op.ready[k + i] = [t1, t2]
            return [t1, t2]

        def three(out, w_h, w_l, x_h, x_l, first, last, after, signal, shared=False):
            matmul(out, w_h, x_h, first, False, after, shared=shared)
            matmul(out, w_h, x_l, False, False, shared=shared)
            return matmul(out, w_l, x_h, False, last, signal=signal, shared=shared)

        held = []

        def release(before=None):
            if before is not None:
                pe.strand = "statistics"
                before()
                pe.strand = "main"
            while held:
                evacuate, m, view, token, bank = held.pop(0)
                banks.give(bank, evacuate(m, view, token))

        def project(kind, layer, op, T, evacuate, t0=0, base=0, hold=False):
            chunk = Chunk(kind, layer)
            kt, w = SHAPES[kind]
            per = 2 if 2 * T <= 512 else 1
            groups = []

            def product(bank, free, m, j, ks):
                for k in ks:
                    w_h, w_l, ready = chunk.part(k, m * P, (m + 1) * P)
                    last = k == kt - 1
                    token = three(bank[:, j * T:(j + 1) * T], w_h, w_l,
                                  op.hi(base + k, t0, t0 + T), op.lo(base + k, t0, t0 + T),
                                  k == 0, last, [ready, free, op.ready[base + k]],
                                  k == ks[-1], shared=chunk.by_inputs)
                return token

            def finished(m0, bank, token):
                view = bank[:, 0:per * T].rearrange("p (n t) -> p n t", n=per)
                held.append((evacuate, chunk.index * (w // P) + m0, view, token, bank))
                if not hold:
                    release()

            if chunk.by_inputs:
                taken = [banks.take() for _ in range(w // P)]
                for half in range(2):
                    for m, (bank, free) in enumerate(taken):
                        token = product(bank, free, m, 0, range(half * chunk.kh, (half + 1) * chunk.kh))
                        if half:
                            finished(m, bank, token)
                            step()
                    chunk.done(half, token)
            else:
                for m0 in range(0, w // P, per):
                    bank, free = banks.take()
                    for j in range(per):
                        m = m0 + j
                        token = product(bank, free, m, j, range(kt))
                        if (m + 1) * P % chunk.wh == 0:
                            chunk.done(m * P // chunk.wh, token)
                        if j == per - 1:
                            finished(m0, bank, token)
                        step()
            op.read = [token]

        def project_tokens(kind, layer, op, starts, evacuate, base=0):
            chunk = Chunk(kind, layer)
            kt, w = SHAPES[kind]

            def product(o, t0, c0, c1, ks, free):
                for k in ks:
                    w_h, w_l, ready = chunk.part(k, c0, c1)
                    x_h, x_l = op.hi(base + k, t0, t0 + P), op.lo(base + k, t0, t0 + P)
                    matmul(o, x_h, w_h, k == 0, False, [ready, free, op.ready[base + k]])
                    matmul(o, x_h, w_l, False, False)
                    token = matmul(o, x_l, w_h, False, k == kt - 1, signal=k == ks[-1])
                return token

            if chunk.by_inputs:
                taken = [banks.take() for _ in starts]
                for half in range(2):
                    for i, (bank, free) in enumerate(taken):
                        token = product(bank[:, 0:w], starts[i], 0, w, range(half * chunk.kh, (half + 1) * chunk.kh),
                                        free)
                        if half:
                            banks.give(bank, evacuate(i, 0, bank[:, 0:w], token))
                        step()
                    chunk.done(half, token)
            else:
                for c0 in range(0, w, chunk.wh):
                    for i, t0 in enumerate(starts):
                        bank, free = banks.take()
                        token = product(bank[:, 0:chunk.wh], t0, c0, c0 + chunk.wh, range(kt), free)
                        banks.give(bank, evacuate(i, c0, bank[:, 0:chunk.wh], token))
                        step()
                    chunk.done(c0 // chunk.wh, token)
            op.read = [token]

        class SquareSum:

            def __init__(self):
                (self.acc, self.free), self.token = temps.take(), None
                self.read = []

            def add(self, src, after, gain=1.0):
                n, T = (1, src.shape[-1]) if len(src.shape) == 2 else (src.shape[1], src.shape[2])
                acc = self.acc[:, 0:n * T]
                if n > 1:
                    acc = acc.rearrange("p (n t) -> p n t", n=n)
                if self.token is None:
                    self.n, self.T = n, T
                    self.token = activate(acc, src, ACT.Square, [after, self.free], scale=gain)
                    return self.token
                sq, free = temps.take()
                v = sq[:, 0:n * T]
                if n > 1:
                    v = v.rearrange("p (n t) -> p n t", n=n)
                t1 = activate(v, src, ACT.Square, [after, free], scale=gain)
                self.token = tt(acc, acc, v, ALU.add, [t1, self.token])
                temps.give(sq, [self.token])
                return t1

            def total(self):
                T = self.T
                if self.n == 2:
                    self.token = tt(self.acc[:, 0:T], self.acc[:, 0:T], self.acc[:, T:2 * T], ALU.add,
                                    [self.token])
                    self.n = 1
                return self.acc, self.token

            def give(self, read):
                temps.give(self.acc, read)

        scratch_read = []

        def token_tiles(T):
            return [(0, META), (META, P), (META + P, P)] if T == T1 else [(0, P), (P, P)]

        def mean_square(temp, token, n_features, T, col, after, eps=EPS):
            tiles = token_tiles(T)
            bank, free = banks.take()
            for i, (t0, _) in enumerate(tiles):
                t1 = matmul(bank[:, i:i + 1], temp[:, t0:t0 + P], ones[:, 0:1], True, True, [token, free],
                            i == len(tiles) - 1)
            t2 = ts(col, bank[:, 0:len(tiles)], 1.0 / n_features, ALU.mult, [t1, after], eps, ALU.add)
            banks.give(bank, [t2])
            return t1, t2

        def rsqrt(col, token):
            return recip(col, col, [activate(col, col, ACT.Sqrt, [token])])

        def spread(row, col, token, T, after):
            tiles = token_tiles(T)
            diag, dfree = temps.take()
            bank, free = banks.take()
            for i, (t0, nt) in enumerate(tiles):
                t1 = ts(diag[0:nt, t0:t0 + nt], ident[0:nt, 0:nt], col[0:nt, i:i + 1], ALU.mult, [token, dfree])
                t2 = matmul(bank[:, t0:t0 + nt], ones[0:nt, :], diag[0:nt, t0:t0 + nt], True, True, [t1, free],
                            i == len(tiles) - 1)
            temps.give(diag, [t2])
            t3 = activate(row, bank[:, 0:T], ACT.Copy, [t2, after])
            banks.give(bank, [t3])
            return t3

        def rstd(temp, token, n_features, T, row, after, col=None):
            scratch = col is None
            if scratch:
                col, after = cols[:, 13:13 + len(token_tiles(T))], [after, scratch_read]
            t1, t2 = mean_square(temp, token, n_features, T, col, after)
            t3 = rsqrt(col, t2)
            t4 = spread(row, col, t3, T, after)
            if scratch:
                scratch_read[:] = [t4]
            return t1, t4, t3

        SWAP = [(r + 16) % 32 for r in range(32)]

        def rope(out, psum, n, T, cos_row, sin_row, token, after):
            a, free_a = temps.take()
            b, free_b = temps.take()
            ap = a[:, 0:n * T].rearrange("p (n t) -> p n t", n=n)
            bp = b[:, 0:n * T].rearrange("p (n t) -> p n t", n=n)
            cb = cos_row.unsqueeze(1).to_broadcast([P, n, T])
            sb_ = sin_row.unsqueeze(1).to_broadcast([P, n, T])
            t1 = activate(ap, psum, ACT.Copy, [token, free_a])
            t2 = on_dve(b[:, 0:n * T], lambda e: e.stream_shuffle(b[:, 0:n * T], a[:, 0:n * T], SWAP), [t1, free_b])
            t3 = tt(bp, bp, sb_, ALU.mult, [t2, after])
            t4 = tt(ap, ap, cb, ALU.mult, [t2, after])
            t5 = tt(out, ap, bp, ALU.add, [t3, t4, after])
            temps.give(a, [t5])
            temps.give(b, [t5])
            return [t1], [t5]

        def softmax(prob, psum, scale, mask_ap, token, free, stats, j):
            qn = psum.shape[0]
            neg, total, inv = (stats[0:qn, 4 * j + c:4 * j + c + 1] for c in range(3))
            if mask_ap is not None:
                t1 = on_dve(prob, lambda e: e.tensor_tensor_reduce(prob, psum, mask_ap, -scale, -3.0 * NEG, ALU.add,
                                                                   ALU.min, neg), [token, free])
                t3 = activate(prob, prob, ACT.Exp, [t1], scale=-1.0, bias=neg, accum=total)
                freed = [t1]
            else:
                t1 = reduce(neg, psum, ALU.min, [token, free])
                t3 = activate(prob, psum, ACT.Exp, [t1, free], scale=-1.0, bias=neg, accum=total)
                freed = [t1, t3]
            t4 = recip(inv, total, [t3])
            return freed, [t3], [t4], inv

        x_sems = [semaphore(f"x_landed{i}") for i in range(4)]
        load_sem = {n: semaphore(f"{n}_landed") for n in ("vectors", "constants", "lambda")}
        x_in = xT.rearrange("(k p) t -> p k t", p=P)

        VEC_IN = load(vec[:], vecs, load_sem["vectors"])
        X_IN = []
        for i in range(4):
            X_IN.append(load(x[:, 2 * i:2 * i + 2, :], x_in[:, 2 * i:2 * i + 2, :], x_sems[i]))
            load_first(i)
        load_next()
        load_next()
        CONST_IN = load(const[:], consts[:, 0:C_LAM], load_sem["constants"])
        load_next()
        lam_in = region(10700, 256)
        LAM_IN = load(lam_in, consts[:, C_LAM:N_CONST], load_sem["lambda"])

        R, RQ, CR, SR, RKV = (rows[:, i, :] for i in range(5))
        qn, kn, qr, kr = region(0, 8, T1), region(2176, 8, T1), region(4352, 4, T1), region(5440, 1, T1)
        V16, V = region(5712, 1024), region(6736, 2, 1024)
        silu_gate = region(8784, 8, T1)
        lat = region(6000, 5, T1)

        op = Operand()
        sum_x = SquareSum()
        for k in range(DT):
            landed = [X_IN[k // 2], VEC_IN]
            split_tile(op, k, x[:, k, :], vcol("a_norm_g", k), landed)
            if k % 2:
                split_first(k // 2)
        for k in range(DT):
            sum_x.add(x[:, k, :], X_IN[k // 2])
        lat_tokens, kr_tokens, gate_tokens = [], [], []

        def statistics_a():
            nonlocal R_READY, ROPE_READY
            temp, t = sum_x.total()
            t_pe, R_READY, _ = rstd(temp, [t, CONST_IN], D, T1, R, [])
            sum_x.give([t_pe])
            t1 = tt(CR, cos, R, ALU.mult, [R_READY])
            ROPE_READY = [t1, tt(SR, sin, R, ALU.mult, [R_READY])]

        R_READY = ROPE_READY = RQ_READY = RKV_READY = RKV_COL_READY = SMALL_READY = LRU_READY = None
        sum_q, sum_kv = SquareSum(), SquareSum()
        latent = Operand()

        def evacuate_a_in(m, psum, token):
            if m < 5:
                t1 = tt(lat[:, m, :], psum[:, 0, :], R, ALU.mult, [token, R_READY])
                lat_tokens.append(t1)
                split_tile(latent, m, lat[:, m, :],
                           vcol("a_q_norm_g", m) if m < 3 else vcol("a_kv_norm_g", m - 3), t1)
                (sum_q if m < 3 else sum_kv).add(lat[:, m, :], t1)
                return [t1]
            if m == 5:
                freed, done = rope(kr, psum, 1, T1, CR, SR, token, ROPE_READY)
                kr_tokens.extend(done)
                return freed
            g = silu_gate[:, m - 6, :]
            t1 = tt(g, psum[:, 0, :], R, ALU.mult, [token, R_READY, SMALL_READY])
            gate_tokens.append(activate(g, g, ACT.Silu, [t1]))
            return [t1]

        def small_values():
            nonlocal SMALL_READY, LRU_READY
            lam_ap = vec[:, VEC_AT["b_lam"]:VEC_AT["b_lam"] + 8]
            t = activate(L[0], lam_ap, ACT.Abs, [VEC_IN])
            t = activate(L[1], L[0], ACT.Exp, [t], scale=-1.0)
            t = ts(L[0], L[1], 2.0, ALU.add, [t])
            t = recip(L[2], L[0], [t])
            t = tt(L[0], L[1], L[2], ALU.mult, [t])
            t = tt(L[1], L[0], L[0], ALU.mult, [t])
            terms = [1.0 / (2 * i + 1) for i in range(10)]
            t = ts(L[2], L[1], terms[9], ALU.mult, [t], terms[8], ALU.add)
            for i in range(7, -1, -1):
                t = tt(L[3], L[2], L[1], ALU.mult, [t])
                t = ts(L[2], L[3], terms[i], ALU.add, [t])
            t = stt(L[3], L[0], 2.0, L[2], ALU.mult, ALU.mult, [t])
            t = ts(L[2], lam_ap, -1.0, ALU.mult, [t], 0.0, ALU.max)
            t = tt(L[3], L[3], L[2], ALU.add, [t])
            t = ts(POS_SCALE, L[3], LRU_C, ALU.mult, [t])
            LRU_READY = ts(NEG_SCALE, L[3], -LRU_C, ALU.mult, [t])
            lam4 = lam_in.rearrange("p (a b d) -> p a b d", a=2, b=2)
            lam_prod = lam4[:, :, 0, :]
            t = tt(lam_prod, lam_prod, lam4[:, :, 1, :], ALU.mult, [LAM_IN])
            t = reduce(cols[:, 8:10], lam_prod, ALU.add, [t])
            t = activate(cols[:, 8:10], cols[:, 8:10], ACT.Exp, [t])
            t = tt(cols[:, 10:11], cols[:, 9:10], cols[:, 8:9], ALU.subtract, [t])
            t = ts(cols[:, 11:12], cols[:, 10:11], -LAMBDA_INIT, ALU.add, [t])
            t2 = tt(both_gains, vec[:, VEC_AT["final_norm_g"]:VEC_AT["final_norm_g"] + DT],
                    vec[:, VEC_AT["a_norm_attn_2"]:VEC_AT["a_norm_attn_2"] + DT], ALU.mult, [VEC_IN])
            SMALL_READY = [t, t2, ts(SUB_GAIN, vcol("a_subln_2"), 1.0 - LAMBDA_INIT, ALU.mult, [VEC_IN])]

        L = [lru[:, 8 * i:8 * i + 8] for i in range(6)]
        POS_SCALE, NEG_SCALE = L[4], L[5]
        both_gains = lru[:, 60:68]
        NEG_LAMBDA, SUB_GAIN = cols[:, 11:12], cols[:, 12:13]

        project("a_in", 0, op, T1, evacuate_a_in, hold=True)
        release(statistics_a)
        for _ in range(2):
            project("a_in", 0, op, T1, evacuate_a_in)
        LAT_DONE = everything()
        kv_starts = (0, META, META + P)

        def statistics_latents():
            nonlocal RQ_READY, RKV_READY, RKV_COL_READY, ROPE_READY
            temp, t = sum_q.total()
            t_pe, RQ_READY, _ = rstd(temp, t, Q_LORA, T1, RQ, [])
            sum_q.give([t_pe])
            temp, t = sum_kv.total()
            t_pe, RKV_READY, RKV_COL_READY = rstd(temp, t, KV_LORA, T1, RKV, [], cols[:, 0:3])
            sum_kv.give([t_pe])
            t1 = tt(CR, cos, RQ, ALU.mult, [RQ_READY, kr_tokens])
            ROPE_READY = [t1, tt(SR, sin, RQ, ALU.mult, [RQ_READY, kr_tokens])]

        small_values()
        project("a_in", 0, op, T1, evacuate_a_in, hold=True)
        release(statistics_latents)
        project("a_in", 0, op, T1, evacuate_a_in)
        q_tokens, k_tokens, v_tokens = {}, {}, []

        def evacuate_q(m, psum, token):
            if m < 8:
                q_tokens[m] = [tt(qn[:, m, :], psum[:, 0, :], RQ, ALU.mult, [token, RQ_READY])]
                return q_tokens[m]
            freed, q_tokens[m] = rope(qr[:, m - 8:m - 7, :], psum, 1, T1, CR, SR, token, ROPE_READY)
            return freed

        def evacuate_k(m, psum, token):
            k_tokens[m] = tt(kn[:, m, :], psum[:, 0, :], RKV, ALU.mult, [token, RKV_READY])
            return [k_tokens[m]]

        def evacuate_v(i, c0, psum, token):
            n, dst = (META, V16[0:META, c0:c0 + 512]) if i == 0 else (P, V[:, i - 1, c0:c0 + 512])
            v_tokens.append(activate(dst, psum[0:n, :], ACT.Copy, [token, RKV_COL_READY, LAT_DONE],
                                     scale=cols[0:n, i:i + 1]))
            return [v_tokens[-1]]

        project("a_uq", 0, latent, T1, evacuate_q)
        project("a_uq", 0, latent, T1, evacuate_q)
        project("a_ukv", 0, latent, T1, evacuate_k, base=3)
        project_tokens("a_ukv", 0, latent, kv_starts, evacuate_v, base=3)

        TILES_A = [(0, META, META), (META, P, META + P), (META + P, P, T1)]
        PROB_AT = [0, META, META + META + P]
        heads_in_flight = deque()
        y_op = Operand()

        def scores_a(h):
            prob, free = temps.take()
            stats, sfree = small.take()
            done = []
            pair, half = h // 2, 64 * (h % 2)
            for j, (q0, nq, nk) in enumerate(TILES_A):
                bank, bfree = banks.take()
                matmul(bank[0:nq, 0:nk], qn[:, h, q0:q0 + nq], kn[:, h, 0:nk], True, False,
                       [bfree, q_tokens[h], k_tokens[h]])
                token = matmul(bank[0:nq, 0:nk], qr[half:half + ROPE, pair, q0:q0 + nq],
                               kr[half:half + ROPE, 0, 0:nk], False, True, [q_tokens[8 + pair], kr_tokens], True)
                at = PROB_AT[j]
                m0 = 144 if j == 0 else (128 if j == 1 else 0)
                freed, t_p, t_i, inv = softmax(prob[0:nq, at:at + nk], bank[0:nq, 0:nk], (NOPE + ROPE) ** -0.5,
                                               mask[0:nq, m0:m0 + nk], token, [free, sfree], stats, j)
                banks.give(bank, freed)
                done.append(ts(prob[0:nq, at:at + nk], prob[0:nq, at:at + nk], inv, ALU.mult, [t_p, t_i]))
            small.give(stats, done)
            heads_in_flight.append((h, prob, done))

        def values_a():
            h, prob, done = heads_in_flight.popleft()
            bank16, free16 = banks.take()
            bank, bfree = banks.take()
            for j, (q0, nq, nk) in enumerate(TILES_A):
                at = PROB_AT[j]
                t16 = transpose(bank16[0:META, q0:q0 + nq], prob[0:nq, at:at + META], nq, [done[j], free16, bfree],
                                j == 2)
                if j:
                    t_pe = transpose(bank[:, q0 - META:q0 - META + nq], prob[0:nq, at + META:at + META + P], nq,
                                     signal=True)
                if j == 2:
                    t_pe = transpose(bank[:, SEQ:SEQ + P], prob[0:nq, at + META + P:at + T1], nq, signal=True)
            temps.give(prob, [t_pe])
            pt, free = temps.take()
            t1 = activate(pt[0:META, 0:T1], bank16[0:META, 0:T1], ACT.Copy, [t16, free])
            t2 = activate(pt[:, T1:T1 + SEQ + P], bank[:, 0:SEQ + P], ACT.Copy, [t_pe, free])
            banks.give(bank16, [t1])
            banks.give(bank, [t2])
            return h, pt, t1, t2

        def outputs_a(h, pt, t1, t2):
            o, ofree = banks.take()
            cs = slice(h * P, (h + 1) * P)
            matmul(o[:, 0:T1], V16[0:META, cs], pt[0:META, 0:T1], True, False, [ofree, t1, t2, v_tokens])
            matmul(o[:, META:T1], V[:, 0, cs], pt[:, T1:T1 + SEQ], False, False)
            t3 = matmul(o[:, META + P:T1], V[:, 1, cs], pt[:, T1 + SEQ:T1 + SEQ + P], False, True, signal=True)
            temps.give(pt, [t3])
            y, yfree = temps.take()
            t4 = tt(y[:, 0:T1], o[:, 0:T1], silu_gate[:, h, :], ALU.mult, [t3, yfree, gate_tokens])
            banks.give(o, [t4])
            temps.give(y, split_tile(y_op, h, y[:, 0:T1], None, t4))

        def latent_attention():
            turned = deque()
            for h in range(HEADS + 2):
                if h < HEADS:
                    scores_a(h)
                    yield
                if len(turned) > 0:
                    outputs_a(*turned.popleft())
                if 1 <= h <= HEADS:
                    turned.append(values_a())
                yield

        MEM_KV = [(t[:, 0:512].rearrange("p (n t) -> p n t", n=2), t[:, 512:1024].rearrange("p (n t) -> p n t", n=2))
                  for t in mem_kv]
        R_MEM, MEM_COL = RKV[:, 0:SEQ], cols[:, 4:6]
        starts2 = (0, P)
        mem_in = memT.rearrange("(k p) t -> p k t", p=P)
        mem_tokens = {}
        MEM_READY = []

        def split_memory(layer, gain, total):
            op = Operand()
            for i in range(4):
                temp, free = temps.take()
                v = temp[:, 0:2 * SEQ].rearrange("p (n t) -> p n t", n=2)
                sem = semaphore(f"memory{layer}_landed{i}")
                src = mem_in[:, 2 * i:2 * i + 2, :]
                in_temp = load(v, src, sem, free)
                read = []
                for j in range(2):
                    read += split_tile(op, 2 * i + j, v[:, j, :], vcol(gain, 2 * i + j), in_temp)
                if total is not None:
                    read.append(total.add(v, in_temp))
                temps.give(temp, read)
            return op

        def memory_keys_values(layer, op, before=None):
            MK, MV = MEM_KV[layer]

            def evacuate_mk(m, psum, token):
                row = R_MEM.unsqueeze(1).to_broadcast([P, 2, SEQ])
                mem_tokens["k", layer] = tt(MK, psum, row, ALU.mult, [token, MEM_READY])
                return [mem_tokens["k", layer]]

            def evacuate_mv(i, c0, psum, token):
                mem_tokens["v", layer, i] = activate(MV[:, i, :], psum, ACT.Copy, [token, MEM_READY],
                                                     scale=cols[:, 4 + i:5 + i])
                return [mem_tokens["v", layer, i]]

            project("mem", layer, op, SEQ, evacuate_mk, hold=before is not None)
            if before is not None:
                release(before)
            project_tokens("mem", layer, op, starts2, evacuate_mv)
            op.give()

        def statistics_memory():
            temp, t = sum_mem.total()
            t_pe, t1, t2 = rstd(temp, t, D, SEQ, R_MEM, list(k_tokens.values()), MEM_COL)
            sum_mem.give([t_pe])
            MEM_READY.extend([t1, t2])

        background(latent_attention())
        project("a_in", 0, op, T1, evacuate_a_in)
        project("a_in", 0, op, T1, evacuate_a_in)
        op.give()
        project("a_uq", 0, latent, T1, evacuate_q)
        latent.give()
        sum_mem = SquareSum()
        mem_op = split_memory(0, "a_mem_norm_2", sum_mem)
        memory_keys_values(0, mem_op, statistics_memory)
        finish_background()

        x_tokens = {k: X_IN[k // 2] for k in range(DT)}

        def add_to_residual(T, t0):
            def evacuate(m, psum, token):
                n = psum.shape[1]
                t1 = tt(x[:, m:m + n, t0:t0 + T], x[:, m:m + n, t0:t0 + T], psum, ALU.add,
                        [token] + [x_tokens[k] for k in range(m, m + n)])
                for i in range(n):
                    x_tokens[m + i] = t1
                return [t1]
            return evacuate

        FENCE = everything()
        next_op = Operand()
        sum_x = SquareSum()

        def residual_then_split(T, t0, op, gain, total):
            add = add_to_residual(T, t0)

            def evacuate(m, psum, token):
                freed = add(m, psum, token)
                n = psum.shape[1]
                if gain is not None:
                    for i in range(n):
                        split_tile(op, m + i, x[:, m + i, t0:t0 + T], vcol(gain, m + i), freed)
                total.add(x[:, m:m + n, t0:t0 + T] if n > 1 else x[:, m, t0:t0 + T], freed)
                return freed
            return evacuate

        for _ in range(4):
            project("a_out", 0, y_op, T1, residual_then_split(T1, 0, next_op, "b_norm_g", sum_x))
        y_op.give()

        U = T1 + PAD
        u = region(0, 8, U)
        a_gate = region(0, 8, U)
        uc, rg = region(2200, 8, T1), region(4376, 8, T1)
        ig, silu_b = region(6552, 8, T1), region(8728, 8, SEQ)

        def statistics_b():
            nonlocal R_READY
            temp, t = sum_x.total()
            t_pe, R_READY, _ = rstd(temp, t, D, T1, R, [FENCE])
            sum_x.give([t_pe])

        t_pad = on_dve(u[:, :, 0:PAD], lambda e: e.memset(u[:, :, 0:PAD], 0.0), [FENCE])
        uc_op = Operand()
        uc_tokens, rg_tokens, ig_tokens, gate_tokens = {}, {}, {}, {}

        def evacuate_u(m, psum, token):
            t0 = tt(u[:, m, PAD:U], psum[:, 0, :], R, ALU.mult, [token, R_READY, FENCE])
            c = uc[:, m, :]
            t1 = activate(c, u[:, m, 0:T1], ACT.Identity, [t0, t_pad, FENCE], scale=vcol("b_conv_w", m),
                          bias=vcol("b_conv_b", m))
            for j in range(1, 4):
                t1 = stt(c, u[:, m, j:j + T1], vcol("b_conv_w", 8 * j + m), c, ALU.mult, ALU.add, [t1])
            uc_tokens[m] = t1
            split_tile(uc_op, m, c, None, t1)
            return [t0]

        def evacuate_gate_b(m, psum, token):
            m, n = m - 8, psum.shape[1]
            row = R[:, META:T1].unsqueeze(1).to_broadcast([P, n, SEQ])
            t1 = tt(silu_b[:, m:m + n, :], psum, row, ALU.mult, [token, R_READY, FENCE])
            for i in range(n):
                gate_tokens[m + i] = t1
            return [t1]

        def block_gates(group):
            chunk = Chunk("b_gates", 0)
            for half, (bias, dst, tokens) in enumerate((("b_b_rg", rg, rg_tokens), ("b_b_ig", ig, ig_tokens))):
                for j in range(4):
                    m = 4 * group + j
                    bank, free = banks.take()
                    for k in range(2):
                        tile = 2 * (m // 2) + k
                        w_h, w_l, ready = chunk.part(4 * half + 2 * (j // 2) + k, P * (j % 2), P * (j % 2) + P)
                        token = three(bank[:, 0:T1], w_h, w_l, uc_op.hi(tile, 0, T1), uc_op.lo(tile, 0, T1),
                                      k == 0, k == 1, [ready, free, uc_op.ready[tile]], k == 1)
                    tokens[m] = activate(dst[:, m, :], bank[:, 0:T1], ACT.Sigmoid, [token, FENCE], bias=vcol(bias, m))
                    banks.give(bank, [tokens[m]])
                chunk.done(half, token)
            uc_op.read = [token]

        th = uc
        tanh_tokens, a_tokens, input_tokens = {}, {}, {}

        def recurrence_inputs(tiles):
            for m in tiles[::2]:
                two = slice(m, m + 2)
                t_in = tt(ig[:, two, :], ig[:, two, :], uc[:, two, :], ALU.mult,
                          [ig_tokens[m], ig_tokens[m + 1], uc_tokens[m], uc_tokens[m + 1]])
                for k in (m, m + 1):
                    tanh_tokens[k] = activate(th[:, k, :], rg[:, k, :], ACT.Tanh,
                                              [rg_tokens[k], LRU_READY, t_in, uc_op.ready[k]],
                                              scale=POS_SCALE[:, k:k + 1])
                    a_tokens[k] = activate(a_gate[:, k, 0:T1], rg[:, k, :], ACT.Exp,
                                           [rg_tokens[k], uc_tokens[k], LRU_READY], scale=NEG_SCALE[:, k:k + 1])
                ready = [tanh_tokens[m], tanh_tokens[m + 1], a_tokens[m], a_tokens[m + 1]]
                t3 = activate(rg[:, two, :], a_gate[:, two, 0:T1], ACT.Square, ready)
                t4 = stt(th[:, two, :], rg[:, two, :], 1.0, th[:, two, :], ALU.add, ALU.mult, [t3, ready])
                t5 = activate(th[:, two, :], th[:, two, :], ACT.Sqrt, [t4])
                input_tokens[m] = input_tokens[m + 1] = tt(ig[:, two, 1:T1], ig[:, two, 1:T1], th[:, two, 1:T1],
                                                           ALU.mult, [t5, t_in])

        def recurrence(tiles):
            t1 = activate(silu_b[:, tiles[0]:tiles[-1] + 1, :], silu_b[:, tiles[0]:tiles[-1] + 1, :], ACT.Silu,
                          [gate_tokens[m] for m in tiles])
            for m in tiles:
                a, inp, h = a_gate[:, m, 0:T1], ig[:, m, :], rg[:, m, :]
                t2 = on_dve(h, lambda e, h=h, a=a, inp=inp: e.tensor_tensor_scan(h, a, inp, 0.0, ALU.mult, ALU.add),
                            [input_tokens[m]], 1.2)
                temp, free = temps.take()
                t3 = tt(temp[:, 0:SEQ], h[:, META:T1], silu_b[:, m, :], ALU.mult, [t1, t2, free])
                temps.give(temp, split_tile(y_op, m, temp[:, 0:SEQ], None, t3))

        def u_tiles():
            project("b_in", 0, next_op, T1, evacuate_u)

        def gate_tiles():
            project("b_in", 0, next_op, SEQ, evacuate_gate_b, t0=META)

        project("b_in", 0, next_op, T1, evacuate_u, hold=True)
        release(statistics_b)
        u_tiles()
        u_tiles()
        block_gates(0)
        y_op = Operand()
        u_tiles()
        recurrence_inputs(range(0, 4))
        gate_tiles()
        block_gates(1)
        uc_op.give()
        gate_tiles()
        recurrence_inputs(range(4, 8))
        recurrence(range(0, 4))
        gate_tiles()
        gate_tiles()
        next_op.give()
        recurrence(range(4, 8))

        FENCE = everything()
        xs = x[:, :, META:T1]

        sum_x, sum_xg = SquareSum(), SquareSum()
        op = Operand()
        add_x = add_to_residual(SEQ, META)
        x_read = {}

        def residual_and_both_sums(m, psum, token):
            freed = add_x(m, psum, token)
            for k in (m, m + 1):
                x_read[k] = split_tile(op, k, xs[:, k, :], both_gains[:, k:k + 1], [freed, SMALL_READY])
                x_read[k] += [sum_x.add(xs[:, k, :], freed), sum_xg.add(xs[:, k, :], freed, vcol("final_norm_g", k))]
            return freed

        for _ in range(4):
            project("b_out", 0, y_op, SEQ, residual_and_both_sums)
        y_op.give()

        q = region(0, 6, SEQ)
        kk = region(1536, 6, SEQ)
        vv = region(3072, 2, 768)
        qm = region(4608, 2, SEQ)
        o_tok = region(5120, 2, 768)
        RC = R[:, 0:SEQ]
        CR2, SR2, R2 = CR[:, 0:SEQ], SR[:, 0:SEQ], RQ[:, 0:SEQ]
        X_COL = cols[:, 0:2]
        TILES = [(0, P, P), (P, P, SEQ)]
        FULL_TILES = [(0, P, SEQ), (P, P, SEQ)]
        scale = DH ** -0.5
        tokens2 = {}

        def statistics_attention():
            temp, t = sum_x.total()
            if layer == 0:
                c1, after = cols[:, 6:8], [FENCE]
                t_pe, t1 = mean_square(temp, t, D, SEQ, c1, after)
                temp, t = sum_xg.total()
                t_pe2, t2 = mean_square(temp, t, D, SEQ, X_COL, after, 0.0)
                sum_xg.give([t_pe2])
                t1 = rsqrt(c1, t1)
                t2 = tt(X_COL, X_COL, c1, ALU.mult, [t1, t2])
                t2 = tt(X_COL, X_COL, c1, ALU.mult, [t2])
                t2 = ts(X_COL, X_COL, EPS, ALU.add, [t2])
                t2 = rsqrt(X_COL, t2)
                t_col = tt(X_COL, X_COL, c1, ALU.mult, [t2])
                t_row = spread(RC, X_COL, t_col, SEQ, after)
                t3 = spread(R2, c1, t1, SEQ, after)
                for k in range(DT):
                    x_tokens[k] = stt(xs[:, k, :], xs[:, k, :], vcol("final_norm_g", k), R2, ALU.mult, ALU.mult,
                                      [t3, x_read[k]])
            else:
                t_pe, t_row, t_col = rstd(temp, t, D, SEQ, RC, [FENCE], X_COL)
            sum_x.give([t_pe])
            tokens2["row"], tokens2["col"] = t_row, t_col
            tokens2["rope"] = [tt(CR2, cos[:, 0:SEQ], RC, ALU.mult, [t_row, FENCE]),
                               tt(SR2, sin[:, 0:SEQ], RC, ALU.mult, [t_row, FENCE])]

        def evacuate_qk(m, psum, token):
            dst, name, m = (q, "q", m) if m < 6 else (kk, "k", m - 6)
            freed, done = rope(dst[:, m:m + 2, :], psum, 2, SEQ, CR2, SR2, token, [tokens2["rope"], FENCE])
            tokens2[name, m] = tokens2[name, m + 1] = done
            return freed

        def evacuate_v2(group):
            def evacuate(i, c0, psum, token):
                t1 = activate(vv[:, i, 256 * group:256 * group + 256], psum, ACT.Copy,
                              [token, tokens2["col"], FENCE], scale=cols[:, i:i + 1])
                tokens2["v", i, group] = t1
                return [t1]
            return evacuate

        def evacuate_qm(m, psum, token):
            row = RC.unsqueeze(1).to_broadcast([P, 2, SEQ])
            t1 = stt(qm, psum, -scale, row, ALU.mult, ALU.mult, [token, tokens2["row"], FENCE])
            tokens2["qm"] = [t1]
            return [t1]

        def score_tile(prob, free, stats, sfree, qt, kt_, p0, tiles, masked, after):
            done = []
            for j, (q0, nq, nk) in enumerate(tiles):
                bank, bfree = banks.take()
                token = matmul(bank[:, 0:nk], qt[p0:p0 + DH, q0:q0 + nq], kt_[p0:p0 + DH, 0:nk], True, True,
                               [bfree, after], True)
                at = 0 if j == 0 else SEQ
                m_ap = None if not masked else (mask[:, 144:144 + P] if j == 0 else mask[:, META:META + SEQ])
                freed, t_p, t_i, inv = softmax(prob[:, at:at + nk], bank[:, 0:nk], scale, m_ap, token,
                                               [free, sfree], stats, j)
                banks.give(bank, freed)
                done.append((t_p, t_i, inv, at, nk))
            return done

        def transposed(prob, done, causal):
            bank, bfree = banks.take()
            transpose(bank[:, 0:P], prob[:, 0:P], P, [done, bfree])
            t_pe = transpose(bank[:, P:SEQ], prob[:, SEQ:SEQ + P], P, signal=True)
            if causal:
                t_pe = transpose(bank[:, SEQ:SEQ + P], prob[:, SEQ + P:2 * SEQ], P, signal=True)
            else:
                transpose(bank[:, SEQ:SEQ + P], prob[:, P:SEQ], P)
                t_pe = transpose(bank[:, SEQ + P:2 * SEQ], prob[:, SEQ + P:2 * SEQ], P, signal=True)
            temps.give(prob, [t_pe])
            n = 3 * P if causal else 2 * SEQ
            pt, free = temps.take()
            t1 = activate(pt[:, 0:n], bank[:, 0:n], ACT.Copy, [t_pe, free])
            banks.give(bank, [t1])
            return pt, [t1]

        def normalize(prob, done):
            return [ts(prob[:, at:at + nk], prob[:, at:at + nk], inv, ALU.mult, [t_p, t_i])
                    for t_p, t_i, inv, at, nk in done]

        def head_pairs(n_heads, qt, kt_, v_of, causal, q_after, v_after, y_first):
            scored, turned, shared = deque(), deque(), {}

            def outputs(h, pt, t_pt):
                p0 = DH * (h % 2)
                if p0 == 0:
                    shared["o"] = banks.take()
                o, ofree = shared["o"]
                matmul(o[p0:p0 + DH, 0:SEQ], v_of(0, h), pt[:, 0:SEQ], True, False, [ofree, t_pt, v_after(h)])
                if causal:
                    t3 = matmul(o[p0:p0 + DH, P:SEQ], v_of(1, h), pt[:, SEQ:SEQ + P], False, True, signal=True)
                else:
                    t3 = matmul(o[p0:p0 + DH, 0:SEQ], v_of(1, h), pt[:, SEQ:2 * SEQ], False, True, signal=True)
                temps.give(pt, [t3])
                if p0:
                    banks.give(o, split_tile(y_op, y_first + h // 2, o[:, 0:SEQ], None, t3))

            for h in range(n_heads + 2):
                if h < n_heads:
                    while causal and ("k", h // 2) not in tokens2:
                        yield
                    prob, free = temps.take()
                    stats, sfree = small.take()
                    done = score_tile(prob, free, stats, sfree, qt[:, h // 2, :], kt_[:, h // 2, :], DH * (h % 2),
                                      TILES if causal else FULL_TILES, causal, q_after(h // 2))
                    normed = normalize(prob, done)
                    small.give(stats, normed)
                    scored.append((h, prob, normed))
                    yield
                if turned:
                    while causal and ("v", 1, turned[0][0] // 4) not in tokens2:
                        yield
                    outputs(*turned.popleft())
                if 1 <= h <= n_heads:
                    hh, prob, normed = scored.popleft()
                    turned.append((hh, *transposed(prob, normed, causal)))
                yield

        sums = lru[:, 48:60]

        def differential_attention():
            scored, turned, squared = deque(), deque(), []

            def outputs(h, pt, t_pt):
                cs = slice(h * P, (h + 1) * P)
                o, ofree = banks.take()
                v_after = [tokens2["v", 0, h // 2], tokens2["v", 1, h // 2]]
                matmul(o[:, 0:P], pt[:, 0:P], vv[:, 0, cs], True, True, [ofree, t_pt, v_after])
                matmul(o[:, P:SEQ], pt[:, P:SEQ], vv[:, 0, cs], True, False)
                t3 = matmul(o[:, P:SEQ], pt[:, SEQ:SEQ + P], vv[:, 1, cs], False, True, signal=True)
                temps.give(pt, [t3])
                t4 = copy(o_tok[:, :, cs], o[:, 0:SEQ].rearrange("p (n t) -> p n t", n=2), [t3, FENCE])
                banks.give(o, [t4])
                junk, jfree = temps.take()
                read = []
                for i in range(2):
                    t5 = activate(junk[:, i * P:(i + 1) * P], o_tok[:, i, cs], ACT.Square, [t4, jfree],
                                  accum=sums[:, 6 * i + h:6 * i + h + 1])
                    read.append(t5)
                squared.extend(read)
                temps.give(junk, read)

            for h in range(DIFF_HEADS + 2):
                if h < DIFF_HEADS:
                    while ("k", h) not in tokens2:
                        yield
                    parts = []
                    for c in range(2):
                        prob, free = temps.take()
                        stats, sfree = small.take()
                        after = [tokens2["q", h], tokens2["k", h]]
                        parts.append((prob, stats, score_tile(prob, free, stats, sfree, q[:, h, :], kk[:, h, :],
                                                              DH * c, TILES, True, after)))
                        if c == 0:
                            yield
                    (p_0, s_0, d_0), (p_1, s_1, d_1) = parts
                    merged = []
                    for j in range(2):
                        (tp0, ti0, inv0, at, nk), (tp1, ti1, inv1, _, _) = d_0[j], d_1[j]
                        t1 = ts(p_1[:, at:at + nk], p_1[:, at:at + nk], inv1, ALU.mult, [tp1, ti1, SMALL_READY],
                                NEG_LAMBDA, ALU.mult)
                        merged.append(stt(p_0[:, at:at + nk], p_0[:, at:at + nk], inv0, p_1[:, at:at + nk],
                                          ALU.mult, ALU.add, [tp0, ti0, t1]))
                    small.give(s_0, merged)
                    small.give(s_1, merged)
                    temps.give(p_1, merged)
                    scored.append((h, p_0, merged))
                    yield
                if turned:
                    while ("v", 1, turned[0][0] // 2) not in tokens2:
                        yield
                    outputs(*turned.popleft())
                if 1 <= h <= DIFF_HEADS:
                    hh, prob, merged = scored.popleft()
                    turned.append((hh, *transposed(prob, merged, True)))
                yield
            t1 = ts(sums, sums, 1.0 / P, ALU.mult, squared, EPS, ALU.add)
            t2 = activate(sums, sums, ACT.Sqrt, [t1])
            t3 = recip(sums, sums, [t2])
            for h in range(0, DIFF_HEADS, 2):
                bank, bfree = banks.take()
                for hh in range(2):
                    cs = slice((h + hh) * P, (h + hh + 1) * P)
                    for i in range(2):
                        s = sums[:, 6 * i + h + hh:6 * i + h + hh + 1]
                        t4 = ts(o_tok[:, i, cs], o_tok[:, i, cs], s, ALU.mult, [t3])
                        t_pe = transpose(bank[:, hh * SEQ + i * P:hh * SEQ + (i + 1) * P], o_tok[:, i, cs], P,
                                         [t4, bfree], True)
                view = bank[:, 0:2 * SEQ].rearrange("p (n t) -> p n t", n=2)
                banks.give(bank, split_tile(y_op, h, view, SUB_GAIN, [t_pe, SMALL_READY], n=2))

        def mlp(layer, x_op, R_row, statistics, after_sum, total_ready):
            hidden = {}
            down_sums = [banks.take() for _ in range(4)]

            def up(quarter, before=None):
                u_op = hidden[quarter] = Operand()

                def evacuate(m, psum, token):
                    m -= 8 * quarter
                    t_buf, free = temps.take()
                    v = t_buf[:, 0:2 * SEQ].rearrange("p (n t) -> p n t", n=2)
                    row = R_row.unsqueeze(1).to_broadcast([P, 2, SEQ])
                    t1 = stt(v, psum, 0.0, row, ALU.max, ALU.mult, [token, total_ready(), free])
                    t2 = activate(v, v, ACT.Square, [t1])
                    temps.give(t_buf, split_tile(u_op, m, v, None, t2, n=2))
                    return [t1]

                for i in range(4):
                    project("up", layer, x_op, SEQ, evacuate, hold=before is not None and i == 0)
                    if i == 0:
                        release(before)

            def down(quarter):
                u_op = hidden.pop(quarter)
                for c in range(4):
                    chunk = Chunk("down", layer)
                    bank, free = down_sums[c]
                    for j in range(2):
                        for k in range(8):
                            w_h, w_l, ready = chunk.part(k, j * P, (j + 1) * P)
                            token = three(bank[:, j * SEQ:(j + 1) * SEQ], w_h, w_l,
                                          u_op.hi(k, 0, SEQ), u_op.lo(k, 0, SEQ),
                                          quarter == 0 and k == 0 and j == 0, quarter == 3 and k == 7,
                                          [ready, free if quarter == 0 else [], u_op.ready[k]],
                                          k == 7, shared=True)
                        chunk.done(j, token)
                    u_op.read = [token]
                    if quarter == 3:
                        view = bank[:, 0:2 * SEQ].rearrange("p (n t) -> p n t", n=2)
                        banks.give(bank, after_sum(2 * c, view, token))
                u_op.give()

            up(0, statistics)
            up(1)
            down(0)
            up(2)
            down(1)
            up(3)
            x_op.give()
            down(2)
            return lambda: down(3)

        for layer in range(2):
            if layer == 0:
                q_op = kv_op = op
            y_op = Operand()
            project("in2", layer, q_op, SEQ, evacuate_qm, hold=True)
            release(statistics_attention)
            MK, MV = MEM_KV[layer]
            background(head_pairs(MEM_HEADS, qm, MK, lambda i, h, MV=MV: MV[:, i, h * DH:(h + 1) * DH], False,
                                  lambda p, layer=layer: [tokens2["qm"], mem_tokens["k", layer]],
                                  lambda h, layer=layer: [mem_tokens["v", layer, 0], mem_tokens["v", layer, 1]], 6),
                       rate=2)
            if layer == 1:
                attention = head_pairs(MOBA_HEADS, q, kk, lambda i, h: vv[:, i, h * DH:(h + 1) * DH], True,
                                       lambda p: [tokens2["q", p], tokens2["k", p]],
                                       lambda h: [tokens2["v", 0, h // 4], tokens2["v", 1, h // 4]], 0)
            else:
                attention = differential_attention()
            for index in IN2_ORDER[1:]:
                if index < 6:
                    project("in2", layer, q_op if index < 3 else kv_op, SEQ, evacuate_qk)
                else:
                    project_tokens("in2", layer, kv_op, starts2, evacuate_v2(index - 6))
                if index == 2 and layer == 1:
                    q_op.give()
                if index == 6:
                    finish_background()
                    background(attention, rate=1 + layer)
            kv_op.give()
            if layer == 0:
                mem_op = split_memory(1, "b_mem_norm_2", None)
                memory_keys_values(1, mem_op)
            finish_background()
            FENCE = everything()
            op = Operand()
            sum_x = SquareSum()
            gain = "a_norm_mlp_2" if layer == 0 else "b_norm_mlp_2"
            for _ in range(4):
                project("out2", layer, y_op, SEQ, residual_then_split(SEQ, META, op, gain, sum_x))
            y_op.give()

            def statistics_mlp():
                temp, t = sum_x.total()
                t_pe, tokens2["mlp"], _ = rstd(temp, t, D, SEQ, R2, [FENCE])
                sum_x.give([t_pe])

            def after_mlp(m, psum, token):
                return finish_x(m, psum, token)

            down_last = mlp(layer, op, R2, statistics_mlp, after_mlp, lambda: tokens2["mlp"])
            sum_x = SquareSum()
            if layer == 0:
                q_op = Operand()
                finish_x = residual_then_split(SEQ, META, q_op, "b_norm_attn_2", sum_x)
                down_last()
                kv_op = Operand()
                for k in range(DT):
                    split_tile(kv_op, k, xs[:, k, :], vcol("kv_norm_2", k), x_tokens[k])
            else:
                finish_x = residual_then_split(SEQ, META, None, None, sum_x)
                down_last()
            FENCE = everything()
            tokens2.clear()

        temp, t = sum_x.total()
        t_pe, R_READY, _ = rstd(temp, t, D, SEQ, RC, [FENCE])
        for k in range(DT):
            x_tokens[k] = activate(xs[:, k, :], xs[:, k, :], ACT.Copy, [x_tokens[k], FENCE],
                                   scale=vcol("final_norm_2", k))
        out_sem = semaphore("output_written")
        stores = []
        row = RC.unsqueeze(1).to_broadcast([P, 2, SEQ])
        for k in (0, 2, 4):
            stores.append((k, 2, [tt(xs[:, k:k + 2, :], xs[:, k:k + 2, :], row, ALU.mult,
                                     [R_READY, x_tokens[k], x_tokens[k + 1]])]))
            if k == 2:
                for kp in (6, 7):
                    v = xs[:, kp, :]
                    t1 = pool.do(lambda e, v=v: e.tensor_tensor(v, v, RC, ALU.mult), [R_READY, x_tokens[kp]])
                    stores.append((kp, 1, [t1]))
        stores.sort(key=lambda s: s[0] if s[0] < 6 else s[0] - 3.5)

        for k, n, tokens in stores:
            dst, src = out[k * P:(k + n) * P, :].rearrange("(n p) t -> p n t", p=P), xs[:, k:k + n, :]
            load(dst, src, out_sem, tokens)
        plan.arrange()

        block = ctx.enter_context(nc.Block())

        @block.sync
        def _(e):
            sp.emit(e)
            e.wait_ge(out_sem, 16 * len(stores))

        @block.scalar
        def _(e):
            act.emit(e)

        @block.vector
        def _(e):
            dve.emit(e)

        @block.tensor
        def _(e):
            pe.emit(e)

        @block.gpsimd
        def _(e):
            pool.emit(e)


def rope_order():
    return [(p % 32) // 16 * 32 + 16 * (p // 32) + p % 16 for p in range(64)]


def rope_columns(first, n_heads, stride):
    return np.concatenate([first + h * stride + np.array(rope_order()) for h in range(n_heads)])


def shape_constants():
    c = np.zeros((P, N_CONST), np.float32)
    c[:, C_IDENT:C_IDENT + P] = np.eye(P, dtype=np.float32)
    c[:, C_ONES:C_ONES + P] = 1.0
    i = np.arange(P)
    c[:, C_MASK + 144:C_MASK + 272] = np.where(i[None, :] <= i[:, None], 0.0, NEG).astype(np.float32)
    inv = (np.float32(10000.0) ** (-np.arange(0, 64, 2, dtype=np.float32) / np.float32(64))).astype(np.float32)
    ang = (np.arange(T1, dtype=np.float32)[:, None] * inv[None, :]).astype(np.float64)
    for p in range(P):
        f = rope_order()[p % 64]
        c[p, C_COS:C_COS + T1] = np.cos(ang[:, f % 32])
        c[p, C_SIN:C_SIN + T1] = np.sin(ang[:, f % 32]) * (-1.0 if f < 32 else 1.0)
    return c


def kernel(**inputs):
    import concourse.bacc as bacc
    from concourse.bass_utils import run_bass_kernel_spmd

    v = {k: np.asarray(a) for k, a in inputs.items()}
    wi = v["a_w_in"][0]
    rope_k = wi[:, 640 + np.array(rope_order())]
    a_in = np.concatenate([wi[:, :640], rope_k, rope_k, wi[:, 704:]], axis=1)
    hd = NOPE + ROPE
    a_uq = v["a_w_uq"][0][:, np.concatenate(
        [h * hd + np.arange(NOPE) for h in range(HEADS)] + [rope_columns(NOPE, HEADS, hd)])]
    a_ukv = v["a_w_ukv"][0][:, np.concatenate(
        [h * 256 + np.arange(NOPE) for h in range(HEADS)] + [h * 256 + NOPE + np.arange(128) for h in range(HEADS)])]
    gates = [np.concatenate([v[n][0].reshape(D, 256)[512 * i:512 * i + 512] for n in ("b_w_rg", "b_w_ig")], axis=0)
             for i in range(2)]
    r12 = rope_columns(0, 12, DH)
    in_a = v["a_w_in_2"][0][:, np.concatenate([r12, 768 + r12, np.arange(1536, 2560)])]
    in_b = np.concatenate([v["b_w_in_2"][0][:, r12], v["w_kv_2"][:, r12], v["w_kv_2"][:, 768:],
                           v["b_w_in_2"][0][:, 768:]], axis=1)
    weights = {
        ("a_in", 0): a_in, ("a_uq", 0): a_uq, ("a_ukv", 0): a_ukv, ("a_out", 0): v["a_w_out"][0],
        ("b_in", 0): v["b_w_in"][0], ("b_out", 0): v["b_w_out"][0],
        ("mem", 0): v["a_w_mem_kv_2"][0], ("mem", 1): v["b_w_mem_kv_2"][0],
        ("in2", 0): in_a, ("in2", 1): in_b,
        ("out2", 0): v["a_w_out_2"][0], ("out2", 1): v["b_w_out_2"][0],
        ("up", 0): v["a_w_up_2"][0], ("up", 1): v["b_w_up_2"][0],
        ("down", 0): v["a_w_down_2"][0], ("down", 1): v["b_w_down_2"][0],
    }
    order = chunk_order()
    stream = np.zeros((len(order), P, CHUNK), np.float32)
    for n, (kind, layer, i) in enumerate(order):
        kt, w = SHAPES[kind]
        if kind == "b_gates":
            block = gates[i]
        elif kind == "down":
            block = weights[kind, layer][(i // 4) * 1024:(i // 4 + 1) * 1024, (i % 4) * w:(i % 4 + 1) * w]
        else:
            block = weights[kind, layer][:, i * w:(i + 1) * w]
        by_inputs, kh, wh = halves_of(kind, i)
        tiles = block.reshape(kt, P, w).transpose(1, 0, 2)
        for half in range(2):
            part = tiles[:, half * kh:(half + 1) * kh] if by_inputs else tiles[:, :, half * wh:(half + 1) * wh]
            stream[n, :, half * kh * wh:(half + 1) * kh * wh] = part.reshape(P, kh * wh)
    vecs = np.concatenate([v[n].reshape(k, P).T for n, k in VECTORS], axis=1)
    consts = shape_constants()
    consts[:, C_LAM:] = v["a_lambda_2"].reshape(1, -1)
    arrays = {
        "stream": stream,
        "xT": np.ascontiguousarray(np.concatenate([v["meta_tokens"], v["x"][0]], axis=0).T),
        "memT": np.ascontiguousarray(v["mem_2"][0].T),
        "vecs": np.ascontiguousarray(vecs),
        "consts": consts,
    }
    nc = bacc.Bacc("TRN2", target_bir_lowering=False, num_devices=1)
    args = [nc.dram_tensor(f"{n}_dram", a.shape, F32, kind="ExternalInput").ap() for n, a in arrays.items()]
    out = nc.dram_tensor("out_dram", (D, SEQ), F32, kind="ExternalOutput").ap()
    program(nc, *args, out)
    r = run_bass_kernel_spmd(nc, [{f"{n}_dram": a for n, a in arrays.items()}], core_ids=[0])
    return np.ascontiguousarray(r.results[0]["out_dram"].T).reshape(1, SEQ, D)
```
